# Optimizing a Trainium2 kernel written in Bass

```python
import jax, jax.numpy as jnp
from jax import lax
import numpy as np

D_MODEL = 1024
BATCH = 1
SEQ = 256
DEPTH = 2

HEAD_DIM = 64
MOBA_HEADS = 8
MOBA_BLOCK = 256
MOBA_TOPK = 3
MOBA_Q_CHUNK = 32
FOX_HEADS = 8
FOX_Q_BLOCK = 128
POOL_WINDOWS = (2, 4, 8, 16)
POOL_GROUP = 128
POOL_WIDTH = POOL_GROUP * len(POOL_WINDOWS)
MEM_HEADS = 4
MEM_HEAD_DIM = 128
MEM_LEN = 256
ROPE_THETA = 500000.0
ROT_DIM = HEAD_DIM // 4
N_BRANCH = 4
BRANCH_WIDTH = 512
D_FF = 2816
RMS_EPS = 1e-6
NEG_INF = -1e30

MOBA_WIDTH = MOBA_HEADS * HEAD_DIM
FOX_WIDTH = FOX_HEADS * HEAD_DIM
MEM_WIDTH = MEM_HEADS * MEM_HEAD_DIM
IN_SIZES = (3 * MOBA_WIDTH, 3 * FOX_WIDTH, FOX_HEADS, POOL_WIDTH, MEM_WIDTH, N_BRANCH * D_MODEL)
IN_SPLITS = tuple(sum(IN_SIZES[:i + 1]) for i in range(len(IN_SIZES) - 1))
D_IN = sum(IN_SIZES)

kernel_name = 'hybrid_moba_pool_fox_memory_macaron'

def rms_norm(x, gain):
    x32 = x.astype(jnp.float32)
    y = x32 * lax.rsqrt(jnp.mean(x32 * x32, axis=-1, keepdims=True) + RMS_EPS)
    return (y * gain.astype(jnp.float32)).astype(x.dtype)

def swiglu(h, w_in, w_out):
    g, u = jnp.split(h @ w_in, 2, axis=-1)
    return (jax.nn.silu(g) * u) @ w_out

def to_heads(t, n, d):
    b, s, _ = t.shape
    return t.reshape(b, s, n, d).transpose(0, 2, 1, 3)

def from_heads(t):
    b, n, s, d = t.shape
    return t.transpose(0, 2, 1, 3).reshape(b, s, n * d)

def split_qkv(t, n, d):
    b, s, _ = t.shape
    t = t.reshape(b, s, 3, n, d)
    return (t[:, :, 0].transpose(0, 2, 1, 3), t[:, :, 1].transpose(0, 2, 1, 3),
            t[:, :, 2].transpose(0, 2, 1, 3))

def partial_rotary(x, positions):
    half = ROT_DIM // 2
    inv_freq = jnp.power(ROPE_THETA, -jnp.arange(half, dtype=jnp.float32) * (2.0 / ROT_DIM))
    ang = positions.astype(jnp.float32)[:, None, :, None] * inv_freq
    cos = jnp.cos(ang).astype(x.dtype)
    sin = jnp.sin(ang).astype(x.dtype)
    x1 = x[..., :half]
    x2 = x[..., half:ROT_DIM]
    return jnp.concatenate([x1 * cos - x2 * sin, x2 * cos + x1 * sin, x[..., ROT_DIM:]], axis=-1)

def moba_attention(q, k, v):
    b, h, s, d = q.shape
    n_blk = -(-s // MOBA_BLOCK)
    s_pad = n_blk * MOBA_BLOCK
    pad = ((0, 0), (0, 0), (0, s_pad - s), (0, 0))
    q, k, v = (jnp.pad(t, pad) for t in (q, k, v))
    kb = k.reshape(b, h, n_blk, MOBA_BLOCK, d)
    vb = v.reshape(b, h, n_blk, MOBA_BLOCK, d)
    k_mean = jnp.mean(kb.astype(jnp.float32), axis=3)
    n_sel = min(MOBA_TOPK, n_blk)
    n_chunk = s_pad // MOBA_Q_CHUNK
    qc = q.reshape(b, h, n_chunk, MOBA_Q_CHUNK, d).transpose(2, 0, 1, 3, 4)
    b_idx = jnp.arange(b)[:, None, None, None]
    h_idx = jnp.arange(h)[None, :, None, None]
    scale = d ** -0.5

    def chunk(args):
        q_i, c_i = args
        start = c_i * MOBA_Q_CHUNK
        blk = start // MOBA_BLOCK
        q_pos = start + jnp.arange(MOBA_Q_CHUNK)
        gate = jnp.einsum('bhqd,bhnd->bhqn', q_i.astype(jnp.float32), k_mean)
        gate = jnp.where(jnp.arange(n_blk) < blk, gate, NEG_INF)
        _, sel = lax.top_k(gate, n_sel)
        valid = sel < blk
        k_sel = kb[b_idx, h_idx, sel]
        v_sel = vb[b_idx, h_idx, sel]
        s_sel = jnp.einsum('bhqd,bhqkld->bhqkl', q_i, k_sel).astype(jnp.float32) * scale
        s_sel = jnp.where(valid[..., None], s_sel, NEG_INF)
        s_sel = s_sel.reshape(b, h, MOBA_Q_CHUNK, n_sel * MOBA_BLOCK)
        k_own = lax.dynamic_index_in_dim(kb, blk, axis=2, keepdims=False)
        v_own = lax.dynamic_index_in_dim(vb, blk, axis=2, keepdims=False)
        s_own = jnp.einsum('bhqd,bhld->bhql', q_i, k_own).astype(jnp.float32) * scale
        k_pos = blk * MOBA_BLOCK + jnp.arange(MOBA_BLOCK)
        s_own = jnp.where(k_pos[None, :] <= q_pos[:, None], s_own, NEG_INF)
        p = jax.nn.softmax(jnp.concatenate([s_sel, s_own], axis=-1), axis=-1).astype(v.dtype)
        p_sel = p[..., :n_sel * MOBA_BLOCK].reshape(b, h, MOBA_Q_CHUNK, n_sel, MOBA_BLOCK)
        p_own = p[..., n_sel * MOBA_BLOCK:]
        return (jnp.einsum('bhqkl,bhqkld->bhqd', p_sel, v_sel)
                + jnp.einsum('bhql,bhld->bhqd', p_own, v_own))

    out = lax.map(chunk, (qc, jnp.arange(n_chunk)))
    out = out.transpose(1, 2, 0, 3, 4).reshape(b, h, s_pad, d)
    return out[:, :, :s]

def forgetting_attention(q, k, v, log_f):
    b, h, s, d = q.shape
    c = jnp.cumsum(log_f, axis=-1)
    n_blk = s // FOX_Q_BLOCK
    qb = q.reshape(b, h, n_blk, FOX_Q_BLOCK, d).transpose(2, 0, 1, 3, 4)
    cb = c.reshape(b, h, n_blk, FOX_Q_BLOCK).transpose(2, 0, 1, 3)
    k_pos = jnp.arange(s)
    scale = d ** -0.5

    def block(args):
        q_i, c_i, i = args
        q_pos = i * FOX_Q_BLOCK + jnp.arange(FOX_Q_BLOCK)
        logits = (jnp.einsum('bhqd,bhkd->bhqk', q_i, k).astype(jnp.float32) * scale
                  + (c_i[..., None] - c[:, :, None, :]))
        logits = jnp.where(k_pos[None, :] <= q_pos[:, None], logits, NEG_INF)
        p = jax.nn.softmax(logits, axis=-1).astype(v.dtype)
        return jnp.einsum('bhqk,bhkd->bhqd', p, v)

    out = lax.map(block, (qb, cb, jnp.arange(n_blk)))
    return out.transpose(1, 2, 0, 3, 4).reshape(b, h, s, d)

def multiscale_pool(u, pool_mix, pool_scale):
    b, s, _ = u.shape
    ug = u.reshape(b, s, len(POOL_WINDOWS), POOL_GROUP)
    csum = jnp.cumsum(ug.astype(jnp.float32), axis=1)
    t = jnp.arange(s)
    means = []
    for g, w in enumerate(POOL_WINDOWS):
        cg = csum[:, :, g]
        prev = jnp.pad(cg, ((0, 0), (w, 0), (0, 0)))[:, :s]
        cnt = jnp.minimum(t + 1, w).astype(jnp.float32)[None, :, None]
        means.append((cg - prev) / cnt)
    pooled = (jnp.stack(means, axis=2) - ug.astype(jnp.float32)).astype(u.dtype)
    mixed = jnp.einsum('bsgc,gce->bsge', pooled, pool_mix)
    return mixed.reshape(b, s, POOL_WIDTH) * pool_scale

def memory_cross_attention(q_flat, mem, norm_gain, w_kv, q_gain, k_gain):
    q = rms_norm(to_heads(q_flat, MEM_HEADS, MEM_HEAD_DIM), q_gain)
    k_m, v_m = jnp.split(rms_norm(mem, norm_gain) @ w_kv, 2, axis=-1)
    k_m = rms_norm(to_heads(k_m, MEM_HEADS, MEM_HEAD_DIM), k_gain)
    v_m = to_heads(v_m, MEM_HEADS, MEM_HEAD_DIM)
    logits = jnp.einsum('bhqd,bhmd->bhqm', q, k_m).astype(jnp.float32) * (MEM_HEAD_DIM ** -0.5)
    p = jax.nn.softmax(logits, axis=-1).astype(v_m.dtype)
    return from_heads(jnp.einsum('bhqm,bhmd->bhqd', p, v_m))

def hybrid_mixer(h, mem, positions, w_in, b_forget, moba_q_gain, moba_k_gain,
                 fox_q_gain, fox_k_gain, norm_mem, w_mem_kv, mem_q_gain, mem_k_gain,
                 pool_mix, pool_scale, w_branch, w_out):
    b, s, _ = h.shape
    proj = h @ w_in
    moba_qkv, fox_qkv, fox_f, pool_u, mem_q, gate_logits = jnp.split(proj, IN_SPLITS, axis=-1)
    q_a, k_a, v_a = split_qkv(moba_qkv, MOBA_HEADS, HEAD_DIM)
    q_a = partial_rotary(rms_norm(q_a, moba_q_gain), positions)
    k_a = partial_rotary(rms_norm(k_a, moba_k_gain), positions)
    o_a = from_heads(moba_attention(q_a, k_a, v_a))
    o_b = multiscale_pool(pool_u, pool_mix, pool_scale)
    q_c, k_c, v_c = split_qkv(fox_qkv, FOX_HEADS, HEAD_DIM)
    log_f = jax.nn.log_sigmoid((fox_f + b_forget).astype(jnp.float32)).transpose(0, 2, 1)
    o_c = from_heads(forgetting_attention(rms_norm(q_c, fox_q_gain), rms_norm(k_c, fox_k_gain),
                                          v_c, log_f))
    o_m = memory_cross_attention(mem_q, mem, norm_mem, w_mem_kv, mem_q_gain, mem_k_gain)
    branches = jnp.stack([o_a, o_b, o_c, o_m], axis=2)
    y = jnp.einsum('bsnc,ncd->bsnd', branches, w_branch)
    gates = jax.nn.sigmoid(gate_logits.reshape(b, s, N_BRANCH, D_MODEL))
    return jnp.sum(gates * y, axis=2) @ w_out

def setup_inputs(seed: int = 0) -> dict:
    key = jax.random.key(seed)
    ks = jax.random.split(key, 26)
    f32 = jnp.float32

    def dense(k, shape, fan_in):
        return jax.random.normal(k, shape, f32) * (fan_in ** -0.5)

    def gain(k, shape):
        return 1.0 + 0.05 * jax.random.normal(k, shape, f32)

    x = jax.random.normal(ks[0], (BATCH, SEQ, D_MODEL), f32)
    mem = jax.random.normal(ks[1], (BATCH, MEM_LEN, D_MODEL), f32)
    offsets = jax.random.randint(ks[2], (BATCH, 1), 0, 1024, dtype=jnp.int32)
    positions = offsets + jnp.arange(SEQ, dtype=jnp.int32)[None, :]
    L = DEPTH
    return {
        'x': x,
        'mem': mem,
        'positions': positions,
        'norm_ffn1': gain(ks[3], (L, D_MODEL)),
        'w_ffn1_in': dense(ks[4], (L, D_MODEL, 2 * D_FF), D_MODEL),
        'w_ffn1_out': dense(ks[5], (L, D_FF, D_MODEL), D_FF),
        'norm_mix': gain(ks[6], (L, D_MODEL)),
        'w_in': dense(ks[7], (L, D_MODEL, D_IN), D_MODEL),
        'b_forget': jax.random.uniform(ks[8], (L, FOX_HEADS), f32, 1.0, 5.0),
        'moba_q_gain': gain(ks[9], (L, HEAD_DIM)),
        'moba_k_gain': gain(ks[10], (L, HEAD_DIM)),
        'fox_q_gain': gain(ks[11], (L, HEAD_DIM)),
        'fox_k_gain': gain(ks[12], (L, HEAD_DIM)),
        'norm_mem': gain(ks[13], (L, D_MODEL)),
        'w_mem_kv': dense(ks[14], (L, D_MODEL, 2 * MEM_WIDTH), D_MODEL),
        'mem_q_gain': gain(ks[15], (L, MEM_HEAD_DIM)),
        'mem_k_gain': gain(ks[16], (L, MEM_HEAD_DIM)),
        'pool_mix': dense(ks[17], (L, len(POOL_WINDOWS), POOL_GROUP, POOL_GROUP), POOL_GROUP),
        'pool_scale': gain(ks[18], (L, POOL_WIDTH)),
        'w_branch': dense(ks[19], (L, N_BRANCH, BRANCH_WIDTH, D_MODEL), BRANCH_WIDTH),
        'w_out': dense(ks[20], (L, D_MODEL, D_MODEL), D_MODEL),
        'norm_ffn2': gain(ks[21], (L, D_MODEL)),
        'w_ffn2_in': dense(ks[22], (L, D_MODEL, 2 * D_FF), D_MODEL),
        'w_ffn2_out': dense(ks[23], (L, D_FF, D_MODEL), D_FF),
    }

def reference(x, mem, positions, norm_ffn1, w_ffn1_in, w_ffn1_out, norm_mix, w_in, b_forget,
              moba_q_gain, moba_k_gain, fox_q_gain, fox_k_gain, norm_mem, w_mem_kv,
              mem_q_gain, mem_k_gain, pool_mix, pool_scale, w_branch, w_out,
              norm_ffn2, w_ffn2_in, w_ffn2_out):
    for l in range(DEPTH):
        x = x + 0.5 * swiglu(rms_norm(x, norm_ffn1[l]), w_ffn1_in[l], w_ffn1_out[l])
        x = x + hybrid_mixer(rms_norm(x, norm_mix[l]), mem, positions, w_in[l], b_forget[l],
                             moba_q_gain[l], moba_k_gain[l], fox_q_gain[l], fox_k_gain[l],
                             norm_mem[l], w_mem_kv[l], mem_q_gain[l], mem_k_gain[l],
                             pool_mix[l], pool_scale[l], w_branch[l], w_out[l])
        x = x + 0.5 * swiglu(rms_norm(x, norm_ffn2[l]), w_ffn2_in[l], w_ffn2_out[l])
    return x


_drawn_inputs = setup_inputs


def setup_inputs(seed=0):
    import zlib

    import numpy as np

    out = dict(_drawn_inputs(seed))
    spreads = {}
    factors = {'moba_q_gain': 8.0,
     'moba_k_gain': 8.0,
     'fox_q_gain': 5.616,
     'fox_k_gain': 6.667,
     'norm_mem': 8.0,
     'mem_q_gain': 8.0,
     'mem_k_gain': 8.0}
    for name, (base, spread) in spreads.items():
        noise = np.random.default_rng([zlib.crc32(name.encode()), seed]).standard_normal(out[name].shape)
        drawn = base * np.exp(spread * noise) if base else spread * noise
        out[name] = __import__('jax').numpy.asarray(drawn.astype(out[name].dtype))
    for name, factor in factors.items():
        out[name] = (out[name] * factor).astype(out[name].dtype)
    return out
```

```python
from contextlib import ExitStack

import numpy as np

import concourse.bass as bass
from concourse import mybir

F32 = mybir.dt.float32
F32R = mybir.dt.float32r
I32 = mybir.dt.int32
ACT = mybir.ActivationFunctionType
ALU = mybir.AluOpType
AX = mybir.AxisListType

P = 128
DEPTH, SEQ, DM, DFF = 2, 256, 1024, 2816
NT = SEQ // P
KC = DM // P
FC = DFF // P
HD, NH = 64, 8
MHD, MH = 128, 4
BW, BC = 512, 4
EPS = 1e-6
WINDOWS = (2, 4, 8, 16)
NEG = -1e30
IN_F = 6 * NH * HD
IN_POOL = IN_F + NH
IN_MEMQ = IN_POOL + BW
IN_GATE = IN_MEMQ + BW

RAW, SLOTS = 4, 4
LOADW, UNITW = 2048, 1024

FFN_STEPS = FC + FC // 2
MIX0 = FFN_STEPS
BLOCKS = [("mk", 0), ("mv", 1), ("qa", 2), ("ka", 3), ("va", 4), ("qc", 5), ("kc", 6)]
MIX = []


def _blocks():
    b = 0

    def proj(kind, arg=None):
        nonlocal b
        MIX.append((kind, arg, b, 0))
        MIX.append((kind, arg, b, 1))
        b += 1

    for kind in ("mk", "mv", "qa", "ka", "va", "qc", "kc"):
        proj(kind)
    MIX.append(("f", None, None, 0))
    for kind in ("qm", "vc", "pu"):
        proj(kind)
    for n in (1, 0, 2, 3):
        for dh in range(2):
            MIX.append(("gate", (n, dh), b, 0))
            if (n, dh) == (1, 0):
                MIX.append(("mixing", None, None, 0))
            MIX.append(("gate", (n, dh), b, 1))
            MIX.append(("y", (n, dh), b + 1, 0))
            b += 2
    for j in range(KC // 2):
        MIX.append(("out", j, None, 0))
    return b


N_BLOCKS = _blocks()
FFN2_0 = MIX0 + len(MIX)
STEPS = FFN2_0 + FFN_STEPS
UNITS = 2 * STEPS
assert STEPS % RAW == 0 and UNITS % SLOTS == 0

BLOCK_KIND = {}
for kind, arg, b, half in MIX:
    if b is not None:
        BLOCK_KIND[b] = kind
BY_ACT = ("mv", "va", "vc", "pu", "gate")


def taken_before(b):
    by_act = BLOCK_KIND[b] in BY_ACT
    return by_act, sum((BLOCK_KIND[i] in BY_ACT) == by_act for i in range(b + 1))


def _step_of(kind, arg=None, half=0):
    return MIX0 + next(i for i, s in enumerate(MIX) if s[0] == kind and s[1] == arg and s[3] == half)


TASKS = {}
for s, task in [
    (_step_of("mk", None, 1), ("norm", None)),
    (_step_of("va"), ("qkT", 0)),
    (_step_of("va", None, 1), ("scores", 0)),
    (_step_of("qc", None, 1), ("probsT", 0)),
    (_step_of("kc"), ("values", 0)), (_step_of("kc"), ("scores", 1)),
    (_step_of("f"), ("probsT", 1)),
    (_step_of("qm"), ("values", 1)), (_step_of("qm"), ("cumsum", None)),
    (_step_of("qm", None, 1), ("qkT", 1)),
    (_step_of("vc"), ("scores", 2)),
    (_step_of("pu"), ("probsT", 2)),
    (_step_of("pu", None, 1), ("values", 2)),
    (_step_of("gate", (1, 0)), ("pool", None)),
    (_step_of("y", (1, 0)), ("scores", 3)),
    (_step_of("gate", (1, 1), 1), ("probsT", 3)),
    (_step_of("y", (1, 1)), ("values", 3)),
    (_step_of("gate", (0, 0)), ("oT", 0)),
    (_step_of("gate", (0, 0), 1), ("oT", 1)),
    (_step_of("y", (0, 0)), ("qkT", 2)),
    (_step_of("gate", (0, 1)), ("scores", 4)),
    (_step_of("y", (0, 1)), ("probsT", 4)),
    (_step_of("gate", (2, 0)), ("values", 4)), (_step_of("gate", (2, 0)), ("scores", 5)),
    (_step_of("y", (2, 0)), ("probsT", 5)),
    (_step_of("gate", (2, 1)), ("values", 5)),
    (_step_of("y", (2, 1)), ("oT", 2)),
    (_step_of("gate", (3, 1)), ("zT", 0)),
    (_step_of("out", 0), ("zT", 1)),
]:
    TASKS.setdefault(s, []).append(task)

SPLITS = ["pooled", "mixed", "o0", "o1", "o2", "z0", "z1"]
NORMED = ["mk", "qa", "ka", "qc", "kc", "qm"]


class Tally:

    def __init__(self, sem, per_layer, credit=0):
        self.sem, self.per_layer, self.credit = sem, per_layer, credit

    def at(self, layer, count):
        return layer * self.per_layer + (self.credit + count)


def build(nc, x_d, mem_d, w1i_d, w1o_d, win_d, wkv_d, pmix_d, wbr_d, wout_d, w2i_d, w2o_d,
          gains_d, pos_d, const_d, sel_d, freq_d, out_d):
    ctx = ExitStack()
    with ctx:
        def sb(name, shape, dt=F32, scope=ctx):
            return scope.enter_context(nc.sbuf_tensor(name, shape, dt))

        const = sb("const", [P, const_d.shape[1]])
        ident = const[:, 0:P]
        mask = const[:, P:P + SEQ]
        upto = const[:, 384:384 + SEQ]
        band = const[:, 640:].rearrange("p (g c) -> p g c", g=4)
        sel = sb("sel", [NH, NH * P])
        freq = sb("freq", [P, 8])
        NORM_AT, POOL_AT, HEAD_AT, FORGET_AT, MOBA_AT, N_GAINS = 0, 32, 36, 40, 48, 176
        gains = sb("gains", [P, DEPTH, N_GAINS])
        own = sb("own", [P, 1, N_GAINS])
        pos_i = sb("pos_i", [P, NT], I32)
        pos_f = sb("pos_f", [P, NT])
        ang = sb("ang", [P, NT, 8])
        turns = sb("turns", [P, NT, 8])
        absang = sb("absang", [P, NT, 8])
        cosv = sb("cosv", [P, NT, 8])
        sinv = sb("sinv", [P, NT, 8])
        ss = sb("ss", [P, 2])
        ms = sb("ms", [P, 16])
        rs = sb("rs", [P, 16])
        ra = sb("ra", [P, 16])
        rb = sb("rb", [P, 16])
        hss = sb("hss", [P, 16])
        rot = sb("rot", [P, 4, NT, NH, 8])
        mx = sb("mx", [P, 8])
        nmx = sb("nmx", [P, 8])
        den = sb("den", [P, 8])
        rden = sb("rden", [P, 8])
        fz = sb("fz", [P, NT, NH])
        fna = sb("fna", [P, NT, NH])
        fe = sb("fe", [P, NT, NH])
        fl = sb("fl", [P, NT, NH])
        lf = sb("lf", [P, NT, NH])
        negc = sb("negc", [NH, SEQ])
        x = sb("x", [P, NT, DM])
        hT = [sb("hT_hi", [P, KC, SEQ], F32R), sb("hT_lo", [P, KC, SEQ], F32R)]
        raw = sb("raw", [P, RAW, LOADW])
        ring = [sb("ring_hi", [P, SLOTS, UNITW], F32R), sb("ring_lo", [P, SLOTS, UNITW], F32R)]
        with ExitStack() as ffn:
            act_hi = sb("act_hi", [P, FC, SEQ], F32R, ffn)
            act_lo = sb("act_lo", [P, FC, SEQ], F32R, ffn)
            silu = sb("silu", [P, 2, SEQ], F32, ffn)
            prod = sb("prod", [P, 2, SEQ], F32, ffn)
        qk = sb("qk", [P, 2, NT, BW])
        vals = sb("vals", [P, 3, NT, BW])
        qkT_buf = sb("qkT", [P, 2, 2, BC, SEQ])
        kmem = sb("kmem", [P, NT, BW])
        with ExitStack() as pooling:
            pooledT = [sb("pooledT_hi", [P, BC, SEQ], F32R, pooling), sb("pooledT_lo", [P, BC, SEQ], F32R, pooling)]
        probs = sb("probs", [P, 1536])
        pT = sb("pT", [P, 3, 512])
        gate = sb("gate", [P, 2, NT, BW])
        xn = gate[:, :, :, :].rearrange("p a t c -> p a (t c)")
        with ExitStack() as early:
            memx = sb("memx", [P, NT, DM], F32, early)
        brT = [[sb(f"brT{i}_{part}", [P, BC, SEQ], F32R) for part in ("hi", "lo")] for i in range(2)]
        with ExitStack() as early:
            memhT = [sb("memhT_hi", [P, KC, SEQ], F32R, early), sb("memhT_lo", [P, KC, SEQ], F32R, early)]
        o = sb("o", [P, 3, NT, BW])
        z = sb("z", [P, NT, DM])

        bank = [ctx.enter_context(nc.psum_tensor(f"bank{i}", [P, 512], F32)) for i in range(8)]

        def tally(name, per_layer, credit=0):
            return Tally(ctx.enter_context(nc.semaphore(name)), per_layer, credit)

        setup_loads = ctx.enter_context(nc.semaphore("setup_loads"))
        x_loaded = ctx.enter_context(nc.semaphore("x_loaded"))
        setup_step = ctx.enter_context(nc.semaphore("setup_step"))
        trig_done = ctx.enter_context(nc.semaphore("trig_done"))
        stored = ctx.enter_context(nc.semaphore("stored"))
        raw_ready = [tally(f"raw_ready{i}", 16 * STEPS // RAW) for i in range(RAW)]
        hi_done = tally("hi_done", UNITS)
        lo_done = tally("lo_done", UNITS, 2 * RAW)
        used = tally("used", UNITS, SLOTS)
        mem_loaded = tally("mem_loaded", 16)
        own_ready = tally("own_ready", 1)
        x_ready = tally("x_ready", 6, 1)
        sumsq = tally("sumsq", 8)
        xn_ready = tally("xn_ready", 8)
        xnT = tally("xnT", 16)
        h_hi = tally("h_hi", 16)
        h_ready = tally("h_ready", 16)
        silu_done = tally("silu_done", 2 * FC)
        prod_done = tally("prod_done", 2 * FC, 4)
        act_hi_done = tally("act_hi_done", 2 * FC)
        act_ready = tally("act_ready", 2 * FC)
        rows0_ready = tally("rows0_ready", 3)
        taken_act = tally("taken_act", sum(k in BY_ACT for k in BLOCK_KIND.values()))
        taken_dve = tally("taken_dve", sum(k not in BY_ACT for k in BLOCK_KIND.values()))
        squares = tally("squares", 2 * len(NORMED))
        qkT_ps = tally("qkT_ps", 3)
        qT_ready = tally("qT_ready", 3)
        kT_ready = tally("kT_ready", 3)
        scores_ready = tally("scores_ready", 6)
        max_ready = tally("max_ready", 6)
        probs_ready = tally("probs_ready", 6)
        pT_ps = tally("pT_ps", 6)
        pT_act = tally("pT_act", 6)
        pT_dve = tally("pT_dve", 6)
        pv_ready = tally("pv_ready", 6)
        o_ready = tally("o_ready", 6)
        fna_ready = tally("fna_ready", 1)
        fe_done = tally("fe_done", 1)
        fl_done = tally("fl_done", 1)
        lf_ready = tally("lf_ready", 1)
        c_ready = tally("c_ready", 1)
        negc_ready = tally("negc_ready", 1)
        split_ps = tally("split_ps", 2 * len(SPLITS) - 2)
        split_hi = tally("split_hi", 2 * len(SPLITS))
        split_lo = tally("split_lo", 2 * len(SPLITS))
        VLINKS = 145
        vlink = tally("vlink", VLINKS)

        def unit_words(step, k):
            local = step if step < MIX0 else step - FFN2_0
            if (step < MIX0 or step >= FFN2_0) and local < FC:
                i, half = divmod(local, 2)
                m = step - local + 2 * i + k
                view = raw[:, m % RAW, :].rearrange("p (k c) -> p k c", k=KC)[:, :, half * P:(half + 1) * P]
                return m, view, UNITW
            n = UNITW
            if MIX0 <= step < FFN2_0:
                n = {"f": KC * NH // 2, "mixing": BW // 2}.get(MIX[step - MIX0][0], UNITW)
            return step, raw[:, step % RAW, k * n:(k + 1) * n], n

        def unit_slot(part, step, k):
            return ring[part][:, (2 * step + k) % SLOTS, :]

        def unit_out(part, step, k):
            _, view, n = unit_words(step, k)
            slot = unit_slot(part, step, k)[:, 0:n]
            return slot.rearrange("p (k c) -> p k c", k=KC) if len(view.shape) == 3 else slot

        def steps_in_loop(engine, first, body):
            with engine.Fori(0, FC // 4) as j:
                for c in range(4):
                    body(j, c)
            for c in range(FC // 4 * 4, FC):
                body(None, c)

        block = ctx.enter_context(nc.Block())

        @block.sync
        def _(sp):
            sp.dma_start(x[:, :, :], x_d[0].rearrange("(t p) d -> p t d", p=P)).then_inc(x_loaded, 16)

            def load(L, m, dst, src, j=None, gates_at=None):
                late = 1 if gates_at is not None and (m - RAW - gates_at) % 2 == 0 and m - RAW >= gates_at else 0
                need = lo_done.at(L, 2 * (m - RAW) + 2 + late)
                sp.wait_ge(lo_done.sem, need if j is None else need + 8 * j)
                sp.dma_start(dst, src).then_inc(raw_ready[m % RAW].sem, 16)

            def ffn_loads(L, base, w_in, w_out):
                def columns(j, i):
                    for k in range(2):
                        m = base + 2 * i + k
                        dst = raw[:, m % RAW, :].rearrange("p (k c) -> p k c", k=KC)
                        at = k * DFF + 2 * P * i
                        cols = slice(at, at + 2 * P) if j is None else bass.ds(j * (4 * P) + at, 2 * P)
                        src = w_in[bass.ds(L, 1), :, cols].rearrange("a (k p) c -> p (a k) c", p=P)
                        load(L, m, dst, src, j, base)
                columns(None, 0)
                columns(None, 1)
                with sp.Fori(0, FC // 4 - 1) as j:
                    columns(j, 2)
                    columns(j, 3)
                for i in range(FC // 4 * 2, FC // 2):
                    columns(None, i)
                if base == 0:
                    sp.dma_start(memx[:, :, :], mem_d[0].rearrange("(t p) d -> p t d", p=P)).then_inc(mem_loaded.sem, 16)
                for r in range(FC // 2):
                    m = base + FC + r
                    src = w_out[bass.ds(L, 1), 2 * P * r:2 * P * (r + 1), :].rearrange("a (h p) c -> p (a h) c", p=P)
                    load(L, m, raw[:, m % RAW, :].rearrange("p (h c) -> p h c", h=2), src, None, base if r < RAW else None)

            with sp.Fori(0, DEPTH) as L:
                ffn_loads(L, 0, w1i_d, w1o_d)
                for i, (kind, arg, b, half) in enumerate(MIX):
                    m = MIX0 + i
                    dst = raw[:, m % RAW, :]
                    rows = slice(half * BW, (half + 1) * BW)
                    if kind in ("mk", "mv"):
                        at = {"mk": 0, "mv": BW}[kind]
                        src = wkv_d[bass.ds(L, 1), rows, at:at + BW].rearrange("a (k p) c -> p (a k) c", p=P)
                        dst = dst.rearrange("p (k c) -> p k c", k=4)
                    elif kind == "f":
                        src = win_d[bass.ds(L, 1), :, IN_F:IN_F + NH].rearrange("a (k p) c -> p (a k) c", p=P)
                        dst = dst[:, 0:KC * NH].rearrange("p (k c) -> p k c", k=KC)
                    elif kind == "mixing":
                        src = pmix_d[bass.ds(L, 1)].rearrange("a g p e -> p (a g) e")
                        dst = dst[:, 0:BW].rearrange("p (g e) -> p g e", g=4)
                    elif kind == "y":
                        n, dh = arg
                        src = wbr_d.rearrange("l n (k p) c -> p (l n k) c", p=P)[:, bass.ds(L * (4 * BC) + n * BC, BC), dh * BW:(dh + 1) * BW]
                        dst = dst.rearrange("p (k c) -> p k c", k=BC)
                    elif kind == "out":
                        src = wout_d[bass.ds(L, 1), 2 * P * arg:2 * P * (arg + 1), :].rearrange("a (h p) c -> p (a h) c", p=P)
                        dst = dst.rearrange("p (h c) -> p h c", h=2)
                    else:
                        at = {"qa": 0, "ka": BW, "va": 2 * BW, "qc": 3 * BW, "kc": 4 * BW, "vc": 5 * BW,
                              "pu": IN_POOL, "qm": IN_MEMQ}.get(kind)
                        if kind == "gate":
                            at = IN_GATE + arg[0] * DM + arg[1] * BW
                        src = win_d[bass.ds(L, 1), rows, at:at + BW].rearrange("a (k p) c -> p (a k) c", p=P)
                        dst = dst.rearrange("p (k c) -> p k c", k=4)
                    load(L, m, dst, src)
                ffn_loads(L, FFN2_0, w2i_d, w2o_d)

            for t in range(NT):
                sp.wait_ge(x_ready.sem, x_ready.at(DEPTH - 1, 4 + t + 1))
                sp.dma_start(out_d[0, t * P:(t + 1) * P, :], x[:, t, :]).then_inc(stored, 16)
            sp.wait_ge(stored, 16 * NT)

        @block.gpsimd
        def _(pool):
            pool.dma_start(const[:, :], const_d).then_inc(setup_loads, 16)
            pool.dma_start(sel[:, :], sel_d).then_inc(setup_loads, 16)
            pool.dma_start(freq[:, :], freq_d).then_inc(setup_loads, 16)
            pool.dma_start(pos_i[:, :], pos_d).then_inc(setup_loads, 16)
            pool.dma_start(gains[:, :, :], gains_d).then_inc(setup_loads, 16)
        N_SETUP = 5

        @block.tensor
        def _(pe):
            def three(out, act_parts, weight_parts, first, last, moving_weights):
                for n, (a, w) in enumerate(((0, 0), (0, 1), (1, 0))):
                    lhsT, rhs = (act_parts[a], weight_parts[w]) if moving_weights else (weight_parts[w], act_parts[a])
                    mm = pe.matmul(out, lhsT, rhs, start=first and n == 0, stop=last and n == 2)
                return mm

            def wait_unit(L, n, j=None):
                need = lo_done.at(L, n + 1)
                pe.wait_ge(lo_done.sem, need if j is None else need + 8 * j)

            def norm_transposes(L, index, banks):
                pe.wait_ge(xn_ready.sem, xn_ready.at(L, 2 * index + 2))
                for b in range(4):
                    for kc in (2 * b, 2 * b + 1):
                        for t in range(NT):
                            at = (kc % 2) * SEQ + t * P
                            mm = pe.transpose(bank[banks + b][:, at:at + P], xn[:, t, kc * P:(kc + 1) * P], ident)
                    mm.then_inc(xnT.sem, 1)

            def hidden(L, base, first_chunk, norm):
                def body(j, c):
                    n = 2 * (base + c)
                    need = prod_done.at(L, first_chunk + c + 1 - 4)
                    pe.wait_ge(prod_done.sem, need if j is None else need + 4 * j)
                    for k in range(2):
                        wait_unit(L, n + k, j)
                        w = [unit_slot(part, base + c, k).rearrange("p (k c) -> p k c", k=KC) for part in range(2)]
                        for kc in range(KC):
                            if c == 0 and k == 0 and kc % 2 == 0:
                                pe.wait_ge(h_ready.sem, h_ready.at(L, 4 * norm + kc // 2 + 1))
                            mm = three(bank[c % 4][:, k * SEQ:(k + 1) * SEQ], [hT[p][:, kc, :] for p in range(2)],
                                       [w[p][:, kc, :] for p in range(2)], kc == 0, kc == KC - 1, False)
                        mm.then_inc(used.sem, 1)
                return body

            def rows(L, step, acts, first, last):
                for k in range(2):
                    wait_unit(L, 2 * step + k)
                    w = [unit_slot(part, step, k) for part in range(2)]
                    for t in range(NT):
                        a = [acts[part][k][:, t * P:(t + 1) * P] for part in range(2)]
                        for (ap, wp) in ((0, 0), (0, 1), (1, 0)):
                            for half in range(2):
                                mm = pe.matmul(bank[4 + 2 * t + half][:, :], a[ap], w[wp][:, half * 512:(half + 1) * 512],
                                               start=first and k == 0 and (ap, wp) == (0, 0),
                                               stop=last and k == 1 and ap == 1)
                        if last and k == 1 and t == 0:
                            mm.then_inc(rows0_ready.sem, 1)
                    mm.then_inc(used.sem, 1)

            def feed_forward(L, which, base):
                steps_in_loop(pe, base, hidden(L, base, which * FC, 3 * which))
                for r in range(FC // 2):
                    pe.wait_ge(act_ready.sem, act_ready.at(L, which * FC + 2 * r + 2))
                    rows(L, base + FC + r, [[a[:, 2 * r + k, :] for k in range(2)] for a in (act_hi, act_lo)],
                         r == 0, r == FC // 2 - 1)
                    if which == 0 and r == 2:
                        pe.wait_ge(prod_done.sem, prod_done.at(L, FC))
                        norm_transposes(L, 1, 0)

            def heads(L, g):
                br = g // 2
                buf = qkT_buf[:, br % 2]
                odd = g % 2
                hs = [(2 * c + odd, c, HD * odd) for c in range(BC)] if br < 2 else [(h, h, 0) for h in (2 * odd, 2 * odd + 1)]
                return br, buf, hs

            def task(L, stage, arg):
                if stage == "norm":
                    norm_transposes(L, 2, 4)
                elif stage == "qkT":
                    pe.wait_ge(taken_dve.sem, taken_dve.at(L, {0: 3, 1: 5, 2: 6}[arg]))
                    if arg == 1:
                        pe.wait_ge(o_ready.sem, o_ready.at(L, 2))
                        pe.wait_ge(negc_ready.sem, negc_ready.at(L, 1))
                    if arg == 2:
                        pe.wait_ge(split_lo.sem, split_lo.at(L, 2 * SPLITS.index("o1") + 2))
                    for i in range(2):
                        src = qk[:, i] if arg < 2 or i == 0 else kmem
                        for c in range(BC):
                            for t in range(NT):
                                at = (c % 2) * SEQ + t * P
                                mm = pe.transpose(bank[4 + 2 * i + c // 2][:, at:at + P], src[:, t, c * P:(c + 1) * P], ident)
                    mm.then_inc(qkT_ps.sem, 1)
                elif stage == "scores":
                    br, buf, hs = heads(L, arg)
                    pe.wait_ge(qT_ready.sem, qT_ready.at(L, br + 1))
                    pe.wait_ge(kT_ready.sem, kT_ready.at(L, br + 1))
                    if arg:
                        pe.wait_ge(pT_act.sem, pT_act.at(L, arg))
                        pe.wait_ge(pT_dve.sem, pT_dve.at(L, arg))
                    if arg == 3:
                        pe.wait_ge(split_lo.sem, split_lo.at(L, 2 * SPLITS.index("mixed") + 2))
                    for i, (h, c, p) in enumerate(hs):
                        q, k = buf[p:p + (HD if br < 2 else MHD), 0, c, :], buf[p:p + (HD if br < 2 else MHD), 1, c, :]
                        if br < 2:
                            outs = [(bank[4][:, i * P:(i + 1) * P], 0, P),
                                    (bank[5 + i // 2][:, (i % 2) * SEQ:(i % 2 + 1) * SEQ], 1, SEQ)]
                        else:
                            outs = [(bank[4 + t][:, i * SEQ:(i + 1) * SEQ], t, SEQ) for t in range(NT)]
                        for out, t, keys in outs:
                            mm = pe.matmul(out, q[:, t * P:(t + 1) * P], k[:, 0:keys], start=True, stop=br != 1)
                            if br == 1:
                                mm = pe.matmul(out, sel[:, h * P:(h + 1) * P], negc[:, 0:keys], start=False, stop=True)
                    mm.then_inc(scores_ready.sem, 1)
                elif stage == "probsT":
                    br, buf, hs = heads(L, arg)
                    pe.wait_ge(probs_ready.sem, probs_ready.at(L, arg + 1))
                    for i in range(len(hs)):
                        if br < 2:
                            tiles = [(4, i, probs[:, i * P:(i + 1) * P])] + [
                                (5 + kt, i, probs[:, 512 + i * SEQ + kt * P:512 + i * SEQ + (kt + 1) * P]) for kt in range(2)]
                        else:
                            tiles = [(4 + t, 2 * i + kt, probs[:, t * 512 + i * SEQ + kt * P:t * 512 + i * SEQ + (kt + 1) * P])
                                     for t in range(NT) for kt in range(2)]
                        for b, at, src in tiles:
                            mm = pe.transpose(bank[b][:, at * P:(at + 1) * P], src, ident)
                    mm.then_inc(pT_ps.sem, 1)
                elif stage == "values":
                    br, buf, hs = heads(L, arg)
                    pe.wait_ge(pT_act.sem, pT_act.at(L, arg + 1))
                    pe.wait_ge(pT_dve.sem, pT_dve.at(L, arg + 1))
                    pe.wait_ge(taken_act.sem, taken_act.at(L, {0: 2, 1: 3, 2: 1}[br]))
                    if arg:
                        pe.wait_ge(o_ready.sem, o_ready.at(L, arg))
                    if arg == 1:
                        pe.wait_ge(fna_ready.sem, fna_ready.at(L, 1))
                    if arg == 4:
                        pe.wait_ge(kT_ready.sem, kT_ready.at(L, 3))
                    for i, (h, c, p) in enumerate(hs):
                        if br < 2:
                            for t in range(NT):
                                out = bank[7][:, t * SEQ + i * HD:t * SEQ + (i + 1) * HD]
                                for kt in range(t + 1):
                                    mm = pe.matmul(out, pT[:, t + kt, i * P:(i + 1) * P], vals[:, br, kt, h * HD:(h + 1) * HD],
                                                   start=kt == 0, stop=kt == t)
                        else:
                            for t in range(NT):
                                out = bank[7][:, t * SEQ + i * MHD:t * SEQ + (i + 1) * MHD]
                                for kt in range(2):
                                    mm = pe.matmul(out, pT[:, t, (2 * i + kt) * P:(2 * i + kt + 1) * P],
                                                   vals[:, 2, kt, h * MHD:(h + 1) * MHD], start=kt == 0, stop=kt == 1)
                    mm.then_inc(pv_ready.sem, 1)
                elif stage == "cumsum":
                    pe.wait_ge(lf_ready.sem, lf_ready.at(L, 1))
                    pe.wait_ge(pT_act.sem, pT_act.at(L, 2))
                    pe.matmul(bank[4][0:NH, 0:SEQ], lf[:, 0, :], upto, start=True, stop=False)
                    pe.matmul(bank[4][0:NH, P:SEQ], lf[:, 1, :], upto[:, 0:P], start=False, stop=True).then_inc(c_ready.sem, 1)
                elif stage == "pool":
                    pe.wait_ge(taken_act.sem, taken_act.at(L, 4))
                    pe.wait_ge(pT_act.sem, pT_act.at(L, 3))
                    pe.wait_ge(pT_dve.sem, pT_dve.at(L, 3))
                    for g in range(4):
                        out = bank[4 + g // 2][:, (g % 2) * SEQ:(g % 2 + 1) * SEQ]
                        pe.matmul(out, qk[:, 1, 0, g * P:(g + 1) * P], band[:, g, 0:SEQ], start=True, stop=False)
                        mm = pe.matmul(out[:, P:SEQ], qk[:, 1, 1, g * P:(g + 1) * P], band[:, g, SEQ:SEQ + P],
                                       start=False, stop=True)
                        if g % 2:
                            mm.then_inc(split_ps.sem, 1)
                elif stage in ("oT", "zT"):
                    if stage == "oT":
                        pe.wait_ge(o_ready.sem, o_ready.at(L, 2 * arg + 2))
                        first = 6 if arg == 1 else 4
                        src = o[:, arg]
                        if arg == 0:
                            pe.wait_ge(pT_act.sem, pT_act.at(L, 4))
                            pe.wait_ge(pT_dve.sem, pT_dve.at(L, 4))
                        if arg == 2:
                            pe.wait_ge(pT_act.sem, pT_act.at(L, 6))
                            pe.wait_ge(pT_dve.sem, pT_dve.at(L, 6))
                    else:
                        pe.wait_ge(taken_dve.sem, taken_dve.at(L, 13 + arg))
                        first = 4 if arg == 0 else 0
                        src = z[:, :, arg * BW:(arg + 1) * BW]
                        if arg == 0:
                            pe.wait_ge(split_lo.sem, split_lo.at(L, 2 * SPLITS.index("o2") + 2))
                    for c in range(BC):
                        for t in range(NT):
                            at = (c % 2) * SEQ + t * P
                            mm = pe.transpose(bank[first + c // 2][:, at:at + P], src[:, t, c * P:(c + 1) * P], ident)
                        if c % 2:
                            mm.then_inc(split_ps.sem, 1)

            def mixer(L):
                for i, (kind, arg, b, half) in enumerate(MIX):
                    s = MIX0 + i
                    if b is not None and b >= 2 and half == 0:
                        by_act, count = taken_before(b - 2)
                        sig = taken_act if by_act else taken_dve
                        pe.wait_ge(sig.sem, sig.at(L, count))
                    if kind in ("mk", "mv") and half == 0:
                        pe.wait_ge(h_ready.sem, h_ready.at(L, 8))
                    elif kind == "qa" and half == 0:
                        pe.wait_ge(h_ready.sem, h_ready.at(L, 12))
                    if kind == "y":
                        pe.wait_ge(split_lo.sem, split_lo.at(L, 2 * SPLITS.index({0: "o0", 1: "mixed", 2: "o1", 3: "o2"}[arg[0]]) + 2))
                        acts = brT[{1: 0, 0: 1, 2: 0, 3: 1}[arg[0]]]
                    elif kind in ("mk", "mv"):
                        acts = memhT
                    else:
                        acts = hT
                    if kind == "f":
                        pe.wait_ge(o_ready.sem, o_ready.at(L, 1))
                        for k in range(2):
                            wait_unit(L, 2 * s + k)
                        w = [[unit_slot(part, s, kc // 4)[:, (kc % 4) * NH:(kc % 4 + 1) * NH] for part in range(2)] for kc in range(KC)]
                        for t in range(NT):
                            for kc in range(KC):
                                mm = three(bank[7][:, t * NH:(t + 1) * NH], [acts[p][:, kc, t * P:(t + 1) * P] for p in range(2)],
                                           w[kc], kc == 0, kc == KC - 1, True)
                                if t == NT - 1 and kc == 3:
                                    mm.then_inc(used.sem, 1)
                        mm.then_inc(used.sem, 1)
                    elif kind == "mixing":
                        pe.wait_ge(split_lo.sem, split_lo.at(L, 2 * SPLITS.index("pooled") + 2))
                        pe.wait_ge(o_ready.sem, o_ready.at(L, 3))
                        for g in range(4):
                            if g % 2 == 0:
                                wait_unit(L, 2 * s + g // 2)
                            w = [unit_slot(part, s, g // 2)[:, (g % 2) * P:(g % 2 + 1) * P] for part in range(2)]
                            mm = three(bank[6 + g // 2][:, (g % 2) * SEQ:(g % 2 + 1) * SEQ],
                                       [pooledT[p][:, g, :] for p in range(2)], w, True, True, False)
                            if g % 2:
                                mm.then_inc(used.sem, 1)
                    elif kind == "out":
                        if arg % 2 == 0:
                            pe.wait_ge(split_lo.sem, split_lo.at(L, 2 * SPLITS.index("z0" if arg == 0 else "z1") + 2))
                        src = brT[0] if arg < 2 else hT
                        rows(L, s, [[src[part][:, 2 * (arg % 2) + k, :] for k in range(2)] for part in range(2)],
                             arg == 0, arg == KC // 2 - 1)
                    else:
                        nk = BC if kind == "y" else KC
                        for k in range(2):
                            wait_unit(L, 2 * s + k)
                            w = [unit_slot(part, s, k).rearrange("p (k c) -> p k c", k=2) for part in range(2)]
                            for kk in range(2):
                                kc = 4 * half + 2 * k + kk
                                for t in range(NT):
                                    mm = three(bank[2 * (b % 2) + t][:, :], [acts[p][:, kc, t * P:(t + 1) * P] for p in range(2)],
                                               [w[p][:, kk, :] for p in range(2)], kc == 0, kc == nk - 1, True)
                            mm.then_inc(used.sem, 1)
                    for stage, targ in TASKS.get(s, ()):
                        task(L, stage, targ)

            pe.sem_inc(used.sem, used.credit)
            pe.wait_ge(setup_loads, 16 * N_SETUP)
            with pe.Fori(0, DEPTH) as L:
                norm_transposes(L, 0, 4)
                feed_forward(L, 0, 0)
                mixer(L)
                norm_transposes(L, 3, 4)
                feed_forward(L, 1, FFN2_0)

        def split_target(name):
            return {"pooled": (pooledT, 4, 1.0), "o0": (brT[1], 4, 1.0), "o1": (brT[0], 6, 1.0), "o2": (brT[1], 4, 1.0),
                    "z0": (brT[0], 4, 0.5), "z1": (hT, 0, 0.5)}[name]

        PS_ORDER = [name for name in SPLITS if name != "mixed"]
        HEAD_DST = {"mk": (kmem, MH), "qa": (qk[:, 0], NH), "ka": (qk[:, 1], NH), "qc": (qk[:, 0], NH),
                    "kc": (qk[:, 1], NH), "qm": (qk[:, 0], MH)}
        GATES = [arg for kind, arg, _, _ in MIX if kind == "y"]

        def gain(at):
            return own[:, 0, at:at + 1]

        @block.scalar
        def _(act):
            def hi(L, step, k, j=None):
                n = 2 * step + k
                m, view, _ = unit_words(step, k)
                arrived, free = raw_ready[m % RAW].at(L, 16 * (m // RAW + 1)), used.at(L, n + 1 - SLOTS)
                act.wait_ge(raw_ready[m % RAW].sem, arrived if j is None else arrived + 16 * j)
                act.wait_ge(used.sem, free if j is None else free + 8 * j)
                act.activation(unit_out(0, step, k), view, ACT.Copy).then_inc(hi_done.sem, 1)

            def norm(L, index, src, dst, banks, ready):
                for t in range(NT):
                    ready(t)
                    act.activation(xn[:, t, :], src[:, t, :], ACT.Square, accum_out=ss[:, t:t + 1]).then_inc(sumsq.sem, 1)

            def norm_hi(L, index, dst, banks):
                if index == 0:
                    act.wait_ge(own_ready.sem, own_ready.at(L, 1))
                for b in range(4):
                    act.wait_ge(xnT.sem, xnT.at(L, 4 * index + b + 1))
                    for kc in (2 * b, 2 * b + 1):
                        last = act.activation(dst[0][:, kc, :], bank[banks + b][:, (kc % 2) * SEQ:(kc % 2 + 1) * SEQ], ACT.Copy,
                                              scale=gain(NORM_AT + index * KC + kc))
                    last.then_inc(h_hi.sem, 1)

            def hidden(L, base, first_chunk):
                def body(j, c):
                    s = base + c
                    def plus(value, per_turn):
                        return value if j is None else value + per_turn * j
                    hi(L, s + 2, 0, j)
                    act.wait_ge(used.sem, plus(used.at(L, 2 * s + 2), 8))
                    act.activation(silu[:, c % 2, :], bank[c % 4][:, 0:SEQ], ACT.Silu).then_inc(silu_done.sem, 1)
                    hi(L, s + 2, 1, j)
                    act.wait_ge(prod_done.sem, plus(prod_done.at(L, first_chunk + c + 1), 4))
                    dst = act_hi[:, c:c + 1, :] if j is None else act_hi[:, bass.ds(4 * j + c, 1), :]
                    act.activation(dst, prod[:, c % 2:c % 2 + 1, :], ACT.Copy).then_inc(act_hi_done.sem, 1)
                return body

            def ahead(L, s):
                if s + 2 < STEPS:
                    hi(L, s + 2, 0)
                    hi(L, s + 2, 1)

            def feed_forward(L, which, base):
                steps_in_loop(act, base, hidden(L, base, which * FC))
                for r in range(FC // 2):
                    ahead(L, base + FC + r)
                    if which == 0 and r == 0:
                        norm(L, 1, memx, memhT, 0, lambda t: act.wait_ge(mem_loaded.sem, mem_loaded.at(L, 16)))
                    if which == 0 and r == 2:
                        norm_hi(L, 1, memhT, 0)

            def split(L, name):
                dst, first, factor = split_target(name)
                at = 2 * PS_ORDER.index(name)
                for b in range(2):
                    act.wait_ge(split_ps.sem, split_ps.at(L, at + b + 1))
                    act.activation(dst[0][:, 2 * b:2 * b + 2, :], bank[first + b][:, :].rearrange("p (c t) -> p c t", c=2), ACT.Copy,
                                   scale=factor).then_inc(split_hi.sem, 1)

            def task(L, stage, arg):
                if stage == "norm":
                    norm_hi(L, 2, hT, 4)
                elif stage == "qkT":
                    act.wait_ge(qkT_ps.sem, qkT_ps.at(L, arg + 1))
                    for b in range(2):
                        last = act.activation(qkT_buf[:, arg % 2, 0, 2 * b:2 * b + 2, :],
                                              bank[4 + b][:, :].rearrange("p (c t) -> p c t", c=2), ACT.Copy,
                                              scale=1.0 if arg == 0 else gain(HEAD_AT + 2 * (arg - 1)))
                    last.then_inc(qT_ready.sem, 1)
                elif stage == "scores":
                    act.wait_ge(max_ready.sem, max_ready.at(L, arg + 1))
                    if arg < 4:
                        for i in range(4):
                            for t in range(NT):
                                p = probs[:, i * P:(i + 1) * P] if t == 0 else probs[:, 512 + i * SEQ:512 + (i + 1) * SEQ]
                                last = act.activation(p, p, ACT.Exp, bias=nmx[:, 4 * t + i:4 * t + i + 1], scale=HD ** -0.5,
                                                      accum_out=den[:, 4 * t + i:4 * t + i + 1])
                    else:
                        act.wait_ge(pT_ps.sem, pT_ps.at(L, arg))
                        for i in range(2):
                            for t in range(NT):
                                last = act.activation(probs[:, t * 512 + i * SEQ:t * 512 + (i + 1) * SEQ],
                                                      bank[4 + t][:, i * SEQ:(i + 1) * SEQ], ACT.Exp,
                                                      bias=nmx[:, 2 * t + i:2 * t + i + 1], scale=MHD ** -0.5,
                                                      accum_out=den[:, 2 * t + i:2 * t + i + 1])
                    last.then_inc(probs_ready.sem, 1)
                elif stage == "probsT":
                    act.wait_ge(pT_ps.sem, pT_ps.at(L, arg + 1))
                    act.activation(pT[:, 0, :], bank[4][:, :], ACT.Copy).then_inc(pT_act.sem, 1)
                elif stage == "pool":
                    split(L, "pooled")
                elif stage == "oT":
                    split(L, f"o{arg}")
                elif stage == "zT":
                    split(L, f"z{arg}")

            def serve(L, s, kind, arg, half):
                if kind == "f":
                    act.wait_ge(fna_ready.sem, fna_ready.at(L, 1))
                    act.activation(fe[:, :, :], fna[:, :, :], ACT.Exp).then_inc(fe_done.sem, 1)
                    act.wait_ge(fe_done.sem, fe_done.at(L, 1))
                    act.activation(fl[:, :, :], fe[:, :, :], ACT.Ln, bias=1.0).then_inc(fl_done.sem, 1)
                elif kind == "mixing":
                    for b in range(2):
                        act.wait_ge(used.sem, used.at(L, 2 * s + b + 1))
                        for g in (2 * b, 2 * b + 1):
                            last = act.activation(brT[0][0][:, g, :], bank[6 + b][:, (g % 2) * SEQ:(g % 2 + 1) * SEQ], ACT.Copy,
                                                  scale=gain(POOL_AT + g))
                        last.then_inc(split_hi.sem, 1)
                elif half == 1 and kind != "out":
                    act.wait_ge(used.sem, used.at(L, 2 * s + 2))
                    banks = [bank[2 * (MIX[s - MIX0][2] % 2) + t] for t in range(NT)]
                    if kind == "gate":
                        idx = GATES.index(arg)
                        if idx >= 2:
                            act.wait_ge(taken_dve.sem, taken_dve.at(L, 6 + idx - 1))
                        for t in range(NT):
                            last = act.activation(gate[:, idx % 2, t, :], banks[t][:, :], ACT.Tanh, scale=0.5)
                        last.then_inc(taken_act.sem, 1)
                    elif kind in BY_ACT:
                        if kind == "pu":
                            act.wait_ge(qkT_ps.sem, qkT_ps.at(L, 2))
                        dst = qk[:, 1] if kind == "pu" else vals[:, {"va": 0, "vc": 1, "mv": 2}[kind]]
                        for t in range(NT):
                            last = act.activation(dst[:, t, :], banks[t][:, :], ACT.Copy)
                        last.then_inc(taken_act.sem, 1)
                    else:
                        if kind in ("qc", "kc", "qm"):
                            act.wait_ge(qkT_ps.sem, qkT_ps.at(L, 2 if kind == "qm" else 1))
                        dst, heads = HEAD_DST[kind]
                        for t in range(NT):
                            act.activation(dst[:, t, :], banks[t][:, :], ACT.Square).then_inc(squares.sem, 1)

            def mixer(L):
                for i, (kind, arg, b, half) in enumerate(MIX):
                    ahead(L, MIX0 + i)
                    if i == 0:
                        norm(L, 2, x, hT, 4, lambda t: act.wait_ge(x_ready.sem, x_ready.at(L, t + 1)))
                    serve(L, MIX0 + i, kind, arg, half)
                    for stage, targ in TASKS.get(MIX0 + i, ()):
                        task(L, stage, targ)

            act.wait_ge(setup_step, ANGLE_LINKS)
            act.activation(sinv[:, :, :], ang[:, :, :], ACT.Sin).then_inc(trig_done, 1)
            act.activation(absang[:, :, :], ang[:, :, :], ACT.Abs).then_inc(trig_done, 1)
            act.wait_ge(trig_done, 2)
            act.wait_ge(setup_step, ANGLE_LINKS + 1)
            act.activation(cosv[:, :, :], turns[:, :, :], ACT.Sin).then_inc(trig_done, 1)
            with act.Fori(0, DEPTH) as L:
                for s in range(2):
                    for k in range(2):
                        hi(L, s, k)
                norm(L, 0, x, hT, 4, lambda t: act.wait_ge(x_ready.sem, x_ready.at(L, 0)))
                norm_hi(L, 0, hT, 4)
                feed_forward(L, 0, 0)
                mixer(L)
                norm(L, 3, x, hT, 4, lambda t: act.wait_ge(x_ready.sem, x_ready.at(L, 2 + t + 1)))
                norm_hi(L, 3, hT, 4)
                feed_forward(L, 1, FFN2_0)

        @block.vector
        def _(dve):
            links = [0]

            def link(L, ins):
                links[0] += 1
                ins.then_inc(vlink.sem, 1)
                dve.wait_ge(vlink.sem, vlink.at(L, links[0]))

            def lo(L, step, k, j=None):
                done = hi_done.at(L, 2 * step + k + 1)
                dve.wait_ge(hi_done.sem, done if j is None else done + 8 * j)
                _, view, _ = unit_words(step, k)
                dve.tensor_tensor(unit_out(1, step, k), view, unit_out(0, step, k).bitcast(F32), ALU.subtract)\
                    .then_inc(lo_done.sem, 1)

            def rsqrt(L, n, total, width):
                link(L, dve.tensor_scalar(ms[:, 0:n], total, 1.0 / width, EPS, ALU.mult, ALU.add))
                link(L, dve.tensor_scalar(rs[:, 0:n].bitcast(I32), ms[:, 0:n].bitcast(I32), -0.5, 1597463007.0, ALU.mult, ALU.add))
                for _ in range(3):
                    link(L, dve.scalar_tensor_tensor(ra[:, 0:n], rs[:, 0:n], -0.5, rs[:, 0:n], ALU.mult, ALU.mult))
                    link(L, dve.tensor_tensor(rb[:, 0:n], ra[:, 0:n], ms[:, 0:n], ALU.mult))
                    link(L, dve.scalar_tensor_tensor(rs[:, 0:n], rb[:, 0:n], 1.5, rs[:, 0:n], ALU.add, ALU.mult))

            def norm(L, index, src):
                dve.wait_ge(sumsq.sem, sumsq.at(L, 2 * index + 2))
                rsqrt(L, NT, ss[:, 0:NT], DM)
                for t in range(NT):
                    dve.tensor_scalar(xn[:, t, :], src[:, t, :], rs[:, t:t + 1], None, ALU.mult).then_inc(xn_ready.sem, 1)

            def norm_lo(L, index, dst, banks):
                for b in range(4):
                    dve.wait_ge(h_hi.sem, h_hi.at(L, 4 * index + b + 1))
                    for kc in (2 * b, 2 * b + 1):
                        last = dve.scalar_tensor_tensor(dst[1][:, kc, :], bank[banks + b][:, (kc % 2) * SEQ:(kc % 2 + 1) * SEQ],
                                                        gain(NORM_AT + index * KC + kc), dst[0][:, kc, :].bitcast(F32),
                                                        ALU.mult, ALU.subtract)
                    last.then_inc(h_ready.sem, 1)

            def hidden(L, base, first_chunk):
                def body(j, c):
                    s = base + c
                    def plus(value, per_turn):
                        return value if j is None else value + per_turn * j
                    lo(L, s + 2, 0, j)
                    dve.wait_ge(silu_done.sem, plus(silu_done.at(L, first_chunk + c + 1), 4))
                    dve.tensor_tensor(prod[:, c % 2, :], silu[:, c % 2, :], bank[c % 4][:, SEQ:2 * SEQ], ALU.mult)\
                        .then_inc(prod_done.sem, 1)
                    lo(L, s + 2, 1, j)
                    dve.wait_ge(act_hi_done.sem, plus(act_hi_done.at(L, first_chunk + c + 1), 4))
                    at = slice(c, c + 1) if j is None else bass.ds(4 * j + c, 1)
                    dve.tensor_tensor(act_lo[:, at, :], prod[:, c % 2:c % 2 + 1, :], act_hi[:, at, :].bitcast(F32), ALU.subtract)\
                        .then_inc(act_ready.sem, 1)
                return body

            def ahead(L, s):
                if s + 2 < STEPS:
                    lo(L, s + 2, 0)
                    lo(L, s + 2, 1)

            def add_rows(L, phase, last_step, factor):
                for t in range(NT):
                    if t == 0:
                        dve.wait_ge(rows0_ready.sem, rows0_ready.at(L, phase + 1))
                    else:
                        dve.wait_ge(used.sem, used.at(L, 2 * last_step + 2))
                    for half in range(2):
                        xs = x[:, t, half * 512:(half + 1) * 512]
                        last = dve.scalar_tensor_tensor(xs, bank[4 + 2 * t + half][:, :], factor, xs, ALU.mult, ALU.add)
                    last.then_inc(x_ready.sem, 1)

            def feed_forward(L, which, base):
                steps_in_loop(dve, base, hidden(L, base, which * FC))
                for r in range(FC // 2):
                    ahead(L, base + FC + r)
                    if which == 0 and r == 0:
                        norm(L, 1, memx)
                    if which == 0 and r == 2:
                        norm_lo(L, 1, memhT, 0)
                add_rows(L, 2 * which, base + FFN_STEPS - 1, 0.5)

            def split(L, name):
                dst, first, factor = split_target(name)
                at = 2 * SPLITS.index(name)
                for b in range(2):
                    dve.wait_ge(split_hi.sem, split_hi.at(L, at + b + 1))
                    chunks = slice(2 * b, 2 * b + 2)
                    dve.scalar_tensor_tensor(dst[1][:, chunks, :], bank[first + b][:, :].rearrange("p (c t) -> p c t", c=2), factor,
                                             dst[0][:, chunks, :].bitcast(F32), ALU.mult, ALU.subtract).then_inc(split_lo.sem, 1)

            def bc(ap, shape):
                return ap.to_broadcast(shape)

            def task(L, stage, arg):
                if stage == "norm":
                    norm_lo(L, 2, hT, 4)
                elif stage == "qkT":
                    dve.wait_ge(qkT_ps.sem, qkT_ps.at(L, arg + 1))
                    for b in range(2):
                        last = dve.tensor_scalar(qkT_buf[:, arg % 2, 1, 2 * b:2 * b + 2, :],
                                                 bank[6 + b][:, :].rearrange("p (c t) -> p c t", c=2),
                                                 1.0 if arg == 0 else gain(HEAD_AT + 2 * (arg - 1) + 1), None, ALU.mult)
                    last.then_inc(kT_ready.sem, 1)
                elif stage == "scores":
                    dve.wait_ge(scores_ready.sem, scores_ready.at(L, arg + 1))
                    if arg < 4:
                        if arg:
                            dve.wait_ge(pT_ps.sem, pT_ps.at(L, arg))
                        dve.tensor_tensor(probs[:, 0:512].rearrange("p (h k) -> p h k", h=4),
                                          bank[4][:, :].rearrange("p (h k) -> p h k", h=4),
                                          mask[:, None, P:SEQ].to_broadcast([P, 4, P]), ALU.add)
                        for b in range(2):
                            at = 512 + 512 * b
                            last = dve.tensor_tensor(probs[:, at:at + 512].rearrange("p (h k) -> p h k", h=2),
                                                     bank[5 + b][:, :].rearrange("p (h k) -> p h k", h=2),
                                                     mask[:, None, :].to_broadcast([P, 2, SEQ]), ALU.add)
                        link(L, last)
                        dve.tensor_reduce(mx[:, 0:4], probs[:, 0:512].rearrange("p (h k) -> p h k", h=4), axis=AX.X, op=ALU.max)
                        link(L, dve.tensor_reduce(mx[:, 4:8], probs[:, 512:].rearrange("p (h k) -> p h k", h=4), axis=AX.X, op=ALU.max))
                        dve.tensor_scalar(nmx[:, :], mx[:, :], -(HD ** -0.5), None, ALU.mult).then_inc(max_ready.sem, 1)
                    else:
                        for t in range(NT):
                            last = dve.tensor_reduce(mx[:, 2 * t:2 * t + 2], bank[4 + t][:, :].rearrange("p (h k) -> p h k", h=2),
                                                     axis=AX.X, op=ALU.max)
                        link(L, last)
                        dve.tensor_scalar(nmx[:, 0:4], mx[:, 0:4], -(MHD ** -0.5), None, ALU.mult).then_inc(max_ready.sem, 1)
                elif stage == "probsT":
                    dve.wait_ge(pT_ps.sem, pT_ps.at(L, arg + 1))
                    for b in range(2 if arg < 4 else 1):
                        last = dve.tensor_copy(pT[:, 1 + b, :], bank[5 + b][:, :])
                    last.then_inc(pT_dve.sem, 1)
                elif stage == "values":
                    br, n, d = arg // 2, 4 if arg < 4 else 2, HD if arg < 4 else MHD
                    dve.wait_ge(pv_ready.sem, pv_ready.at(L, arg + 1))
                    link(L, dve.reciprocal(rden[:, 0:2 * n], den[:, 0:2 * n]))
                    if arg < 4:
                        dst = o[:, br].rearrange("p t (h two d) -> p t h two d", two=2, d=d)[:, :, :, arg % 2, :]
                    else:
                        dst = o[:, br].rearrange("p t (two h d) -> p t two h d", two=2, d=d)[:, :, arg % 2]
                    dve.tensor_tensor(dst,
                                      bank[7][:, :].rearrange("p (t h d) -> p t h d", t=NT, h=n),
                                      rden[:, 0:2 * n].rearrange("p (t h) -> p t h", t=NT)[:, :, :, None].to_broadcast([P, NT, n, d]),
                                      ALU.mult).then_inc(o_ready.sem, 1)
                elif stage == "cumsum":
                    dve.wait_ge(c_ready.sem, c_ready.at(L, 1))
                    dve.tensor_scalar(negc[:, :], bank[4][0:NH, 0:SEQ], -float(HD ** 0.5), None, ALU.mult).then_inc(negc_ready.sem, 1)
                elif stage == "pool":
                    split(L, "pooled")
                elif stage == "oT":
                    split(L, f"o{arg}")
                elif stage == "zT":
                    split(L, f"z{arg}")

            def serve(L, s, kind, arg, half):
                if kind == "f":
                    dve.wait_ge(used.sem, used.at(L, 2 * s + 2))
                    link(L, dve.tensor_tensor(fz[:, :, :], bank[7][:, 0:NT * NH].rearrange("p (t h) -> p t h", t=NT),
                                              own[:, :, FORGET_AT:FORGET_AT + NH].to_broadcast([P, NT, NH]), ALU.add))
                    dve.scalar_tensor_tensor(fna[:, :, :], fz[:, :, :], -1.0, fz[:, :, :], ALU.mult, ALU.min).then_inc(fna_ready.sem, 1)
                    dve.wait_ge(fl_done.sem, fl_done.at(L, 1))
                    dve.scalar_tensor_tensor(lf[:, :, :], fz[:, :, :], 0.0, fl[:, :, :], ALU.min, ALU.subtract).then_inc(lf_ready.sem, 1)
                elif kind == "mixing":
                    at = 2 * SPLITS.index("mixed")
                    for b in range(2):
                        dve.wait_ge(split_hi.sem, split_hi.at(L, at + b + 1))
                        for g in (2 * b, 2 * b + 1):
                            last = dve.scalar_tensor_tensor(brT[0][1][:, g, :], bank[6 + b][:, (g % 2) * SEQ:(g % 2 + 1) * SEQ],
                                                            gain(POOL_AT + g), brT[0][0][:, g, :].bitcast(F32),
                                                            ALU.mult, ALU.subtract)
                        last.then_inc(split_lo.sem, 1)
                elif kind == "y":
                    n, dh = arg
                    idx = GATES.index(arg)
                    dve.wait_ge(taken_act.sem, taken_act.at(L, 4 + idx + 1))
                    dve.wait_ge(used.sem, used.at(L, 2 * s + 2))
                    banks = [bank[2 * (MIX[s - MIX0][2] % 2) + t] for t in range(NT)]
                    zs = [z[:, t, dh * BW:(dh + 1) * BW] for t in range(NT)]
                    gs = [gate[:, idx % 2, t, :] for t in range(NT)]
                    for t in range(NT):
                        last = dve.scalar_tensor_tensor(zs[t] if idx < 2 else gs[t], gs[t], 1.0, banks[t][:, :], ALU.add, ALU.mult)
                    if idx >= 2:
                        link(L, last)
                        for t in range(NT):
                            last = dve.tensor_tensor(zs[t], zs[t], gs[t], ALU.add)
                    last.then_inc(taken_dve.sem, 1)
                elif half == 1 and kind in NORMED:
                    dst, heads = HEAD_DST[kind]
                    d = BW // heads
                    banks = [bank[2 * (MIX[s - MIX0][2] % 2) + t] for t in range(NT)]
                    dve.wait_ge(squares.sem, squares.at(L, 2 * NORMED.index(kind) + 2))
                    link(L, dve.tensor_reduce(hss[:, 0:NT * heads].rearrange("p (t h) -> p t h", t=NT),
                                              dst[:, :, :].rearrange("p t (h d) -> p t h d", h=heads), axis=AX.X, op=ALU.add))
                    rsqrt(L, NT * heads, hss[:, 0:NT * heads], d)
                    for t in range(NT):
                        last = dve.tensor_tensor(dst[:, t, :].rearrange("p (h d) -> p h d", h=heads),
                                                 banks[t][:, :].rearrange("p (h d) -> p h d", h=heads),
                                                 rs[:, t * heads:(t + 1) * heads, None].to_broadcast([P, heads, d]), ALU.mult)
                    if kind in ("qa", "ka"):
                        link(L, last)
                        at = MOBA_AT + (0 if kind == "qa" else HD)
                        for t in range(NT):
                            rows = dst[:, t, :].rearrange("p (h d) -> p h d", h=heads)
                            last = dve.tensor_tensor(rows, rows, own[:, :, at:at + HD].to_broadcast([P, heads, HD]), ALU.mult)
                        link(L, last)
                        halves = [dst[:, :, :].rearrange("p t (h d) -> p t h d", h=heads)[:, :, :, 8 * i:8 * i + 8] for i in range(2)]
                        tables = [v[:, :, None, :].to_broadcast([P, NT, heads, 8]) for v in (cosv, sinv)]
                        for i, (a, b) in enumerate(((0, 0), (1, 1), (1, 0), (0, 1))):
                            last = dve.tensor_tensor(rot[:, i], halves[a], tables[b], ALU.mult)
                        link(L, last)
                        dve.tensor_tensor(halves[0], rot[:, 0], rot[:, 1], ALU.subtract)
                        last = dve.tensor_tensor(halves[1], rot[:, 2], rot[:, 3], ALU.add)
                    last.then_inc(taken_dve.sem, 1)
                elif kind == "out" and arg == KC // 2 - 1:
                    add_rows(L, 1, s, 1.0)

            def mixer(L):
                for i, (kind, arg, b, half) in enumerate(MIX):
                    ahead(L, MIX0 + i)
                    if i == 0:
                        norm(L, 2, x)
                    if kind != "out":
                        serve(L, MIX0 + i, kind, arg, half)
                    for stage, targ in TASKS.get(MIX0 + i, ()):
                        task(L, stage, targ)
                    if kind == "out":
                        serve(L, MIX0 + i, kind, arg, half)

            dve.sem_inc(lo_done.sem, lo_done.credit)
            dve.sem_inc(prod_done.sem, prod_done.credit)
            dve.wait_ge(x_loaded, 16)
            dve.sem_inc(x_ready.sem, x_ready.credit)

            step = [0]

            def setup(ins):
                step[0] += 1
                ins.then_inc(setup_step, 1)
                dve.wait_ge(setup_step, step[0])

            dve.wait_ge(setup_loads, 16 * N_SETUP)
            setup(dve.tensor_copy(pos_f[:, :], pos_i[:, :]))
            for t in range(NT):
                last = dve.tensor_scalar(ang[:, t, :], freq[:, :], pos_f[:, t:t + 1], None, ALU.mult)
            setup(last)
            setup(dve.tensor_scalar(turns[:, :, :], ang[:, :, :], float(1 / (2 * np.pi)), 12582912.0, ALU.mult, ALU.add))
            setup(dve.tensor_scalar(turns[:, :, :], turns[:, :, :], 12582912.0, None, ALU.subtract))
            for part in TWO_PI_PARTS:
                setup(dve.scalar_tensor_tensor(ang[:, :, :], turns[:, :, :], -part, ang[:, :, :], ALU.mult, ALU.add))
            setup(dve.tensor_scalar(ang[:, :, :], ang[:, :, :], 3.1415925, -3.1415925, ALU.min, ALU.max))
            assert step[0] == ANGLE_LINKS
            dve.wait_ge(trig_done, 2)
            setup(dve.tensor_scalar(turns[:, :, :], absang[:, :, :], -1.0, float(np.pi / 2), ALU.mult, ALU.add))
            dve.wait_ge(trig_done, 3)
            with dve.Fori(0, DEPTH) as L:
                dve.tensor_copy(own[:, :, :], gains[:, bass.ds(L, 1), :]).then_inc(own_ready.sem, 1)
                dve.wait_ge(own_ready.sem, own_ready.at(L, 1))
                norm(L, 0, x)
                for s in range(2):
                    for k in range(2):
                        lo(L, s, k)
                norm_lo(L, 0, hT, 4)
                feed_forward(L, 0, 0)
                mixer(L)
                norm(L, 3, x)
                norm_lo(L, 3, hT, 4)
                feed_forward(L, 1, FFN2_0)
            assert links[0] == VLINKS, links


ANGLE_LINKS = 8
TWO_PI_PARTS = []
_rest = 2 * np.pi
for _bits in (9, 11, 24):
    _unit = 2.0 ** (np.floor(np.log2(abs(_rest))) - _bits + 1)
    _part = float(np.float32(np.round(_rest / _unit) * _unit))
    TWO_PI_PARTS.append(_part)
    _rest -= _part

_INS = ["x", "mem", "w_ffn1_in", "w_ffn1_out", "w_in", "w_mem_kv", "pool_mix", "w_branch", "w_out",
        "w_ffn2_in", "w_ffn2_out"]


def lay_out_gains(v):
    def columns(a):
        return a.reshape(DEPTH, -1, P).transpose(2, 0, 1)

    def rows(a):
        return np.broadcast_to(a[None], (P,) + a.shape)

    parts = [columns(v[n]) for n in ("norm_ffn1", "norm_mem", "norm_mix", "norm_ffn2", "pool_scale")]
    parts += [columns(np.concatenate([v[n], v[n]], axis=1)) for n in ("fox_q_gain", "fox_k_gain")]
    parts += [columns(v[n]) for n in ("mem_q_gain", "mem_k_gain")]
    parts += [rows(v[n]) for n in ("b_forget", "moba_q_gain", "moba_k_gain")]
    return np.concatenate(parts, axis=2)


def shape_constants():
    s, t = np.arange(P)[:, None], np.arange(SEQ)[None, :]
    mask = np.where((t >= P) & (t - P > s), NEG, 0.0)
    upto = (s <= t).astype(np.float64)
    bands = []
    for w in WINDOWS:
        for first, tt in ((0, t), (P, t[:, P:])):
            src = s + first
            inside = (src <= tt) & (src > tt - w)
            bands.append(inside / np.minimum(tt + 1, w) - (src == tt))
    const = np.concatenate([np.eye(P), mask, upto] + bands, axis=1).astype(np.float32)
    sel = np.repeat(np.eye(NH), P, axis=1).astype(np.float32)
    half = HD // 8
    freq = np.power(np.float32(500000.0), -np.arange(half, dtype=np.float32) * np.float32(2.0 / (2 * half))).astype(np.float32)
    return const, sel, np.broadcast_to(freq[None], (P, half))


def kernel(**inputs):
    import concourse.bacc as bacc
    from concourse.bass_utils import run_bass_kernel_spmd

    nc = bacc.Bacc("TRN2", target_bir_lowering=False, num_devices=1)
    arrays, args = {}, []

    def take(name, a):
        arrays[name] = np.ascontiguousarray(a)
        args.append(nc.dram_tensor(name, a.shape, mybir.dt.from_np(a.dtype), kind="ExternalInput").ap())

    inputs = {name: np.asarray(a) for name, a in inputs.items()}
    for name in _INS:
        take(f"in_{name}", inputs[name])
    take("gains_dram", lay_out_gains(inputs))
    take("positions_dram", inputs["positions"].reshape(NT, P).T)
    for name, a in zip(("const_dram", "sel_dram", "freq_dram"), shape_constants()):
        take(name, a)
    args.append(nc.dram_tensor("out_dram", (1, SEQ, DM), F32, kind="ExternalOutput").ap())
    build(nc, *args)
    r = run_bass_kernel_spmd(nc, [arrays], core_ids=[0])
    return r.results[0]["out_dram"]
```

```python
from contextlib import ExitStack

import numpy as np

import concourse.bass as bass
from concourse import mybir

F32 = mybir.dt.float32
F32R = mybir.dt.float32r
I32 = mybir.dt.int32
ACT = mybir.ActivationFunctionType
ALU = mybir.AluOpType
AX = mybir.AxisListType

P = 128
DEPTH, SEQ, DM, DFF = 2, 256, 1024, 2816
NT = SEQ // P
KC = DM // P
FC = DFF // P
HD, NH = 64, 8
MHD, MH = 128, 4
BW, BC = 512, 4
EPS = 1e-6
WINDOWS = (2, 4, 8, 16)
NEG = -1e30
IN_F = 6 * NH * HD
IN_POOL = IN_F + NH
IN_MEMQ = IN_POOL + BW
IN_GATE = IN_MEMQ + BW

RAW, SLOTS = 4, 4
LOADW, UNITW = 2048, 1024

FFN_STEPS = FC + FC // 2
TOP = 2
FFN1_0 = TOP
MIX0 = FFN1_0 + FFN_STEPS
MIX = []
TOP_MIX = [("mk", None, -1, 0), ("mk", None, -1, 1)]


def _blocks():
    b = 1

    def proj(kind, arg=None):
        nonlocal b
        MIX.append((kind, arg, b, 0))
        MIX.append((kind, arg, b, 1))
        b += 1

    for kind in ("mv", "qa", "ka", "va", "qc", "kc", "vc"):
        proj(kind)
    MIX.append(("f", None, None, 0))
    for kind in ("qm", "pu"):
        proj(kind)
    proj("gate", (1, 0))
    MIX.append(("gate", (1, 1), b, 0))
    MIX.append(("mixing", None, None, 0))
    MIX.append(("gate", (1, 1), b, 1))
    for dh in range(2):
        MIX.append(("y", (1, dh), b + 1 + dh, 0))
    b += 3
    for n in (0, 2, 3):
        for dh in range(2):
            proj("gate", (n, dh))
            MIX.append(("y", (n, dh), b, 0))
            b += 1
    for j in range(KC // 2):
        MIX.append(("out", j, None, 0))
    return b


N_BLOCKS = _blocks()
FFN2_0 = MIX0 + len(MIX)
STEPS = FFN2_0 + FFN_STEPS
UNITS = 2 * STEPS
assert STEPS % RAW == 0 and UNITS % SLOTS == 0

BLOCK_KIND = {}
for kind, arg, b, half in TOP_MIX + MIX:
    if b is not None:
        BLOCK_KIND[b] = kind
BY_ACT = ("mv", "va", "vc", "pu", "gate")


def taken_before(b):
    by_act = BLOCK_KIND[b] in BY_ACT
    return by_act, sum((kind in BY_ACT) == by_act for i, kind in BLOCK_KIND.items() if i <= b)


def _step_of(kind, arg=None, half=0):
    return MIX0 + next(i for i, s in enumerate(MIX) if s[0] == kind and s[1] == arg and s[3] == half)


TASKS = {}
for s, task in [
    (_step_of("mv"), ("norm", None)),
    (_step_of("va", None, 1), ("qkT", 0)),
    (_step_of("qc"), ("scores", 0)),
    (_step_of("kc"), ("probsT", 0)),
    (_step_of("kc", None, 1), ("values", 0)), (_step_of("kc", None, 1), ("scores", 1)),
    (_step_of("vc", None, 1), ("probsT", 1)),
    (_step_of("qm"), ("values", 1)), (_step_of("qm"), ("cumsum", None)),
    (_step_of("qm", None, 1), ("qkT", 1)),
    (_step_of("pu"), ("scores", 2)),
    (_step_of("gate", (1, 0)), ("probsT", 2)),
    (_step_of("gate", (1, 0), 1), ("values", 2)), (_step_of("gate", (1, 0), 1), ("pool", None)),
    (_step_of("gate", (1, 1), 1), ("scores", 3)),
    (_step_of("y", (1, 1)), ("probsT", 3)),
    (_step_of("gate", (0, 0)), ("values", 3)), (_step_of("gate", (0, 0)), ("oT", 0)),
    (_step_of("gate", (0, 0), 1), ("oT", 1)),
    (_step_of("y", (0, 0)), ("qkT", 2)),
    (_step_of("gate", (0, 1)), ("scores", 4)),
    (_step_of("y", (0, 1)), ("probsT", 4)),
    (_step_of("gate", (2, 0)), ("values", 4)), (_step_of("gate", (2, 0)), ("scores", 5)),
    (_step_of("y", (2, 0)), ("probsT", 5)),
    (_step_of("gate", (2, 1)), ("values", 5)),
    (_step_of("y", (2, 1)), ("oT", 2)),
    (_step_of("gate", (3, 1)), ("zT", 0)),
    (_step_of("out", 0), ("zT", 1)),
]:
    TASKS.setdefault(s, []).append(task)

SPLITS = ["pooled", "mixed", "o0", "o1", "o2", "z0", "z1"]
NORMED = ["mk", "qa", "ka", "qc", "kc", "qm"]


class Tally:

    def __init__(self, sem, per_layer, credit=0):
        self.sem, self.per_layer, self.credit = sem, per_layer, credit

    def at(self, layer, count):
        return layer * self.per_layer + (self.credit + count)


def build(nc, x_d, mem_d, w1i_d, w1o_d, win_d, wkv_d, pmix_d, wbr_d, wout_d, w2i_d, w2o_d,
          gains_d, pos_d, const_d, freq_d, out_d):
    ctx = ExitStack()
    with ctx:
        def sb(name, shape, dt=F32, scope=ctx):
            return scope.enter_context(nc.sbuf_tensor(name, shape, dt))

        const = sb("const", [P, const_d.shape[1]])
        ident = const[:, 0:P]
        mask = const[:, P:P + SEQ]
        upto = const[:, 384:384 + SEQ]
        band = const[:, 640:].rearrange("p (g c) -> p g c", g=4)
        freq = sb("freq", [P, 8])
        NORM_AT, POOL_AT, HEAD_AT, FORGET_AT, MOBA_AT, N_GAINS = 0, 32, 36, 40, 48, 176
        MEMORY_AT = NORM_AT + 3 * KC
        gains = sb("gains", [P, DEPTH + 1, N_GAINS])
        own = sb("own", [P, 1, N_GAINS])
        next_gain = sb("next_gain", [P, 1, KC])
        pos_i = sb("pos_i", [P, NT], I32)
        pos_f = sb("pos_f", [P, NT])
        ang = sb("ang", [P, NT, 8])
        turns = sb("turns", [P, NT, 8])
        absang = sb("absang", [P, NT, 8])
        cosv = sb("cosv", [P, NT, 8])
        sinv = sb("sinv", [P, NT, 8])
        ss = sb("ss", [P, NT, 2])
        ms = sb("ms", [P, 16])
        rs = sb("rs", [P, 16])
        ra = sb("ra", [P, 16])
        rb = sb("rb", [P, 16])
        hss = sb("hss", [P, 16])
        mx = sb("mx", [P, 8])
        nmx = sb("nmx", [P, 8])
        den = sb("den", [P, 8])
        rden = sb("rden", [P, 8])
        fz = sb("fz", [P, NT, NH])
        fna = sb("fna", [P, NT, NH])
        fe = sb("fe", [P, NT, NH])
        fl = sb("fl", [P, NT, NH])
        lf = sb("lf", [P, NT, NH])
        negc = sb("negc", [NH, SEQ])
        x = sb("x", [P, NT, DM])
        memN = sb("memN", [P, KC, SEQ])
        hT = [sb("hT_hi", [P, KC, SEQ], F32R), sb("hT_lo", [P, KC, SEQ], F32R)]
        raw = sb("raw", [P, RAW, LOADW])
        ring = [sb("ring_hi", [P, SLOTS, UNITW], F32R), sb("ring_lo", [P, SLOTS, UNITW], F32R)]
        with ExitStack() as ffn:
            act_hi = sb("act_hi", [P, FC, SEQ], F32R, ffn)
            act_lo = sb("act_lo", [P, FC, SEQ], F32R, ffn)
            silu = sb("silu", [P, 2, SEQ], F32, ffn)
            prod = sb("prod", [P, 2, SEQ], F32, ffn)
        qk = sb("qk", [P, 2, NT, BW])
        mem_n = qk[:, :, :, :].rearrange("p a t c -> p a (t c)")
        vals = sb("vals", [P, 3, NT, BW])
        qkT_buf = sb("qkT", [P, 2, 2, BC, SEQ])
        with ExitStack() as pooling:
            pooledT = [sb("pooledT_hi", [P, BC, SEQ], F32R, pooling), sb("pooledT_lo", [P, BC, SEQ], F32R, pooling)]
        probs = sb("probs", [P, 1536])
        pT = sb("pT", [P, 3, 512])
        kmem = sb("kmem", [P, NT, BW])
        gate = sb("gate", [P, 2, NT, BW])
        xn = gate[:, :, :, :].rearrange("p a t c -> p a (t c)")
        with ExitStack() as early:
            memx = sb("memx", [P, NT, DM], F32, early)
        brT = [[sb(f"brT{i}_{part}", [P, BC, SEQ], F32R) for part in ("hi", "lo")] for i in range(2)]
        with ExitStack() as early:
            memhT = [sb("memhT_hi", [P, KC, SEQ], F32R, early), sb("memhT_lo", [P, KC, SEQ], F32R, early)]
        o = sb("o", [P, 3, NT, BW])
        z = sb("z", [P, NT, DM])
        rot = z[:, 1, 0:4 * NT * NH * 8].rearrange("p (i t h d) -> p i t h d", i=4, t=NT, h=NH)

        bank = [ctx.enter_context(nc.psum_tensor(f"bank{i}", [P, 512], F32)) for i in range(8)]

        def tally(name, per_layer, credit=0):
            return Tally(ctx.enter_context(nc.semaphore(name)), per_layer, credit)

        setup_loads = ctx.enter_context(nc.semaphore("setup_loads"))
        x_loaded = ctx.enter_context(nc.semaphore("x_loaded"))
        setup_step = ctx.enter_context(nc.semaphore("setup_step"))
        stored = ctx.enter_context(nc.semaphore("stored"))
        raw_ready = [tally(f"raw_ready{i}", 16 * STEPS // RAW) for i in range(RAW)]
        hi_done = tally("hi_done", UNITS)
        lo_done = tally("lo_done", UNITS, 2 * RAW)
        used = tally("used", UNITS, SLOTS)
        mem_loaded = [ctx.enter_context(nc.semaphore(f"mem_loaded{t}")) for t in range(NT)]
        ident_loaded = ctx.enter_context(nc.semaphore("ident_loaded"))
        gains_loaded = ctx.enter_context(nc.semaphore("gains_loaded"))
        mem_squares = ctx.enter_context(nc.semaphore("mem_squares"))
        mem_rows = ctx.enter_context(nc.semaphore("mem_rows"))
        mem_turned = ctx.enter_context(nc.semaphore("mem_turned"))
        memN_act = ctx.enter_context(nc.semaphore("memN_act"))
        memN_dve = ctx.enter_context(nc.semaphore("memN_dve"))
        next_gain_ready = tally("next_gain_ready", 1)
        memh_hi = tally("memh_hi", 4)
        memh_ready = tally("memh_ready", 4)
        ang_ready = tally("ang_ready", 2)
        trig_done = tally("trig_done", 2)
        own_ready = tally("own_ready", 1)
        x_ready = tally("x_ready", 12, 1)
        sumsq = tally("sumsq", 12)
        xn_ready = tally("xn_ready", 12)
        xnT = tally("xnT", 12)
        h_hi = tally("h_hi", 12)
        h_ready = tally("h_ready", 12)
        silu_done = tally("silu_done", 2 * FC)
        prod_done = tally("prod_done", 2 * FC, 4)
        act_hi_done = tally("act_hi_done", 2 * FC)
        act_ready = tally("act_ready", 2 * FC)
        rows0_ready = tally("rows0_ready", 3)
        taken_act = tally("taken_act", sum(k in BY_ACT for k in BLOCK_KIND.values()))
        taken_dve = tally("taken_dve", sum(k not in BY_ACT for k in BLOCK_KIND.values()))
        squares = tally("squares", 2 * len(NORMED))
        qkT_ps = tally("qkT_ps", 3)
        qT_ready = tally("qT_ready", 3)
        kT_ready = tally("kT_ready", 3)
        scores_ready = tally("scores_ready", 6)
        max_ready = tally("max_ready", 6)
        probs_ready = tally("probs_ready", 6)
        pT_ps = tally("pT_ps", 6)
        pT_act = tally("pT_act", 6)
        pT_dve = tally("pT_dve", 6)
        pv_ready = tally("pv_ready", 6)
        o_ready = tally("o_ready", 6)
        fna_ready = tally("fna_ready", 1)
        fe_done = tally("fe_done", 1)
        fl_done = tally("fl_done", 1)
        lf_ready = tally("lf_ready", 1)
        c_ready = tally("c_ready", 1)
        negc_ready = tally("negc_ready", 1)
        split_ps = tally("split_ps", 2 * len(SPLITS) - 2)
        split_hi = tally("split_hi", 2 * len(SPLITS))
        split_lo = tally("split_lo", 2 * len(SPLITS))
        VLINKS = 162
        vlink = tally("vlink", VLINKS)

        def unit_words(step, k):
            local = step - (FFN1_0 if step < MIX0 else FFN2_0)
            if (step < MIX0 or step >= FFN2_0) and 0 <= local < FC:
                i, half = divmod(local, 2)
                m = step - local + 2 * i + k
                view = raw[:, m % RAW, :].rearrange("p (k c) -> p k c", k=KC)[:, :, half * P:(half + 1) * P]
                return m, view, UNITW
            n = UNITW
            if MIX0 <= step < FFN2_0:
                n = {"f": KC * NH // 2, "mixing": BW // 2}.get(MIX[step - MIX0][0], UNITW)
            return step, raw[:, step % RAW, k * n:(k + 1) * n], n

        def unit_slot(part, step, k):
            return ring[part][:, (2 * step + k) % SLOTS, :]

        def unit_out(part, step, k):
            _, view, n = unit_words(step, k)
            slot = unit_slot(part, step, k)[:, 0:n]
            return slot.rearrange("p (k c) -> p k c", k=KC) if len(view.shape) == 3 else slot

        def steps_in_loop(engine, first, body):
            with engine.Fori(0, FC // 4) as j:
                for c in range(4):
                    body(j, c)
            for c in range(FC // 4 * 4, FC):
                body(None, c)

        N_SETUP = 3
        block = ctx.enter_context(nc.Block())

        @block.sync
        def _(sp):
            for t in range(NT):
                sp.dma_start(memx[:, t, :], mem_d[0, t * P:(t + 1) * P, :]).then_inc(mem_loaded[t], 16)
            sp.dma_start(x[:, :, :], x_d[0].rearrange("(t p) d -> p t d", p=P)).then_inc(x_loaded, 16)

            def load(L, m, dst, src, j=None, gates_at=None):
                late = 1 if gates_at is not None and (m - RAW - gates_at) % 2 == 0 and m - RAW >= gates_at else 0
                need = lo_done.at(L, 2 * (m - RAW) + 2 + late)
                sp.wait_ge(lo_done.sem, need if j is None else need + 8 * j)
                sp.dma_start(dst, src).then_inc(raw_ready[m % RAW].sem, 16)

            def ffn_loads(L, base, w_in, w_out):
                def columns(j, i):
                    for k in range(2):
                        m = base + 2 * i + k
                        dst = raw[:, m % RAW, :].rearrange("p (k c) -> p k c", k=KC)
                        at = k * DFF + 2 * P * i
                        cols = slice(at, at + 2 * P) if j is None else bass.ds(j * (4 * P) + at, 2 * P)
                        src = w_in[bass.ds(L, 1), :, cols].rearrange("a (k p) c -> p (a k) c", p=P)
                        load(L, m, dst, src, j, base)
                columns(None, 0)
                columns(None, 1)
                with sp.Fori(0, FC // 4 - 1) as j:
                    columns(j, 2)
                    columns(j, 3)
                for i in range(FC // 4 * 2, FC // 2):
                    columns(None, i)
                for r in range(FC // 2):
                    m = base + FC + r
                    src = w_out[bass.ds(L, 1), 2 * P * r:2 * P * (r + 1), :].rearrange("a (h p) c -> p (a h) c", p=P)
                    load(L, m, raw[:, m % RAW, :].rearrange("p (h c) -> p h c", h=2), src, None, base if r < RAW else None)

            with sp.Fori(0, DEPTH) as L:
                for i, (kind, arg, b, half) in enumerate(TOP_MIX + MIX):
                    if i == TOP:
                        ffn_loads(L, FFN1_0, w1i_d, w1o_d)
                    m = i if i < TOP else MIX0 + i - TOP
                    dst = raw[:, m % RAW, :]
                    rows = slice(half * BW, (half + 1) * BW)
                    if kind in ("mk", "mv"):
                        at = {"mk": 0, "mv": BW}[kind]
                        src = wkv_d[bass.ds(L, 1), rows, at:at + BW].rearrange("a (k p) c -> p (a k) c", p=P)
                        dst = dst.rearrange("p (k c) -> p k c", k=4)
                    elif kind == "f":
                        src = win_d[bass.ds(L, 1), :, IN_F:IN_F + NH].rearrange("a (k p) c -> p (a k) c", p=P)
                        dst = dst[:, 0:KC * NH].rearrange("p (k c) -> p k c", k=KC)
                    elif kind == "mixing":
                        src = pmix_d[bass.ds(L, 1)].rearrange("a g p e -> p (a g) e")
                        dst = dst[:, 0:BW].rearrange("p (g e) -> p g e", g=4)
                    elif kind == "y":
                        n, dh = arg
                        src = wbr_d.rearrange("l n (k p) c -> p (l n k) c", p=P)[:, bass.ds(L * (4 * BC) + n * BC, BC), dh * BW:(dh + 1) * BW]
                        dst = dst.rearrange("p (k c) -> p k c", k=BC)
                    elif kind == "out":
                        src = wout_d[bass.ds(L, 1), 2 * P * arg:2 * P * (arg + 1), :].rearrange("a (h p) c -> p (a h) c", p=P)
                        dst = dst.rearrange("p (h c) -> p h c", h=2)
                    else:
                        at = {"qa": 0, "ka": BW, "va": 2 * BW, "qc": 3 * BW, "kc": 4 * BW, "vc": 5 * BW,
                              "pu": IN_POOL, "qm": IN_MEMQ}.get(kind)
                        if kind == "gate":
                            at = IN_GATE + arg[0] * DM + arg[1] * BW
                        src = win_d[bass.ds(L, 1), rows, at:at + BW].rearrange("a (k p) c -> p (a k) c", p=P)
                        dst = dst.rearrange("p (k c) -> p k c", k=4)
                    load(L, m, dst, src)
                ffn_loads(L, FFN2_0, w2i_d, w2o_d)

            for t in range(NT):
                sp.wait_ge(x_ready.sem, x_ready.at(DEPTH - 1, 8 + 2 * t + 2))
                sp.dma_start(out_d[0, t * P:(t + 1) * P, :], x[:, t, :]).then_inc(stored, 16)
            sp.wait_ge(stored, 16 * NT)

        @block.tensor
        def _(pe):
            def three(out, act_parts, weight_parts, first, last, moving_weights):
                for n, (a, w) in enumerate(((0, 0), (0, 1), (1, 0))):
                    lhsT, rhs = (act_parts[a], weight_parts[w]) if moving_weights else (weight_parts[w], act_parts[a])
                    mm = pe.matmul(out, lhsT, rhs, start=first and n == 0, stop=last and n == 2)
                return mm

            def wait_unit(L, n, j=None):
                need = lo_done.at(L, n + 1)
                pe.wait_ge(lo_done.sem, need if j is None else need + 8 * j)

            def norm_transposes(L, index, banks, by_tile, tiles=(0, 1)):
                for t in tiles:
                    for kc in range(KC):
                        if t == 0 and not by_tile and kc == 0:
                            pe.wait_ge(xn_ready.sem, xn_ready.at(L, 4 * index + 4))
                        if by_tile and kc % 4 == 0:
                            pe.wait_ge(xn_ready.sem, xn_ready.at(L, 4 * index + 2 * t + kc // 4 + 1))
                        at = (kc % 2) * SEQ + t * P
                        mm = pe.transpose(bank[banks + kc // 2][:, at:at + P], xn[:, t, kc * P:(kc + 1) * P], ident)
                        if t == NT - 1 and kc % 2:
                            mm.then_inc(xnT.sem, 1)

            def hidden(L, base, first_chunk, norm):
                def body(j, c):
                    n = 2 * (base + c)
                    need = prod_done.at(L, first_chunk + c + 1 - 4)
                    pe.wait_ge(prod_done.sem, need if j is None else need + 4 * j)
                    if c == 2 and norm == 0:
                        pe.wait_ge(taken_dve.sem, taken_dve.at(L, 1))
                    for k in range(2):
                        wait_unit(L, n + k, j)
                        w = [unit_slot(part, base + c, k).rearrange("p (k c) -> p k c", k=KC) for part in range(2)]
                        for kc in range(KC):
                            if c == 0 and k == 0 and kc % 2 == 0:
                                pe.wait_ge(h_ready.sem, h_ready.at(L, 4 * norm + kc // 2 + 1))
                            mm = three(bank[c % 4][:, k * SEQ:(k + 1) * SEQ], [hT[p][:, kc, :] for p in range(2)],
                                       [w[p][:, kc, :] for p in range(2)], kc == 0, kc == KC - 1, False)
                        mm.then_inc(used.sem, 1)
                return body

            def rows(L, steps, acts, first, last, before_end=None):
                units = [(step, k) for step in steps for k in range(2)]

                def product(t, u):
                    step, k = units[u]
                    w = [unit_slot(part, step, k) for part in range(2)]
                    a = [acts[part][u][:, t * P:(t + 1) * P] for part in range(2)]
                    for (ap, wp) in ((0, 0), (0, 1), (1, 0)):
                        for half in range(2):
                            mm = pe.matmul(bank[4 + 2 * t + half][:, :], a[ap], w[wp][:, half * 512:(half + 1) * 512],
                                           start=first and u == 0 and (ap, wp) == (0, 0),
                                           stop=last and u == len(units) - 1 and ap == 1)
                    return mm

                if last:
                    for u, (step, k) in enumerate(units):
                        wait_unit(L, 2 * step + k)
                        mm = product(0, u)
                    mm.then_inc(rows0_ready.sem, 1)
                    for u in range(len(units)):
                        if before_end is not None and u == len(units) - 1:
                            before_end()
                        product(1, u).then_inc(used.sem, 1)
                else:
                    for u, (step, k) in enumerate(units):
                        wait_unit(L, 2 * step + k)
                        product(0, u)
                        product(1, u).then_inc(used.sem, 1)

            def feed_forward(L, which, base):
                steps_in_loop(pe, base, hidden(L, base, which * FC, 2 * which))
                for r in range(FC // 2 - 1):
                    last = r == FC // 2 - 2
                    n = 4 if last else 2
                    pe.wait_ge(act_ready.sem, act_ready.at(L, which * FC + 2 * r + n))
                    rows(L, [base + FC + r + i for i in range(n // 2)], [[a[:, 2 * r + k, :] for k in range(n)] for a in (act_hi, act_lo)],
                         r == 0, last)

            def heads(L, g):
                br = g // 2
                buf = qkT_buf[:, br % 2]
                odd = g % 2
                hs = [(2 * c + odd, c, HD * odd) for c in range(BC)] if br < 2 else [(h, h, 0) for h in (2 * odd, 2 * odd + 1)]
                return br, buf, hs

            def task(L, stage, arg):
                if stage == "norm":
                    norm_transposes(L, 1, 4, False)
                elif stage == "qkT":
                    pe.wait_ge(taken_dve.sem, taken_dve.at(L, {0: 3, 1: 5, 2: 6}[arg]))
                    if arg == 1:
                        pe.wait_ge(o_ready.sem, o_ready.at(L, 2))
                        pe.wait_ge(negc_ready.sem, negc_ready.at(L, 1))
                    if arg == 2:
                        pe.wait_ge(split_lo.sem, split_lo.at(L, 2 * SPLITS.index("o1") + 2))
                    for i in range(2):
                        src = qk[:, i] if arg < 2 or i == 0 else kmem
                        for c in range(BC):
                            for t in range(NT):
                                at = (c % 2) * SEQ + t * P
                                mm = pe.transpose(bank[4 + 2 * i + c // 2][:, at:at + P], src[:, t, c * P:(c + 1) * P], ident)
                    mm.then_inc(qkT_ps.sem, 1)
                elif stage == "scores":
                    br, buf, hs = heads(L, arg)
                    pe.wait_ge(qT_ready.sem, qT_ready.at(L, br + 1))
                    pe.wait_ge(kT_ready.sem, kT_ready.at(L, br + 1))
                    if arg:
                        pe.wait_ge(pT_act.sem, pT_act.at(L, arg))
                        pe.wait_ge(pT_dve.sem, pT_dve.at(L, arg))
                    if arg == 3:
                        pe.wait_ge(split_lo.sem, split_lo.at(L, 2 * SPLITS.index("mixed") + 2))
                    for i, (h, c, p) in enumerate(hs):
                        q, k = buf[p:p + (HD if br < 2 else MHD), 0, c, :], buf[p:p + (HD if br < 2 else MHD), 1, c, :]
                        if br < 2:
                            outs = [(bank[4][:, i * P:(i + 1) * P], 0, P),
                                    (bank[5 + i // 2][:, (i % 2) * SEQ:(i % 2 + 1) * SEQ], 1, SEQ)]
                        else:
                            outs = [(bank[4 + t][:, i * SEQ:(i + 1) * SEQ], t, SEQ) for t in range(NT)]
                        for out, t, keys in outs:
                            mm = pe.matmul(out, q[:, t * P:(t + 1) * P], k[:, 0:keys], start=True, stop=br != 1)
                            if br == 1:
                                mm = pe.matmul(out, ident[0:NH, h:h + 1].to_broadcast([NH, P]), negc[:, 0:keys], start=False, stop=True)
                    mm.then_inc(scores_ready.sem, 1)
                elif stage == "probsT":
                    br, buf, hs = heads(L, arg)
                    pe.wait_ge(probs_ready.sem, probs_ready.at(L, arg + 1))
                    for i in range(len(hs)):
                        if br < 2:
                            tiles = [(4, i, probs[:, i * P:(i + 1) * P])] + [
                                (5 + kt, i, probs[:, 512 + i * SEQ + kt * P:512 + i * SEQ + (kt + 1) * P]) for kt in range(2)]
                        else:
                            tiles = [(4 + t, 2 * i + kt, probs[:, t * 512 + i * SEQ + kt * P:t * 512 + i * SEQ + (kt + 1) * P])
                                     for t in range(NT) for kt in range(2)]
                        for b, at, src in tiles:
                            mm = pe.transpose(bank[b][:, at * P:(at + 1) * P], src, ident)
                    mm.then_inc(pT_ps.sem, 1)
                elif stage == "values":
                    br, buf, hs = heads(L, arg)
                    pe.wait_ge(pT_act.sem, pT_act.at(L, arg + 1))
                    pe.wait_ge(pT_dve.sem, pT_dve.at(L, arg + 1))
                    pe.wait_ge(taken_act.sem, taken_act.at(L, {0: 2, 1: 3, 2: 1}[br]))
                    if arg:
                        pe.wait_ge(o_ready.sem, o_ready.at(L, arg))
                    if arg == 1:
                        pe.wait_ge(fna_ready.sem, fna_ready.at(L, 1))
                    if arg == 4:
                        pe.wait_ge(kT_ready.sem, kT_ready.at(L, 3))
                    for i, (h, c, p) in enumerate(hs):
                        if br < 2:
                            for t in range(NT):
                                out = bank[7][:, t * SEQ + i * HD:t * SEQ + (i + 1) * HD]
                                for kt in range(t + 1):
                                    mm = pe.matmul(out, pT[:, t + kt, i * P:(i + 1) * P], vals[:, br, kt, h * HD:(h + 1) * HD],
                                                   start=kt == 0, stop=kt == t)
                        else:
                            for t in range(NT):
                                out = bank[7][:, t * SEQ + i * MHD:t * SEQ + (i + 1) * MHD]
                                for kt in range(2):
                                    mm = pe.matmul(out, pT[:, t, (2 * i + kt) * P:(2 * i + kt + 1) * P],
                                                   vals[:, 2, kt, h * MHD:(h + 1) * MHD], start=kt == 0, stop=kt == 1)
                    mm.then_inc(pv_ready.sem, 1)
                elif stage == "cumsum":
                    pe.wait_ge(lf_ready.sem, lf_ready.at(L, 1))
                    pe.wait_ge(pT_act.sem, pT_act.at(L, 2))
                    pe.matmul(bank[4][0:NH, 0:SEQ], lf[:, 0, :], upto, start=True, stop=False)
                    pe.matmul(bank[4][0:NH, P:SEQ], lf[:, 1, :], upto[:, 0:P], start=False, stop=True).then_inc(c_ready.sem, 1)
                elif stage == "pool":
                    pe.wait_ge(taken_act.sem, taken_act.at(L, 4))
                    pe.wait_ge(pT_act.sem, pT_act.at(L, 3))
                    pe.wait_ge(pT_dve.sem, pT_dve.at(L, 3))
                    for g in range(4):
                        out = bank[4 + g // 2][:, (g % 2) * SEQ:(g % 2 + 1) * SEQ]
                        pe.matmul(out, qk[:, 1, 0, g * P:(g + 1) * P], band[:, g, 0:SEQ], start=True, stop=False)
                        mm = pe.matmul(out[:, P:SEQ], qk[:, 1, 1, g * P:(g + 1) * P], band[:, g, SEQ:SEQ + P],
                                       start=False, stop=True)
                        if g % 2:
                            mm.then_inc(split_ps.sem, 1)
                elif stage in ("oT", "zT"):
                    if stage == "oT":
                        pe.wait_ge(o_ready.sem, o_ready.at(L, 2 * arg + 2))
                        first = 6 if arg == 1 else 4
                        src = o[:, arg]
                        if arg == 0:
                            pe.wait_ge(pT_act.sem, pT_act.at(L, 4))
                            pe.wait_ge(pT_dve.sem, pT_dve.at(L, 4))
                        if arg == 2:
                            pe.wait_ge(pT_act.sem, pT_act.at(L, 6))
                            pe.wait_ge(pT_dve.sem, pT_dve.at(L, 6))
                    else:
                        pe.wait_ge(taken_dve.sem, taken_dve.at(L, 13 + arg))
                        first = 4 if arg == 0 else 0
                        src = z[:, :, arg * BW:(arg + 1) * BW]
                        if arg == 0:
                            pe.wait_ge(split_lo.sem, split_lo.at(L, 2 * SPLITS.index("o2") + 2))
                    for c in range(BC):
                        for t in range(NT):
                            at = (c % 2) * SEQ + t * P
                            mm = pe.transpose(bank[first + c // 2][:, at:at + P], src[:, t, c * P:(c + 1) * P], ident)
                        if c % 2:
                            mm.then_inc(split_ps.sem, 1)

            def dense(L, s, kind, arg, b, half):
                    if b is not None and b >= 3 and half == 0:
                        by_act, count = taken_before(b - 2)
                        sig = taken_act if by_act else taken_dve
                        pe.wait_ge(sig.sem, sig.at(L, count))
                    if kind == "y":
                        pe.wait_ge(split_lo.sem, split_lo.at(L, 2 * SPLITS.index({0: "o0", 1: "mixed", 2: "o1", 3: "o2"}[arg[0]]) + 2))
                        acts = brT[{1: 0, 0: 1, 2: 0, 3: 1}[arg[0]]]
                    elif kind in ("mk", "mv"):
                        acts = memhT
                    else:
                        acts = hT
                    if kind == "f":
                        pe.wait_ge(o_ready.sem, o_ready.at(L, 1))
                        for k in range(2):
                            wait_unit(L, 2 * s + k)
                        w = [[unit_slot(part, s, kc // 4)[:, (kc % 4) * NH:(kc % 4 + 1) * NH] for part in range(2)] for kc in range(KC)]
                        for t in range(NT):
                            for kc in range(KC):
                                mm = three(bank[7][:, t * NH:(t + 1) * NH], [acts[p][:, kc, t * P:(t + 1) * P] for p in range(2)],
                                           w[kc], kc == 0, kc == KC - 1, True)
                                if t == NT - 1 and kc == 3:
                                    mm.then_inc(used.sem, 1)
                        mm.then_inc(used.sem, 1)
                    elif kind == "mixing":
                        pe.wait_ge(split_lo.sem, split_lo.at(L, 2 * SPLITS.index("pooled") + 2))
                        pe.wait_ge(o_ready.sem, o_ready.at(L, 3))
                        for g in range(4):
                            if g % 2 == 0:
                                wait_unit(L, 2 * s + g // 2)
                            w = [unit_slot(part, s, g // 2)[:, (g % 2) * P:(g % 2 + 1) * P] for part in range(2)]
                            mm = three(bank[6 + g // 2][:, (g % 2) * SEQ:(g % 2 + 1) * SEQ],
                                       [pooledT[p][:, g, :] for p in range(2)], w, True, True, False)
                            if g % 2:
                                mm.then_inc(used.sem, 1)
                    elif kind == "out":
                        if arg % 2 == 0:
                            pe.wait_ge(split_lo.sem, split_lo.at(L, 2 * SPLITS.index("z0" if arg == 0 else "z1") + 2))
                        src, n = (brT[0], 2) if arg < 2 else (hT, 4)
                        if arg < 3:
                            rows(L, [s + i for i in range(n // 2)],
                                 [[src[part][:, 2 * (arg % 2) + k, :] for k in range(n)] for part in range(2)], arg == 0, arg == 2,
                                 (lambda: norm_transposes(L, 2, 0, True, (0,))) if arg == 2 else None)
                    else:
                        nk = BC if kind == "y" else KC
                        for k in range(2):
                            wait_unit(L, 2 * s + k)
                            w = [unit_slot(part, s, k).rearrange("p (k c) -> p k c", k=2) for part in range(2)]
                            for kk in range(2):
                                kc = 4 * half + 2 * k + kk
                                if kind == "mk" and kc % 2 == 0:
                                    pe.wait_ge(memh_ready.sem, memh_ready.at(L, kc // 2 + 1))
                                if kind == "qa" and kc % 2 == 0:
                                    pe.wait_ge(h_ready.sem, h_ready.at(L, 4 + kc // 2 + 1))
                                for t in range(NT):
                                    mm = three(bank[2 * (b % 2) + t][:, :], [acts[p][:, kc, t * P:(t + 1) * P] for p in range(2)],
                                               [w[p][:, kk, :] for p in range(2)], kc == 0, kc == nk - 1, True)
                            mm.then_inc(used.sem, 1)

            def mixer(L):
                for i, (kind, arg, b, half) in enumerate(MIX):
                    dense(L, MIX0 + i, kind, arg, b, half)
                    for stage, targ in TASKS.get(MIX0 + i, ()):
                        task(L, stage, targ)

            pe.sem_inc(used.sem, used.credit)
            pe.wait_ge(ident_loaded, 16)
            for t in range(NT):
                pe.wait_ge(mem_rows, t + 1)
                for kc in range(KC):
                    at = (kc % 2) * SEQ + t * P
                    mm = pe.transpose(bank[kc // 2][:, at:at + P], mem_n[:, t, kc * P:(kc + 1) * P], ident)
            mm.then_inc(mem_turned, 1)
            pe.wait_ge(memN_act, 1)
            pe.wait_ge(memN_dve, 1)
            pe.wait_ge(setup_loads, 16 * N_SETUP)
            with pe.Fori(0, DEPTH) as L:
                dense(L, 0, "mk", None, -1, 0)
                norm_transposes(L, 0, 4, True)
                dense(L, 1, "mk", None, -1, 1)
                feed_forward(L, 0, FFN1_0)
                mixer(L)
                norm_transposes(L, 2, 0, True, (1,))
                feed_forward(L, 1, FFN2_0)

        def split_target(name):
            return {"pooled": (pooledT, 4, 1.0), "o0": (brT[1], 4, 1.0), "o1": (brT[0], 6, 1.0), "o2": (brT[1], 4, 1.0),
                    "z0": (brT[0], 4, 0.5), "z1": (hT, 0, 0.5)}[name]

        PS_ORDER = [name for name in SPLITS if name != "mixed"]
        HEAD_DST = {"mk": (kmem, MH), "qa": (qk[:, 0], NH), "ka": (qk[:, 1], NH), "qc": (qk[:, 0], NH),
                    "kc": (qk[:, 1], NH), "qm": (qk[:, 0], MH)}
        GATES = [arg for kind, arg, _, _ in MIX if kind == "y"]

        def banks_of(s):
            b = TOP_MIX[s][2] if s < TOP else MIX[s - MIX0][2]
            return [bank[2 * (b % 2) + t] for t in range(NT)]

        def gain(at):
            return own[:, 0, at:at + 1]

        @block.scalar
        def _(act):
            def hi(L, step, k, j=None):
                n = 2 * step + k
                m, view, _ = unit_words(step, k)
                arrived, free = raw_ready[m % RAW].at(L, 16 * (m // RAW + 1)), used.at(L, n + 1 - SLOTS)
                act.wait_ge(raw_ready[m % RAW].sem, arrived if j is None else arrived + 16 * j)
                act.wait_ge(used.sem, free if j is None else free + 8 * j)
                act.activation(unit_out(0, step, k), view, ACT.Copy).then_inc(hi_done.sem, 1)

            def norm(L, index, t, ready):
                for half in range(2):
                    if L is not None:
                        act.wait_ge(x_ready.sem, x_ready.at(L, ready if index == 0 else ready + 2 * t + half + 1))
                    at = slice(half * 512, (half + 1) * 512)
                    act.activation(xn[:, t, at], x[:, t, at], ACT.Square, accum_out=ss[:, t, half:half + 1]).then_inc(sumsq.sem, 1)

            def norm_hi(L, index, banks):
                if index == 0:
                    act.wait_ge(own_ready.sem, own_ready.at(L, 1))
                for b in range(4):
                    act.wait_ge(xnT.sem, xnT.at(L, 4 * index + b + 1))
                    for kc in (2 * b, 2 * b + 1):
                        last = act.activation(hT[0][:, kc, :], bank[banks + b][:, (kc % 2) * SEQ:(kc % 2 + 1) * SEQ], ACT.Copy,
                                              scale=gain(NORM_AT + index * KC + kc))
                    last.then_inc(h_hi.sem, 1)

            def memory_hi(L, count):
                act.wait_ge(next_gain_ready.sem, next_gain_ready.at(L, count))
                for kc in range(KC):
                    last = act.activation(memhT[0][:, kc, :], memN[:, kc, :], ACT.Copy, scale=next_gain[:, 0, kc:kc + 1])
                    if kc % 2:
                        last.then_inc(memh_hi.sem, 1)

            def hidden(L, base, first_chunk):
                def body(j, c):
                    s = base + c
                    def plus(value, per_turn):
                        return value if j is None else value + per_turn * j
                    act.wait_ge(used.sem, plus(used.at(L, 2 * s + 2), 8))
                    act.activation(silu[:, c % 2, :], bank[c % 4][:, 0:SEQ], ACT.Silu).then_inc(silu_done.sem, 1)
                    hi(L, s + 2, 0, j)
                    hi(L, s + 2, 1, j)
                    act.wait_ge(prod_done.sem, plus(prod_done.at(L, first_chunk + c + 1), 4))
                    dst = act_hi[:, c:c + 1, :] if j is None else act_hi[:, bass.ds(4 * j + c, 1), :]
                    act.activation(dst, prod[:, c % 2:c % 2 + 1, :], ACT.Copy).then_inc(act_hi_done.sem, 1)
                return body

            def ahead(L, s):
                if s + 2 < STEPS:
                    hi(L, s + 2, 0)
                    hi(L, s + 2, 1)

            def boundary(L, index, s, ready):
                norm(L, index, 0, ready)
                hi(L, s + 2, 0)
                hi(L, s + 2, 1)
                hi(L, s + 3, 0)
                norm(L, index, 1, ready)
                hi(L, s + 3, 1)

            def feed_forward(L, which, base):
                steps_in_loop(act, base, hidden(L, base, which * FC))
                for r in range(FC // 2 - 2):
                    ahead(L, base + FC + r)
                    if which == 0 and r == 2:
                        act.wait_ge(ang_ready.sem, ang_ready.at(L, 1))
                        act.activation(sinv[:, :, :], ang[:, :, :], ACT.Sin)
                        act.activation(absang[:, :, :], ang[:, :, :], ACT.Abs).then_inc(trig_done.sem, 1)
                        act.wait_ge(ang_ready.sem, ang_ready.at(L, 2))
                        act.activation(cosv[:, :, :], turns[:, :, :], ACT.Sin).then_inc(trig_done.sem, 1)
                    if which == 1 and r == 2:
                        memory_hi(L, 2)
                if which == 0:
                    boundary(L, 1, base + FFN_STEPS - 2, 0)
                else:
                    norm(L, 3, 0, 8)

            def split(L, name):
                dst, first, factor = split_target(name)
                at = 2 * PS_ORDER.index(name)
                for b in range(2):
                    act.wait_ge(split_ps.sem, split_ps.at(L, at + b + 1))
                    act.activation(dst[0][:, 2 * b:2 * b + 2, :], bank[first + b][:, :].rearrange("p (c t) -> p c t", c=2), ACT.Copy,
                                   scale=factor).then_inc(split_hi.sem, 1)

            def task(L, stage, arg):
                if stage == "norm":
                    norm_hi(L, 1, 4)
                elif stage == "qkT":
                    act.wait_ge(qkT_ps.sem, qkT_ps.at(L, arg + 1))
                    for b in range(2):
                        last = act.activation(qkT_buf[:, arg % 2, 0, 2 * b:2 * b + 2, :],
                                              bank[4 + b][:, :].rearrange("p (c t) -> p c t", c=2), ACT.Copy,
                                              scale=1.0 if arg == 0 else gain(HEAD_AT + 2 * (arg - 1)))
                    last.then_inc(qT_ready.sem, 1)
                elif stage == "scores":
                    act.wait_ge(max_ready.sem, max_ready.at(L, arg + 1))
                    if arg < 4:
                        for i in range(4):
                            for t in range(NT):
                                p = probs[:, i * P:(i + 1) * P] if t == 0 else probs[:, 512 + i * SEQ:512 + (i + 1) * SEQ]
                                last = act.activation(p, p, ACT.Exp, bias=nmx[:, 4 * t + i:4 * t + i + 1], scale=HD ** -0.5,
                                                      accum_out=den[:, 4 * t + i:4 * t + i + 1])
                    else:
                        act.wait_ge(pT_ps.sem, pT_ps.at(L, arg))
                        for i in range(2):
                            for t in range(NT):
                                last = act.activation(probs[:, t * 512 + i * SEQ:t * 512 + (i + 1) * SEQ],
                                                      bank[4 + t][:, i * SEQ:(i + 1) * SEQ], ACT.Exp,
                                                      bias=nmx[:, 2 * t + i:2 * t + i + 1], scale=MHD ** -0.5,
                                                      accum_out=den[:, 2 * t + i:2 * t + i + 1])
                    last.then_inc(probs_ready.sem, 1)
                elif stage == "probsT":
                    act.wait_ge(pT_ps.sem, pT_ps.at(L, arg + 1))
                    act.activation(pT[:, 0, :], bank[4][:, :], ACT.Copy).then_inc(pT_act.sem, 1)
                elif stage == "pool":
                    split(L, "pooled")
                elif stage == "oT":
                    split(L, f"o{arg}")
                elif stage == "zT":
                    split(L, f"z{arg}")

            def serve(L, s, kind, arg, half):
                if kind == "f":
                    act.wait_ge(fna_ready.sem, fna_ready.at(L, 1))
                    act.activation(fe[:, :, :], fna[:, :, :], ACT.Exp).then_inc(fe_done.sem, 1)
                    act.wait_ge(fe_done.sem, fe_done.at(L, 1))
                    act.activation(fl[:, :, :], fe[:, :, :], ACT.Ln, bias=1.0).then_inc(fl_done.sem, 1)
                elif kind == "mixing":
                    for b in range(2):
                        act.wait_ge(used.sem, used.at(L, 2 * s + b + 1))
                        for g in (2 * b, 2 * b + 1):
                            last = act.activation(brT[0][0][:, g, :], bank[6 + b][:, (g % 2) * SEQ:(g % 2 + 1) * SEQ], ACT.Copy,
                                                  scale=gain(POOL_AT + g))
                        last.then_inc(split_hi.sem, 1)
                elif half == 1 and kind != "out":
                    act.wait_ge(used.sem, used.at(L, 2 * s + 2))
                    banks = banks_of(s)
                    if kind == "gate":
                        idx = GATES.index(arg)
                        if idx >= 2:
                            act.wait_ge(taken_dve.sem, taken_dve.at(L, 6 + idx - 1))
                        for t in range(NT):
                            last = act.activation(gate[:, idx % 2, t, :], banks[t][:, :], ACT.Tanh, scale=0.5)
                        last.then_inc(taken_act.sem, 1)
                    elif kind in BY_ACT:
                        if kind == "pu":
                            act.wait_ge(qkT_ps.sem, qkT_ps.at(L, 2))
                        dst = qk[:, 1] if kind == "pu" else vals[:, {"va": 0, "vc": 1, "mv": 2}[kind]]
                        for t in range(NT):
                            last = act.activation(dst[:, t, :], banks[t][:, :], ACT.Copy)
                        last.then_inc(taken_act.sem, 1)
                    else:
                        if kind in ("qc", "kc", "qm"):
                            act.wait_ge(qkT_ps.sem, qkT_ps.at(L, 2 if kind == "qm" else 1))
                        dst, heads = HEAD_DST[kind]
                        for t in range(NT):
                            act.activation(dst[:, t, :], banks[t][:, :], ACT.Square).then_inc(squares.sem, 1)

            def mixer(L):
                for i, (kind, arg, b, half) in enumerate(MIX):
                    if (kind, arg) == ("out", 2):
                        break
                    ahead(L, MIX0 + i)
                    serve(L, MIX0 + i, kind, arg, half)
                    for stage, targ in TASKS.get(MIX0 + i, ()):
                        task(L, stage, targ)
                boundary(L, 2, FFN2_0 - 2, 4)

            act.dma_start(ident, const_d[:, 0:P]).then_inc(ident_loaded, 16)
            act.dma_start(gains[:, :, :], gains_d).then_inc(gains_loaded, 16)
            act.dma_start(const[:, P:], const_d[:, P:]).then_inc(setup_loads, 16)
            act.dma_start(freq[:, :], freq_d).then_inc(setup_loads, 16)
            act.dma_start(pos_i[:, :], pos_d).then_inc(setup_loads, 16)
            for t in range(NT):
                act.wait_ge(mem_loaded[t], 16)
                act.activation(mem_n[:, t, :], memx[:, t, :], ACT.Square, accum_out=ss[:, t, 0:1]).then_inc(mem_squares, 1)
            act.wait_ge(mem_turned, 1)
            for b in range(2):
                last = act.activation(memN[:, 2 * b:2 * b + 2, :], bank[b][:, :].rearrange("p (c t) -> p c t", c=2), ACT.Copy)
            last.then_inc(memN_act, 1)
            act.wait_ge(memN_act, 1)
            act.wait_ge(memN_dve, 1)
            memory_hi(0, 1)
            act.wait_ge(x_loaded, 16)
            norm(None, 0, 0, 0)
            with act.Fori(0, DEPTH) as L:
                for k in range(2):
                    hi(L, 0, k)
                norm(L, 0, 1, 0)
                for k in range(2):
                    hi(L, 1, k)
                norm_hi(L, 0, 4)
                ahead(L, 0)
                ahead(L, 1)
                serve(L, 1, "mk", None, 1)
                feed_forward(L, 0, FFN1_0)
                mixer(L)
                norm_hi(L, 2, 0)
                feed_forward(L, 1, FFN2_0)

        @block.vector
        def _(dve):
            links, setups = [0], [0]

            def link(L, ins):
                if L is None:
                    setups[0] += 1
                    ins.then_inc(setup_step, 1)
                    dve.wait_ge(setup_step, setups[0])
                else:
                    links[0] += 1
                    ins.then_inc(vlink.sem, 1)
                    dve.wait_ge(vlink.sem, vlink.at(L, links[0]))

            def lo(L, step, k, j=None):
                done = hi_done.at(L, 2 * step + k + 1)
                dve.wait_ge(hi_done.sem, done if j is None else done + 8 * j)
                _, view, _ = unit_words(step, k)
                dve.tensor_tensor(unit_out(1, step, k), view, unit_out(0, step, k).bitcast(F32), ALU.subtract)\
                    .then_inc(lo_done.sem, 1)

            def newton(L, r, m, n):
                link(L, dve.tensor_scalar(r.bitcast(I32), m.bitcast(I32), -0.5, 1597463007.0, ALU.mult, ALU.add))
                for _ in range(3):
                    link(L, dve.scalar_tensor_tensor(ra[:, 0:n], r, -0.5, r, ALU.mult, ALU.mult))
                    link(L, dve.tensor_tensor(rb[:, 0:n], ra[:, 0:n], m, ALU.mult))
                    link(L, dve.scalar_tensor_tensor(r, rb[:, 0:n], 1.5, r, ALU.add, ALU.mult))

            def newton_row(L):
                link(L, dve.tensor_scalar(rs[:, 0:1].bitcast(I32), ms[:, 0:1].bitcast(I32), -0.5, 1597463007.0 - 2.0 ** 22,
                                          ALU.mult, ALU.add))
                for _ in range(3):
                    link(L, dve.scalar_tensor_tensor(ra[:, 0:1], rs[:, 0:1], ms[:, 0:1], rs[:, 0:1], ALU.mult, ALU.mult))
                    link(L, dve.scalar_tensor_tensor(rs[:, 0:1], ra[:, 0:1], -1.5, rs[:, 0:1], ALU.add, ALU.mult))

            def norm(L, index, t):
                layer = 0 if L is None else L
                dve.wait_ge(sumsq.sem, sumsq.at(layer, 4 * index + 2 * t + 1))
                link(L, dve.tensor_scalar(ms[:, 0:1], ss[:, t, 0:1], 0.5 / DM, 0.5 * EPS, ALU.mult, ALU.add))
                dve.wait_ge(sumsq.sem, sumsq.at(layer, 4 * index + 2 * t + 2))
                link(L, dve.scalar_tensor_tensor(ms[:, 0:1], ss[:, t, 1:2], 0.5 / DM, ms[:, 0:1], ALU.mult, ALU.add))
                newton_row(L)
                for half in range(2):
                    at = slice(half * 512, (half + 1) * 512)
                    dve.tensor_scalar(xn[:, t, at], x[:, t, at], rs[:, 0:1], -1.0, ALU.mult, ALU.mult).then_inc(xn_ready.sem, 1)

            def norm_lo(L, index, banks):
                for b in range(4):
                    dve.wait_ge(h_hi.sem, h_hi.at(L, 4 * index + b + 1))
                    for kc in (2 * b, 2 * b + 1):
                        last = dve.scalar_tensor_tensor(hT[1][:, kc, :], bank[banks + b][:, (kc % 2) * SEQ:(kc % 2 + 1) * SEQ],
                                                        gain(NORM_AT + index * KC + kc), hT[0][:, kc, :].bitcast(F32),
                                                        ALU.mult, ALU.subtract)
                    last.then_inc(h_ready.sem, 1)

            def memory_lo(L, count):
                for kc in range(KC):
                    if kc % 2 == 0:
                        dve.wait_ge(memh_hi.sem, memh_hi.at(L, 4 * (count - 1) + kc // 2 + 1))
                    last = dve.scalar_tensor_tensor(memhT[1][:, kc, :], memN[:, kc, :], next_gain[:, 0, kc:kc + 1],
                                                    memhT[0][:, kc, :].bitcast(F32), ALU.mult, ALU.subtract)
                    if kc % 2:
                        last.then_inc(memh_ready.sem, 1)

            def hidden(L, base, first_chunk):
                def body(j, c):
                    s = base + c
                    def plus(value, per_turn):
                        return value if j is None else value + per_turn * j
                    lo(L, s + 2, 0, j)
                    dve.wait_ge(silu_done.sem, plus(silu_done.at(L, first_chunk + c + 1), 4))
                    dve.tensor_tensor(prod[:, c % 2, :], silu[:, c % 2, :], bank[c % 4][:, SEQ:2 * SEQ], ALU.mult)\
                        .then_inc(prod_done.sem, 1)
                    lo(L, s + 2, 1, j)
                    dve.wait_ge(act_hi_done.sem, plus(act_hi_done.at(L, first_chunk + c + 1), 4))
                    at = slice(c, c + 1) if j is None else bass.ds(4 * j + c, 1)
                    dve.tensor_tensor(act_lo[:, at, :], prod[:, c % 2:c % 2 + 1, :], act_hi[:, at, :].bitcast(F32), ALU.subtract)\
                        .then_inc(act_ready.sem, 1)
                return body

            def ahead(L, s):
                if s + 2 < STEPS:
                    lo(L, s + 2, 0)
                    lo(L, s + 2, 1)

            def add_rows(L, phase, t, last_step, factor):
                if t == 0:
                    dve.wait_ge(rows0_ready.sem, rows0_ready.at(L, phase + 1))
                else:
                    dve.wait_ge(used.sem, used.at(L, 2 * last_step + 2))
                for half in range(2):
                    xs = x[:, t, half * 512:(half + 1) * 512]
                    dve.scalar_tensor_tensor(xs, bank[4 + 2 * t + half][:, :], factor, xs, ALU.mult, ALU.add)\
                        .then_inc(x_ready.sem, 1)

            def boundary(L, phase, index, s, factor):
                add_rows(L, phase, 0, s + 1, factor)
                norm(L, index, 0)
                lo(L, s + 2, 0)
                lo(L, s + 2, 1)
                add_rows(L, phase, 1, s + 1, factor)
                lo(L, s + 3, 0)
                norm(L, index, 1)
                lo(L, s + 3, 1)

            def angles(L):
                link(L, dve.tensor_copy(pos_f[:, :], pos_i[:, :]))
                for t in range(NT):
                    last = dve.tensor_scalar(ang[:, t, :], freq[:, :], pos_f[:, t:t + 1], None, ALU.mult)
                link(L, last)
                link(L, dve.tensor_scalar(turns[:, :, :], ang[:, :, :], float(1 / (2 * np.pi)), 12582912.0, ALU.mult, ALU.add))
                link(L, dve.tensor_scalar(turns[:, :, :], turns[:, :, :], 12582912.0, None, ALU.subtract))
                for part in TWO_PI_PARTS:
                    link(L, dve.scalar_tensor_tensor(ang[:, :, :], turns[:, :, :], -part, ang[:, :, :], ALU.mult, ALU.add))
                dve.tensor_scalar(ang[:, :, :], ang[:, :, :], 3.1415925, -3.1415925, ALU.min, ALU.max).then_inc(ang_ready.sem, 1)
                dve.wait_ge(trig_done.sem, trig_done.at(L, 1))
                dve.tensor_scalar(turns[:, :, :], absang[:, :, :], -1.0, float(np.pi / 2), ALU.mult, ALU.add).then_inc(ang_ready.sem, 1)

            def feed_forward(L, which, base):
                steps_in_loop(dve, base, hidden(L, base, which * FC))
                last_two = base + FFN_STEPS - 2
                for r in range(FC // 2 - 2):
                    ahead(L, base + FC + r)
                    if which == 0 and r == 2:
                        angles(L)
                    if which == 1 and r == 2:
                        dve.tensor_copy(next_gain[:, :, :], gains[:, bass.ds(L + 1, 1), MEMORY_AT:MEMORY_AT + KC])\
                            .then_inc(next_gain_ready.sem, 1)
                        memory_lo(L, 2)
                if which == 0:
                    boundary(L, 0, 1, last_two, 0.5)
                else:
                    add_rows(L, 2, 0, last_two + 1, 0.5)
                    norm(L, 3, 0)
                    add_rows(L, 2, 1, last_two + 1, 0.5)

            def split(L, name):
                dst, first, factor = split_target(name)
                at = 2 * SPLITS.index(name)
                for b in range(2):
                    dve.wait_ge(split_hi.sem, split_hi.at(L, at + b + 1))
                    chunks = slice(2 * b, 2 * b + 2)
                    dve.scalar_tensor_tensor(dst[1][:, chunks, :], bank[first + b][:, :].rearrange("p (c t) -> p c t", c=2), factor,
                                             dst[0][:, chunks, :].bitcast(F32), ALU.mult, ALU.subtract).then_inc(split_lo.sem, 1)

            def bc(ap, shape):
                return ap.to_broadcast(shape)

            def task(L, stage, arg):
                if stage == "norm":
                    norm_lo(L, 1, 4)
                elif stage == "qkT":
                    dve.wait_ge(qkT_ps.sem, qkT_ps.at(L, arg + 1))
                    for b in range(2):
                        last = dve.tensor_scalar(qkT_buf[:, arg % 2, 1, 2 * b:2 * b + 2, :],
                                                 bank[6 + b][:, :].rearrange("p (c t) -> p c t", c=2),
                                                 1.0 if arg == 0 else gain(HEAD_AT + 2 * (arg - 1) + 1), None, ALU.mult)
                    last.then_inc(kT_ready.sem, 1)
                elif stage == "scores":
                    dve.wait_ge(scores_ready.sem, scores_ready.at(L, arg + 1))
                    if arg < 4:
                        if arg:
                            dve.wait_ge(pT_ps.sem, pT_ps.at(L, arg))
                        dve.tensor_tensor(probs[:, 0:512].rearrange("p (h k) -> p h k", h=4),
                                          bank[4][:, :].rearrange("p (h k) -> p h k", h=4),
                                          mask[:, None, P:SEQ].to_broadcast([P, 4, P]), ALU.add)
                        for b in range(2):
                            at = 512 + 512 * b
                            last = dve.tensor_tensor(probs[:, at:at + 512].rearrange("p (h k) -> p h k", h=2),
                                                     bank[5 + b][:, :].rearrange("p (h k) -> p h k", h=2),
                                                     mask[:, None, :].to_broadcast([P, 2, SEQ]), ALU.add)
                        link(L, last)
                        dve.tensor_reduce(mx[:, 0:4], probs[:, 0:512].rearrange("p (h k) -> p h k", h=4), axis=AX.X, op=ALU.max)
                        link(L, dve.tensor_reduce(mx[:, 4:8], probs[:, 512:].rearrange("p (h k) -> p h k", h=4), axis=AX.X, op=ALU.max))
                        dve.tensor_scalar(nmx[:, :], mx[:, :], -(HD ** -0.5), None, ALU.mult).then_inc(max_ready.sem, 1)
                    else:
                        for t in range(NT):
                            last = dve.tensor_reduce(mx[:, 2 * t:2 * t + 2], bank[4 + t][:, :].rearrange("p (h k) -> p h k", h=2),
                                                     axis=AX.X, op=ALU.max)
                        link(L, last)
                        dve.tensor_scalar(nmx[:, 0:4], mx[:, 0:4], -(MHD ** -0.5), None, ALU.mult).then_inc(max_ready.sem, 1)
                elif stage == "probsT":
                    dve.wait_ge(pT_ps.sem, pT_ps.at(L, arg + 1))
                    for b in range(2 if arg < 4 else 1):
                        last = dve.tensor_copy(pT[:, 1 + b, :], bank[5 + b][:, :])
                    last.then_inc(pT_dve.sem, 1)
                elif stage == "values":
                    br, n, d = arg // 2, 4 if arg < 4 else 2, HD if arg < 4 else MHD
                    dve.wait_ge(pv_ready.sem, pv_ready.at(L, arg + 1))
                    link(L, dve.reciprocal(rden[:, 0:2 * n], den[:, 0:2 * n]))
                    if arg < 4:
                        dst = o[:, br].rearrange("p t (h two d) -> p t h two d", two=2, d=d)[:, :, :, arg % 2, :]
                    else:
                        dst = o[:, br].rearrange("p t (two h d) -> p t two h d", two=2, d=d)[:, :, arg % 2]
                    dve.tensor_tensor(dst,
                                      bank[7][:, :].rearrange("p (t h d) -> p t h d", t=NT, h=n),
                                      rden[:, 0:2 * n].rearrange("p (t h) -> p t h", t=NT)[:, :, :, None].to_broadcast([P, NT, n, d]),
                                      ALU.mult).then_inc(o_ready.sem, 1)
                elif stage == "cumsum":
                    dve.wait_ge(c_ready.sem, c_ready.at(L, 1))
                    dve.tensor_scalar(negc[:, :], bank[4][0:NH, 0:SEQ], -float(HD ** 0.5), None, ALU.mult).then_inc(negc_ready.sem, 1)
                elif stage == "pool":
                    split(L, "pooled")
                elif stage == "oT":
                    split(L, f"o{arg}")
                elif stage == "zT":
                    split(L, f"z{arg}")

            def serve(L, s, kind, arg, half):
                if kind == "f":
                    dve.wait_ge(used.sem, used.at(L, 2 * s + 2))
                    link(L, dve.tensor_tensor(fz[:, :, :], bank[7][:, 0:NT * NH].rearrange("p (t h) -> p t h", t=NT),
                                              own[:, :, FORGET_AT:FORGET_AT + NH].to_broadcast([P, NT, NH]), ALU.add))
                    dve.scalar_tensor_tensor(fna[:, :, :], fz[:, :, :], -1.0, fz[:, :, :], ALU.mult, ALU.min).then_inc(fna_ready.sem, 1)
                    dve.wait_ge(fl_done.sem, fl_done.at(L, 1))
                    dve.scalar_tensor_tensor(lf[:, :, :], fz[:, :, :], 0.0, fl[:, :, :], ALU.min, ALU.subtract).then_inc(lf_ready.sem, 1)
                elif kind == "mixing":
                    at = 2 * SPLITS.index("mixed")
                    for b in range(2):
                        dve.wait_ge(split_hi.sem, split_hi.at(L, at + b + 1))
                        for g in (2 * b, 2 * b + 1):
                            last = dve.scalar_tensor_tensor(brT[0][1][:, g, :], bank[6 + b][:, (g % 2) * SEQ:(g % 2 + 1) * SEQ],
                                                            gain(POOL_AT + g), brT[0][0][:, g, :].bitcast(F32),
                                                            ALU.mult, ALU.subtract)
                        last.then_inc(split_lo.sem, 1)
                elif kind == "y":
                    n, dh = arg
                    idx = GATES.index(arg)
                    dve.wait_ge(taken_act.sem, taken_act.at(L, 4 + idx + 1))
                    dve.wait_ge(used.sem, used.at(L, 2 * s + 2))
                    banks = banks_of(s)
                    zs = [z[:, t, dh * BW:(dh + 1) * BW] for t in range(NT)]
                    gs = [gate[:, idx % 2, t, :] for t in range(NT)]
                    for t in range(NT):
                        last = dve.scalar_tensor_tensor(zs[t] if idx < 2 else gs[t], gs[t], 1.0, banks[t][:, :], ALU.add, ALU.mult)
                    if idx >= 2:
                        link(L, last)
                        for t in range(NT):
                            last = dve.tensor_tensor(zs[t], zs[t], gs[t], ALU.add)
                    last.then_inc(taken_dve.sem, 1)
                elif half == 1 and kind in NORMED:
                    dst, heads = HEAD_DST[kind]
                    d = BW // heads
                    banks = banks_of(s)
                    dve.wait_ge(squares.sem, squares.at(L, 2 * NORMED.index(kind) + 2))
                    link(L, dve.tensor_reduce(hss[:, 0:NT * heads].rearrange("p (t h) -> p t h", t=NT),
                                              dst[:, :, :].rearrange("p t (h d) -> p t h d", h=heads), axis=AX.X, op=ALU.add))
                    n = NT * heads
                    link(L, dve.tensor_scalar(ms[:, 0:n], hss[:, 0:n], 1.0 / d, EPS, ALU.mult, ALU.add))
                    newton(L, rs[:, 0:n], ms[:, 0:n], n)
                    for t in range(NT):
                        last = dve.tensor_tensor(dst[:, t, :].rearrange("p (h d) -> p h d", h=heads),
                                                 banks[t][:, :].rearrange("p (h d) -> p h d", h=heads),
                                                 rs[:, t * heads:(t + 1) * heads, None].to_broadcast([P, heads, d]), ALU.mult)
                    if kind in ("qa", "ka"):
                        link(L, last)
                        at = MOBA_AT + (0 if kind == "qa" else HD)
                        for t in range(NT):
                            rows = dst[:, t, :].rearrange("p (h d) -> p h d", h=heads)
                            last = dve.tensor_tensor(rows, rows, own[:, :, at:at + HD].to_broadcast([P, heads, HD]), ALU.mult)
                        link(L, last)
                        dve.wait_ge(trig_done.sem, trig_done.at(L, 2))
                        halves = [dst[:, :, :].rearrange("p t (h d) -> p t h d", h=heads)[:, :, :, 8 * i:8 * i + 8] for i in range(2)]
                        tables = [v[:, :, None, :].to_broadcast([P, NT, heads, 8]) for v in (cosv, sinv)]
                        for i, (a, b) in enumerate(((0, 0), (1, 1), (1, 0), (0, 1))):
                            last = dve.tensor_tensor(rot[:, i], halves[a], tables[b], ALU.mult)
                        link(L, last)
                        dve.tensor_tensor(halves[0], rot[:, 0], rot[:, 1], ALU.subtract)
                        last = dve.tensor_tensor(halves[1], rot[:, 2], rot[:, 3], ALU.add)
                    last.then_inc(taken_dve.sem, 1)

            def mixer(L):
                for i, (kind, arg, b, half) in enumerate(MIX):
                    if (kind, arg) == ("out", 2):
                        break
                    ahead(L, MIX0 + i)
                    serve(L, MIX0 + i, kind, arg, half)
                    for stage, targ in TASKS.get(MIX0 + i, ()):
                        task(L, stage, targ)
                boundary(L, 1, 2, FFN2_0 - 2, 1.0)

            dve.sem_inc(lo_done.sem, lo_done.credit)
            dve.sem_inc(prod_done.sem, prod_done.credit)

            for t in range(NT):
                dve.wait_ge(mem_squares, t + 1)
                link(None, dve.tensor_scalar(ms[:, 0:1], ss[:, t, 0:1], 0.5 / DM, 0.5 * EPS, ALU.mult, ALU.add))
                newton_row(None)
                dve.tensor_scalar(mem_n[:, t, :], memx[:, t, :], rs[:, 0:1], -1.0, ALU.mult, ALU.mult).then_inc(mem_rows, 1)
            dve.wait_ge(gains_loaded, 16)
            dve.tensor_copy(next_gain[:, :, :], gains[:, 0:1, MEMORY_AT:MEMORY_AT + KC]).then_inc(next_gain_ready.sem, 1)
            dve.wait_ge(mem_turned, 1)
            for b in range(2, 4):
                last = dve.tensor_copy(memN[:, 2 * b:2 * b + 2, :], bank[b][:, :].rearrange("p (c t) -> p c t", c=2))
            last.then_inc(memN_dve, 1)
            memory_lo(0, 1)
            dve.wait_ge(x_loaded, 16)
            norm(None, 0, 0)
            dve.sem_inc(x_ready.sem, x_ready.credit)
            dve.wait_ge(setup_loads, 16 * N_SETUP)
            with dve.Fori(0, DEPTH) as L:
                for k in range(2):
                    lo(L, 0, k)
                dve.tensor_copy(own[:, :, :], gains[:, bass.ds(L, 1), :]).then_inc(own_ready.sem, 1)
                norm(L, 0, 1)
                for k in range(2):
                    lo(L, 1, k)
                dve.wait_ge(own_ready.sem, own_ready.at(L, 1))
                norm_lo(L, 0, 4)
                ahead(L, 0)
                ahead(L, 1)
                serve(L, 1, "mk", None, 1)
                feed_forward(L, 0, FFN1_0)
                mixer(L)
                norm_lo(L, 2, 0)
                feed_forward(L, 1, FFN2_0)
            assert links[0] == VLINKS, links


TWO_PI_PARTS = []
_rest = 2 * np.pi
for _bits in (9, 11, 24):
    _unit = 2.0 ** (np.floor(np.log2(abs(_rest))) - _bits + 1)
    _part = float(np.float32(np.round(_rest / _unit) * _unit))
    TWO_PI_PARTS.append(_part)
    _rest -= _part

_INS = ["x", "mem", "w_ffn1_in", "w_ffn1_out", "w_in", "w_mem_kv", "pool_mix", "w_branch", "w_out",
        "w_ffn2_in", "w_ffn2_out"]


def lay_out_gains(v):
    def columns(a):
        return a.reshape(DEPTH, -1, P).transpose(2, 0, 1)

    def rows(a):
        return np.broadcast_to(a[None], (P,) + a.shape)

    parts = [columns(v[n]) for n in ("norm_ffn1", "norm_mix", "norm_ffn2", "norm_mem", "pool_scale")]
    parts += [columns(np.concatenate([v[n], v[n]], axis=1)) for n in ("fox_q_gain", "fox_k_gain")]
    parts += [columns(v[n]) for n in ("mem_q_gain", "mem_k_gain")]
    parts += [rows(v[n]) for n in ("b_forget", "moba_q_gain", "moba_k_gain")]
    laid = np.concatenate(parts, axis=2)
    return np.concatenate([laid, np.zeros_like(laid[:, :1])], axis=1)


def shape_constants():
    s, t = np.arange(P)[:, None], np.arange(SEQ)[None, :]
    mask = np.where((t >= P) & (t - P > s), NEG, 0.0)
    upto = (s <= t).astype(np.float64)
    bands = []
    for w in WINDOWS:
        for first, tt in ((0, t), (P, t[:, P:])):
            src = s + first
            inside = (src <= tt) & (src > tt - w)
            bands.append(inside / np.minimum(tt + 1, w) - (src == tt))
    const = np.concatenate([np.eye(P), mask, upto] + bands, axis=1).astype(np.float32)
    half = HD // 8
    freq = np.power(np.float32(500000.0), -np.arange(half, dtype=np.float32) * np.float32(2.0 / (2 * half))).astype(np.float32)
    return const, np.broadcast_to(freq[None], (P, half))


def kernel(**inputs):
    import concourse.bacc as bacc
    from concourse.bass_utils import run_bass_kernel_spmd

    nc = bacc.Bacc("TRN2", target_bir_lowering=False, num_devices=1)
    arrays, args = {}, []

    def take(name, a):
        arrays[name] = np.ascontiguousarray(a)
        args.append(nc.dram_tensor(name, a.shape, mybir.dt.from_np(a.dtype), kind="ExternalInput").ap())

    inputs = {name: np.asarray(a) for name, a in inputs.items()}
    for name in _INS:
        take(f"in_{name}", inputs[name])
    take("gains_dram", lay_out_gains(inputs))
    take("positions_dram", inputs["positions"].reshape(NT, P).T)
    for name, a in zip(("const_dram", "freq_dram"), shape_constants()):
        take(name, a)
    args.append(nc.dram_tensor("out_dram", (1, SEQ, DM), F32, kind="ExternalOutput").ap())
    build(nc, *args)
    r = run_bass_kernel_spmd(nc, [arrays], core_ids=[0])
    return r.results[0]["out_dram"]
```

```python
from contextlib import ExitStack

import numpy as np

import concourse.bass as bass
from concourse import mybir

F32 = mybir.dt.float32
F32R = mybir.dt.float32r
I32 = mybir.dt.int32
ACT = mybir.ActivationFunctionType
ALU = mybir.AluOpType
AX = mybir.AxisListType

P = 128
DEPTH, SEQ, DM, DFF = 2, 256, 1024, 2816
NT = SEQ // P
KC = DM // P
FC = DFF // P
HD, NH = 64, 8
MHD, MH = 128, 4
BW, BC = 512, 4
EPS = 1e-6
WINDOWS = (2, 4, 8, 16)
NEG = -1e30
IN_F = 6 * NH * HD
IN_POOL = IN_F + NH
IN_MEMQ = IN_POOL + BW
IN_GATE = IN_MEMQ + BW

RAW, SLOTS = 4, 4
LOADW, UNITW = 2048, 1024

FFN_STEPS = FC + FC // 2
TOP = 2
FFN1_0 = TOP
MIX0 = FFN1_0 + FFN_STEPS
MIX = []
TOP_MIX = [("mk", None, -1, 0), ("mk", None, -1, 1)]


def _blocks():
    b = 1

    def proj(kind, arg=None):
        nonlocal b
        MIX.append((kind, arg, b, 0))
        MIX.append((kind, arg, b, 1))
        b += 1

    for kind in ("mv", "qa", "ka", "va", "qc", "kc"):
        proj(kind)
    MIX.append(("f", None, None, 0))
    for kind in ("vc", "pu"):
        proj(kind)
    proj("gate", (1, 0))
    MIX.append(("mixing", None, None, 0))
    proj("qm")
    proj("gate", (1, 1))
    for dh in range(2):
        MIX.append(("y", (1, dh), b + dh, 0))
    b += 2
    for n in (0, 2, 3):
        for dh in range(2):
            proj("gate", (n, dh))
            MIX.append(("y", (n, dh), b, 0))
            b += 1
    for j in range(KC // 2):
        MIX.append(("out", j, None, 0))


_blocks()
FFN2_0 = MIX0 + len(MIX)
STEPS = FFN2_0 + FFN_STEPS
UNITS = 2 * STEPS
assert STEPS % RAW == 0 and UNITS % SLOTS == 0

BLOCK_KIND, BLOCK_OF = {}, {}
for kind, arg, b, half in TOP_MIX + MIX:
    if b is not None:
        BLOCK_KIND[b] = kind
        BLOCK_OF[kind, arg] = b
BY_ACT = ("mv", "va", "vc", "pu", "gate")


def taken_before(b):
    by_act = BLOCK_KIND[b] in BY_ACT
    return by_act, sum((kind in BY_ACT) == by_act for i, kind in BLOCK_KIND.items() if i <= b)


def release(kind, arg=None):
    return taken_before(BLOCK_OF[kind, arg])[1]


def _step_of(kind, arg=None, half=0):
    return MIX0 + next(i for i, s in enumerate(MIX) if s[0] == kind and s[1] == arg and s[3] == half)


TASKS = {}
for s, task in [
    (_step_of("mv"), ("norm", None)),
    (_step_of("va", None, 1), ("qkT", 0)),
    (_step_of("qc"), ("scores", 0)),
    (_step_of("kc"), ("probsT", 0)),
    (_step_of("vc"), ("scores", 1)),
    (_step_of("vc", None, 1), ("values", 0)),
    (_step_of("pu"), ("probsT", 1)),
    (_step_of("pu", None, 1), ("values", 1)),
    (_step_of("gate", (1, 0)), ("pool", None)),
    (_step_of("qm", None, 1), ("qkT", 1)),
    (_step_of("gate", (1, 1)), ("scores", 2)),
    (_step_of("gate", (1, 1), 1), ("probsT", 2)),
    (_step_of("y", (1, 0)), ("values", 2)),
    (_step_of("y", (1, 0)), ("oT", 0)),
    (_step_of("y", (1, 1)), ("scores", 3)),
    (_step_of("gate", (0, 0), 1), ("probsT", 3)),
    (_step_of("y", (0, 0)), ("values", 3)),
    (_step_of("gate", (0, 1)), ("oT", 1)),
    (_step_of("gate", (0, 1), 1), ("qkT", 2)),
    (_step_of("y", (0, 1)), ("scores", 4)),
    (_step_of("gate", (2, 0), 1), ("probsT", 4)),
    (_step_of("y", (2, 0)), ("values", 4)),
    (_step_of("y", (2, 0)), ("scores", 5)),
    (_step_of("gate", (2, 1), 1), ("probsT", 5)),
    (_step_of("y", (2, 1)), ("values", 5)),
    (_step_of("gate", (3, 0)), ("oT", 2)),
    (_step_of("gate", (3, 1)), ("zT", 0)),
    (_step_of("out", 0), ("zT", 1)),
]:
    TASKS.setdefault(s, []).append(task)

SPLITS = ["pooled", "mixed", "o0", "o1", "o2", "z0", "z1"]
NORMED = ["mk", "qa", "ka", "qc", "kc", "qm"]


class Tally:

    def __init__(self, sem, per_layer, credit=0):
        self.sem, self.per_layer, self.credit = sem, per_layer, credit

    def at(self, layer, count):
        return layer * self.per_layer + (self.credit + count)


def build(nc, x_d, mem_d, w1i_d, w1o_d, win_d, wkv_d, pmix_d, wbr_d, wout_d, w2i_d, w2o_d,
          gains_d, pos_d, const_d, freq_d, out_d):
    ctx = ExitStack()
    with ctx:
        def sb(name, shape, dt=F32, scope=ctx):
            return scope.enter_context(nc.sbuf_tensor(name, shape, dt))

        const = sb("const", [P, const_d.shape[1]])
        ident = const[:, 0:P]
        mask = const[:, P:P + SEQ]
        band = const[:, P + SEQ:].rearrange("p (g c) -> p g c", g=4)
        freq = sb("freq", [P, 8])
        NORM_AT, POOL_AT, HEAD_AT, FORGET_AT, MOBA_AT, N_GAINS = 0, 32, 36, 40, 41, 169
        MEMORY_AT = NORM_AT + 3 * KC
        gains = sb("gains", [P, DEPTH + 1, N_GAINS])
        own = sb("own", [P, 1, N_GAINS])
        next_gain = sb("next_gain", [P, 1, KC])
        pos_i = sb("pos_i", [P, NT], I32)
        pos_f = sb("pos_f", [P, NT])
        ang = sb("ang", [P, NT, 8])
        turns = sb("turns", [P, NT, 8])
        absang = sb("absang", [P, NT, 8])
        cosv = sb("cosv", [P, NT, 8])
        sinv = sb("sinv", [P, NT, 8])
        ss = sb("ss", [P, NT, 2])
        ms = sb("ms", [P, 16])
        rs = sb("rs", [P, 16])
        row_rs = sb("row_rs", [P, NT])
        ra = sb("ra", [P, 16])
        rb = sb("rb", [P, 16])
        hss = sb("hss", [P, 16])
        mx = sb("mx", [P, 8])
        nmx = sb("nmx", [P, 8])
        den = sb("den", [P, 2, 8])
        rden = sb("rden", [P, 8])
        negc = sb("negc", [NH, SEQ])
        x = sb("x", [P, NT, DM])
        memN = sb("memN", [P, KC, SEQ])
        hT = [sb("hT_hi", [P, KC, SEQ], F32R), sb("hT_lo", [P, KC, SEQ], F32R)]
        raw = sb("raw", [P, RAW, LOADW])
        ring = [sb("ring_hi", [P, SLOTS, UNITW], F32R), sb("ring_lo", [P, SLOTS, UNITW], F32R)]
        with ExitStack() as ffn:
            act_hi = sb("act_hi", [P, FC, SEQ], F32R, ffn)
            act_lo = sb("act_lo", [P, FC, SEQ], F32R, ffn)
            silu = sb("silu", [P, 2, SEQ], F32, ffn)
            prod = sb("prod", [P, 2, SEQ], F32, ffn)
        qk = sb("qk", [P, 2, NT, BW])
        mem_n = qk[:, :, :, :].rearrange("p a t c -> p a (t c)")
        vals = sb("vals", [P, 3, NT, BW])
        qkT_buf = sb("qkT", [P, 2, 2, BC, SEQ])
        with ExitStack() as pooling:
            pooledT = [sb("pooledT_hi", [P, BC, SEQ], F32R, pooling), sb("pooledT_lo", [P, BC, SEQ], F32R, pooling)]
        probs = sb("probs", [P, 1536])
        pT = sb("pT", [P, 3, 512])
        kmem = sb("kmem", [P, NT, BW])
        gate = sb("gate", [P, 2, NT, BW])
        xn = gate[:, :, :, :].rearrange("p a t c -> p a (t c)")
        with ExitStack() as early:
            memx = sb("memx", [P, NT, DM], F32, early)
        brT = [[sb(f"brT{i}_{part}", [P, BC, SEQ], F32R) for part in ("hi", "lo")] for i in range(2)]
        with ExitStack() as early:
            memhT = [sb("memhT_hi", [P, KC, SEQ], F32R, early), sb("memhT_lo", [P, KC, SEQ], F32R, early)]
        o = sb("o", [P, 3, NT, BW])
        z = sb("z", [P, NT, DM])
        fz, fmin, fna, fe, fl, csum = (z[0:NH, i // 3, i % 3 * SEQ:(i % 3 + 1) * SEQ] for i in range(6))
        rot = z[:, 1, 0:4 * NT * NH * 8].rearrange("p (i t h d) -> p i t h d", i=4, t=NT, h=NH)

        bank = [ctx.enter_context(nc.psum_tensor(f"bank{i}", [P, 512], F32)) for i in range(8)]

        def tally(name, per_layer, credit=0):
            return Tally(ctx.enter_context(nc.semaphore(name)), per_layer, credit)

        setup_loads = ctx.enter_context(nc.semaphore("setup_loads"))
        x_loaded = ctx.enter_context(nc.semaphore("x_loaded"))
        setup_step = ctx.enter_context(nc.semaphore("setup_step"))
        stored = ctx.enter_context(nc.semaphore("stored"))
        raw_ready = [tally(f"raw_ready{i}", 16 * STEPS // RAW) for i in range(RAW)]
        hi_done = tally("hi_done", UNITS)
        lo_done = tally("lo_done", UNITS, 2 * RAW)
        used = tally("used", UNITS, SLOTS)
        mem_loaded = [ctx.enter_context(nc.semaphore(f"mem_loaded{t}")) for t in range(NT)]
        ident_loaded = ctx.enter_context(nc.semaphore("ident_loaded"))
        gains_loaded = ctx.enter_context(nc.semaphore("gains_loaded"))
        mem_squares = ctx.enter_context(nc.semaphore("mem_squares"))
        mem_rows = ctx.enter_context(nc.semaphore("mem_rows"))
        mem_turned = ctx.enter_context(nc.semaphore("mem_turned"))
        memN_act = ctx.enter_context(nc.semaphore("memN_act"))
        next_gain_ready = tally("next_gain_ready", 1)
        memh_hi = tally("memh_hi", 4)
        memh_ready = tally("memh_ready", 4)
        ang_ready = tally("ang_ready", 2)
        trig_done = tally("trig_done", 2)
        own_ready = tally("own_ready", 1)
        x_ready = tally("x_ready", 12, 1)
        sumsq = tally("sumsq", 12)
        rs_ready = tally("rs_ready", 6)
        xn_first = tally("xn_first", 6)
        xn_second = tally("xn_second", 6)
        xnT = tally("xnT", 12)
        h_hi = tally("h_hi", 12)
        h_ready = tally("h_ready", 12)
        silu_done = tally("silu_done", 2 * FC)
        prod_done = tally("prod_done", 2 * FC, 4)
        act_hi_done = tally("act_hi_done", 2 * FC)
        act_ready = tally("act_ready", 2 * FC)
        rows0_ready = tally("rows0_ready", 3)
        half_row_ready = tally("half_row_ready", 1)
        taken_act = tally("taken_act", sum(k in BY_ACT for k in BLOCK_KIND.values()))
        taken_dve = tally("taken_dve", sum(k not in BY_ACT for k in BLOCK_KIND.values()))
        rotated = tally("rotated", 2)
        squares = tally("squares", 2 * len(NORMED))
        qkT_ps = tally("qkT_ps", 3)
        qT_ready = tally("qT_ready", 3)
        kT_ready = tally("kT_ready", 3)
        scores_ready = tally("scores_ready", 6)
        max_ready = tally("max_ready", 6)
        probs_ready = tally("probs_ready", 6)
        pT_ps = tally("pT_ps", 6)
        pT_act = tally("pT_act", 6)
        pT_dve = tally("pT_dve", 6)
        pv_ready = tally("pv_ready", 6)
        o_ready = tally("o_ready", 6)
        fna_ready = tally("fna_ready", 1)
        fe_done = tally("fe_done", 1)
        fl_done = tally("fl_done", 1)
        negc_ready = tally("negc_ready", 1)
        split_ps = tally("split_ps", 2 * len(SPLITS) - 2)
        split_hi = tally("split_hi", 2 * len(SPLITS))
        split_lo = tally("split_lo", 2 * len(SPLITS))
        VLINKS = 156
        vlink = tally("vlink", VLINKS)

        def unit_words(step, k):
            local = step - (FFN1_0 if step < MIX0 else FFN2_0)
            if (step < MIX0 or step >= FFN2_0) and 0 <= local < FC:
                i, half = divmod(local, 2)
                m = step - local + 2 * i + k
                view = raw[:, m % RAW, :].rearrange("p (k c) -> p k c", k=KC)[:, :, half * P:(half + 1) * P]
                return m, view, UNITW
            n = UNITW
            if MIX0 <= step < FFN2_0:
                n = {"f": KC * NH // 2, "mixing": BW // 2}.get(MIX[step - MIX0][0], UNITW)
            return step, raw[:, step % RAW, k * n:(k + 1) * n], n

        def unit_slot(part, step, k):
            return ring[part][:, (2 * step + k) % SLOTS, :]

        def unit_out(part, step, k):
            _, view, n = unit_words(step, k)
            slot = unit_slot(part, step, k)[:, 0:n]
            return slot.rearrange("p (k c) -> p k c", k=KC) if len(view.shape) == 3 else slot

        def steps_in_loop(engine, body):
            with engine.Fori(0, FC // 4) as j:
                for c in range(4):
                    body(j, c)
            for c in range(FC // 4 * 4, FC):
                body(None, c)

        N_SETUP = 3
        block = ctx.enter_context(nc.Block())

        @block.sync
        def _(sp):
            for t in range(NT):
                sp.dma_start(memx[:, t, :], mem_d[0, t * P:(t + 1) * P, :]).then_inc(mem_loaded[t], 16)
            sp.dma_start(x[:, :, :], x_d[0].rearrange("(t p) d -> p t d", p=P)).then_inc(x_loaded, 16)

            def load(L, m, dst, src, j=None, gates_at=None):
                late = 1 if gates_at is not None and (m - RAW - gates_at) % 2 == 0 and m - RAW >= gates_at else 0
                need = lo_done.at(L, 2 * (m - RAW) + 2 + late)
                sp.wait_ge(lo_done.sem, need if j is None else need + 8 * j)
                sp.dma_start(dst, src).then_inc(raw_ready[m % RAW].sem, 16)

            def ffn_loads(L, base, w_in, w_out):
                def columns(j, i):
                    for k in range(2):
                        m = base + 2 * i + k
                        dst = raw[:, m % RAW, :].rearrange("p (k c) -> p k c", k=KC)
                        at = k * DFF + 2 * P * i
                        cols = slice(at, at + 2 * P) if j is None else bass.ds(j * (4 * P) + at, 2 * P)
                        src = w_in[bass.ds(L, 1), :, cols].rearrange("a (k p) c -> p (a k) c", p=P)
                        load(L, m, dst, src, j, base)
                columns(None, 0)
                columns(None, 1)
                with sp.Fori(0, FC // 4 - 1) as j:
                    columns(j, 2)
                    columns(j, 3)
                for i in range(FC // 4 * 2, FC // 2):
                    columns(None, i)
                for r in range(FC // 2):
                    m = base + FC + r
                    src = w_out[bass.ds(L, 1), 2 * P * r:2 * P * (r + 1), :].rearrange("a (h p) c -> p (a h) c", p=P)
                    load(L, m, raw[:, m % RAW, :].rearrange("p (h c) -> p h c", h=2), src, None, base if r < RAW else None)

            with sp.Fori(0, DEPTH) as L:
                for i, (kind, arg, b, half) in enumerate(TOP_MIX + MIX):
                    if i == TOP:
                        ffn_loads(L, FFN1_0, w1i_d, w1o_d)
                    m = i if i < TOP else MIX0 + i - TOP
                    dst = raw[:, m % RAW, :]
                    rows = slice(half * BW, (half + 1) * BW)
                    if kind in ("mk", "mv"):
                        at = {"mk": 0, "mv": BW}[kind]
                        src = wkv_d[bass.ds(L, 1), rows, at:at + BW].rearrange("a (k p) c -> p (a k) c", p=P)
                        dst = dst.rearrange("p (k c) -> p k c", k=4)
                    elif kind == "f":
                        src = win_d[bass.ds(L, 1), :, IN_F:IN_F + NH].rearrange("a (k p) c -> p (a k) c", p=P)
                        dst = dst[:, 0:KC * NH].rearrange("p (k c) -> p k c", k=KC)
                    elif kind == "mixing":
                        src = pmix_d[bass.ds(L, 1)].rearrange("a g p e -> p (a g) e")
                        dst = dst[:, 0:BW].rearrange("p (g e) -> p g e", g=4)
                    elif kind == "y":
                        n, dh = arg
                        src = wbr_d.rearrange("l n (k p) c -> p (l n k) c", p=P)[:, bass.ds(L * (4 * BC) + n * BC, BC), dh * BW:(dh + 1) * BW]
                        dst = dst.rearrange("p (k c) -> p k c", k=BC)
                    elif kind == "out":
                        src = wout_d[bass.ds(L, 1), 2 * P * arg:2 * P * (arg + 1), :].rearrange("a (h p) c -> p (a h) c", p=P)
                        dst = dst.rearrange("p (h c) -> p h c", h=2)
                    else:
                        at = {"qa": 0, "ka": BW, "va": 2 * BW, "qc": 3 * BW, "kc": 4 * BW, "vc": 5 * BW,
                              "pu": IN_POOL, "qm": IN_MEMQ}.get(kind)
                        if kind == "gate":
                            at = IN_GATE + arg[0] * DM + arg[1] * BW
                        src = win_d[bass.ds(L, 1), rows, at:at + BW].rearrange("a (k p) c -> p (a k) c", p=P)
                        dst = dst.rearrange("p (k c) -> p k c", k=4)
                    load(L, m, dst, src)
                ffn_loads(L, FFN2_0, w2i_d, w2o_d)

            for t in range(NT):
                sp.wait_ge(x_ready.sem, x_ready.at(DEPTH - 1, 8 + 2 * t + 2))
                sp.dma_start(out_d[0, t * P:(t + 1) * P, :], x[:, t, :]).then_inc(stored, 16)
            sp.wait_ge(stored, 16 * NT)

        @block.tensor
        def _(pe):
            def three(out, act_parts, weight_parts, first, last, moving_weights):
                for n, (a, w) in enumerate(((0, 0), (0, 1), (1, 0))):
                    lhsT, rhs = (act_parts[a], weight_parts[w]) if moving_weights else (weight_parts[w], act_parts[a])
                    mm = pe.matmul(out, lhsT, rhs, start=first and n == 0, stop=last and n == 2)
                return mm

            def wait_unit(L, n, j=None):
                need = lo_done.at(L, n + 1)
                pe.wait_ge(lo_done.sem, need if j is None else need + 8 * j)

            def norm_transposes(L, index, banks, by_tile, tiles=(0, 1)):
                for t in tiles:
                    for kc in range(KC):
                        if t == 0 and not by_tile and kc == 0:
                            pe.wait_ge(xn_first.sem, xn_first.at(L, 2 * index + 2))
                        if kc % 4 == 0:
                            half = xn_second if kc else xn_first
                            pe.wait_ge(half.sem, half.at(L, 2 * index + t + 1))
                        at = (kc % 2) * SEQ + t * P
                        mm = pe.transpose(bank[banks + kc // 2][:, at:at + P], xn[:, t, kc * P:(kc + 1) * P], ident)
                        if t == NT - 1 and kc % 2:
                            mm.then_inc(xnT.sem, 1)

            def hidden(L, base, first_chunk, norm):
                def body(j, c):
                    n = 2 * (base + c)
                    need = prod_done.at(L, first_chunk + c + 1 - 4)
                    pe.wait_ge(prod_done.sem, need if j is None else need + 4 * j)
                    if c == 2 and norm == 0:
                        pe.wait_ge(taken_dve.sem, taken_dve.at(L, release("mk")))
                    for k in range(2):
                        wait_unit(L, n + k, j)
                        w = [unit_slot(part, base + c, k).rearrange("p (k c) -> p k c", k=KC) for part in range(2)]
                        for kc in range(KC):
                            if c == 0 and k == 0 and kc % 2 == 0:
                                pe.wait_ge(h_ready.sem, h_ready.at(L, 4 * norm + kc // 2 + 1))
                            mm = three(bank[c % 4][:, k * SEQ:(k + 1) * SEQ], [hT[p][:, kc, :] for p in range(2)],
                                       [w[p][:, kc, :] for p in range(2)], kc == 0, kc == KC - 1, False)
                        mm.then_inc(used.sem, 1)
                return body

            def rows(L, steps, acts, first, last, turn_tile0=None):
                units = [(step, k) for step in steps for k in range(2)]

                def product(t, u, halves=(0, 1)):
                    step, k = units[u]
                    w = [unit_slot(part, step, k) for part in range(2)]
                    a = [acts[part][u][:, t * P:(t + 1) * P] for part in range(2)]
                    for (ap, wp) in ((0, 0), (0, 1), (1, 0)):
                        for half in halves:
                            mm = pe.matmul(bank[4 + 2 * t + half][:, :], a[ap], w[wp][:, half * 512:(half + 1) * 512],
                                           start=first and u == 0 and (ap, wp) == (0, 0),
                                           stop=last and u == len(units) - 1 and ap == 1)
                    return mm

                for u, (step, k) in enumerate(units):
                    wait_unit(L, 2 * step + k)
                    mm = product(0, u)
                    if not last:
                        product(1, u).then_inc(used.sem, 1)
                if last:
                    mm.then_inc(rows0_ready.sem, 1)
                    if turn_tile0 is not None:
                        for u in range(len(units)):
                            mm = product(1, u, (0,))
                        mm.then_inc(half_row_ready.sem, 1)
                    for u in range(len(units)):
                        if turn_tile0 is not None and u == len(units) - 1:
                            turn_tile0()
                        product(1, u, (0, 1) if turn_tile0 is None else (1,)).then_inc(used.sem, 1)

            def feed_forward(L, which, base):
                steps_in_loop(pe, hidden(L, base, which * FC, 2 * which))
                for r in range(FC // 2 - 1):
                    last = r == FC // 2 - 2
                    n = 4 if last else 2
                    pe.wait_ge(act_ready.sem, act_ready.at(L, which * FC + 2 * r + n))
                    rows(L, [base + FC + r + i for i in range(n // 2)], [[a[:, 2 * r + k, :] for k in range(n)] for a in (act_hi, act_lo)],
                         r == 0, last)

            def heads(L, g):
                br = g // 2
                buf = qkT_buf[:, br % 2]
                odd = g % 2
                hs = [(2 * c + odd, c, HD * odd) for c in range(BC)] if br < 2 else [(h, h, 0) for h in (2 * odd, 2 * odd + 1)]
                return br, buf, hs

            def task(L, stage, arg):
                if stage == "norm":
                    norm_transposes(L, 1, 4, False)
                elif stage == "qkT":
                    if arg == 0:
                        pe.wait_ge(rotated.sem, rotated.at(L, 2))
                    pe.wait_ge(taken_dve.sem, taken_dve.at(L, release({0: "ka", 1: "kc", 2: "qm"}[arg])))
                    if arg == 1:
                        pe.wait_ge(split_lo.sem, split_lo.at(L, 2 * SPLITS.index("mixed") + 2))
                    if arg == 2:
                        pe.wait_ge(split_lo.sem, split_lo.at(L, 2 * SPLITS.index("o1") + 2))
                    for i in range(2):
                        src = qk[:, i] if arg < 2 or i == 0 else kmem
                        for c in range(BC):
                            for t in range(NT):
                                at = (c % 2) * SEQ + t * P
                                mm = pe.transpose(bank[4 + 2 * i + c // 2][:, at:at + P], src[:, t, c * P:(c + 1) * P], ident)
                    mm.then_inc(qkT_ps.sem, 1)
                elif stage == "scores":
                    br, buf, hs = heads(L, arg)
                    pe.wait_ge(qT_ready.sem, qT_ready.at(L, br + 1))
                    pe.wait_ge(kT_ready.sem, kT_ready.at(L, br + 1))
                    if arg:
                        pe.wait_ge(pT_act.sem, pT_act.at(L, arg))
                        pe.wait_ge(pT_dve.sem, pT_dve.at(L, arg))
                    if arg == 2:
                        pe.wait_ge(negc_ready.sem, negc_ready.at(L, 1))
                    if arg == 3:
                        pe.wait_ge(split_lo.sem, split_lo.at(L, 2 * SPLITS.index("o0") + 2))
                    for i, (h, c, p) in enumerate(hs):
                        q, k = buf[p:p + (HD if br < 2 else MHD), 0, c, :], buf[p:p + (HD if br < 2 else MHD), 1, c, :]
                        if br < 2:
                            outs = [(bank[4][:, i * P:(i + 1) * P], 0, P),
                                    (bank[5 + i // 2][:, (i % 2) * SEQ:(i % 2 + 1) * SEQ], 1, SEQ)]
                        else:
                            outs = [(bank[4 + t][:, i * SEQ:(i + 1) * SEQ], t, SEQ) for t in range(NT)]
                        for out, t, keys in outs:
                            mm = pe.matmul(out, q[:, t * P:(t + 1) * P], k[:, 0:keys], start=True, stop=br != 1)
                            if br == 1:
                                mm = pe.matmul(out, ident[0:NH, h:h + 1].to_broadcast([NH, P]), negc[:, 0:keys], start=False, stop=True)
                    mm.then_inc(scores_ready.sem, 1)
                elif stage == "probsT":
                    br, buf, hs = heads(L, arg)
                    pe.wait_ge(probs_ready.sem, probs_ready.at(L, arg + 1))
                    for i in range(len(hs)):
                        if br < 2:
                            tiles = [(4, i, probs[:, i * P:(i + 1) * P])] + [
                                (5 + kt, i, probs[:, 512 + i * SEQ + kt * P:512 + i * SEQ + (kt + 1) * P]) for kt in range(2)]
                        else:
                            tiles = [(4 + t, 2 * i + kt, probs[:, t * 512 + i * SEQ + kt * P:t * 512 + i * SEQ + (kt + 1) * P])
                                     for t in range(NT) for kt in range(2)]
                        for b, at, src in tiles:
                            mm = pe.transpose(bank[b][:, at * P:(at + 1) * P], src, ident)
                    mm.then_inc(pT_ps.sem, 1)
                elif stage == "values":
                    br, buf, hs = heads(L, arg)
                    pe.wait_ge(pT_act.sem, pT_act.at(L, arg + 1))
                    pe.wait_ge(pT_dve.sem, pT_dve.at(L, arg + 1))
                    pe.wait_ge(taken_act.sem, taken_act.at(L, release({0: "va", 1: "vc", 2: "mv"}[br])))
                    if arg:
                        pe.wait_ge(o_ready.sem, o_ready.at(L, arg))
                    if arg == 0:
                        pe.wait_ge(fna_ready.sem, fna_ready.at(L, 1))
                    if arg == 4:
                        pe.wait_ge(kT_ready.sem, kT_ready.at(L, 3))
                    for i, (h, c, p) in enumerate(hs):
                        if br < 2:
                            for t in range(NT):
                                out = bank[7][:, t * SEQ + i * HD:t * SEQ + (i + 1) * HD]
                                for kt in range(t + 1):
                                    mm = pe.matmul(out, pT[:, t + kt, i * P:(i + 1) * P], vals[:, br, kt, h * HD:(h + 1) * HD],
                                                   start=kt == 0, stop=kt == t)
                        else:
                            for t in range(NT):
                                out = bank[7][:, t * SEQ + i * MHD:t * SEQ + (i + 1) * MHD]
                                for kt in range(2):
                                    mm = pe.matmul(out, pT[:, t, (2 * i + kt) * P:(2 * i + kt + 1) * P],
                                                   vals[:, 2, kt, h * MHD:(h + 1) * MHD], start=kt == 0, stop=kt == 1)
                    mm.then_inc(pv_ready.sem, 1)
                elif stage == "pool":
                    pe.wait_ge(taken_act.sem, taken_act.at(L, release("pu")))
                    pe.wait_ge(pT_act.sem, pT_act.at(L, 2))
                    pe.wait_ge(pT_dve.sem, pT_dve.at(L, 2))
                    for g in range(4):
                        out = bank[4 + g // 2][:, (g % 2) * SEQ:(g % 2 + 1) * SEQ]
                        pe.matmul(out, o[:, 2, 0, g * P:(g + 1) * P], band[:, g, 0:SEQ], start=True, stop=False)
                        mm = pe.matmul(out[:, P:SEQ], o[:, 2, 1, g * P:(g + 1) * P], band[:, g, SEQ:SEQ + P],
                                       start=False, stop=True)
                        if g % 2:
                            mm.then_inc(split_ps.sem, 1)
                elif stage in ("oT", "zT"):
                    if stage == "oT":
                        pe.wait_ge(o_ready.sem, o_ready.at(L, 2 * arg + 2))
                        first = 6 if arg == 1 else 4
                        src = o[:, arg]
                        if arg == 0:
                            pe.wait_ge(pT_act.sem, pT_act.at(L, 3))
                            pe.wait_ge(pT_dve.sem, pT_dve.at(L, 3))
                        if arg == 2:
                            pe.wait_ge(pT_act.sem, pT_act.at(L, 6))
                            pe.wait_ge(pT_dve.sem, pT_dve.at(L, 6))
                    else:
                        pe.wait_ge(taken_dve.sem, taken_dve.at(L, release("y", (3, arg))))
                        first = 4 if arg == 0 else 0
                        src = z[:, :, arg * BW:(arg + 1) * BW]
                        if arg == 0:
                            pe.wait_ge(split_lo.sem, split_lo.at(L, 2 * SPLITS.index("o2") + 2))
                    for c in range(BC):
                        for t in range(NT):
                            at = (c % 2) * SEQ + t * P
                            mm = pe.transpose(bank[first + c // 2][:, at:at + P], src[:, t, c * P:(c + 1) * P], ident)
                        if c % 2:
                            mm.then_inc(split_ps.sem, 1)

            def dense(L, s, kind, arg, b, half):
                    if b is not None and b >= 3 and half == 0:
                        by_act, count = taken_before(b - 2)
                        sig = taken_act if by_act else taken_dve
                        pe.wait_ge(sig.sem, sig.at(L, count))
                    if kind == "y":
                        pe.wait_ge(split_lo.sem, split_lo.at(L, 2 * SPLITS.index({0: "o0", 1: "mixed", 2: "o1", 3: "o2"}[arg[0]]) + 2))
                        acts = brT[{1: 0, 0: 1, 2: 0, 3: 1}[arg[0]]]
                    elif kind in ("mk", "mv"):
                        acts = memhT
                    else:
                        acts = hT
                    if kind == "f":
                        pe.wait_ge(kT_ready.sem, kT_ready.at(L, 1))
                        for kc in range(KC):
                            if kc % 4 == 0:
                                wait_unit(L, 2 * s + kc // 4)
                            w = [unit_slot(part, s, kc // 4)[:, (kc % 4) * NH:(kc % 4 + 1) * NH] for part in range(2)]
                            mm = three(bank[7][0:NH, 0:SEQ], [acts[p][:, kc, :] for p in range(2)], w, kc == 0, kc == KC - 1, False)
                            if kc % 4 == 3:
                                mm.then_inc(used.sem, 1)
                    elif kind == "mixing":
                        pe.wait_ge(split_lo.sem, split_lo.at(L, 2 * SPLITS.index("pooled") + 2))
                        pe.wait_ge(o_ready.sem, o_ready.at(L, 2))
                        for g in range(4):
                            if g % 2 == 0:
                                wait_unit(L, 2 * s + g // 2)
                            w = [unit_slot(part, s, g // 2)[:, (g % 2) * P:(g % 2 + 1) * P] for part in range(2)]
                            mm = three(bank[6 + g // 2][:, (g % 2) * SEQ:(g % 2 + 1) * SEQ],
                                       [pooledT[p][:, g, :] for p in range(2)], w, True, True, False)
                            if g % 2:
                                mm.then_inc(used.sem, 1)
                    elif kind == "out":
                        if arg % 2 == 0:
                            pe.wait_ge(split_lo.sem, split_lo.at(L, 2 * SPLITS.index("z0" if arg == 0 else "z1") + 2))
                        src, n = (brT[0], 2) if arg < 2 else (hT, 4)
                        if arg < 3:
                            rows(L, [s + i for i in range(n // 2)],
                                 [[src[part][:, 2 * (arg % 2) + k, :] for k in range(n)] for part in range(2)], arg == 0, arg == 2,
                                 (lambda: norm_transposes(L, 2, 0, True, (0,))) if arg == 2 else None)
                    else:
                        nk = BC if kind == "y" else KC
                        for k in range(2):
                            wait_unit(L, 2 * s + k)
                            w = [unit_slot(part, s, k).rearrange("p (k c) -> p k c", k=2) for part in range(2)]
                            for kk in range(2):
                                kc = 4 * half + 2 * k + kk
                                if kind == "mk" and kc % 2 == 0:
                                    pe.wait_ge(memh_ready.sem, memh_ready.at(L, kc // 2 + 1))
                                if kind == "qa" and kc % 2 == 0:
                                    pe.wait_ge(h_ready.sem, h_ready.at(L, 4 + kc // 2 + 1))
                                for t in range(NT):
                                    mm = three(bank[2 * (b % 2) + t][:, :], [acts[p][:, kc, t * P:(t + 1) * P] for p in range(2)],
                                               [w[p][:, kk, :] for p in range(2)], kc == 0, kc == nk - 1, True)
                            mm.then_inc(used.sem, 1)

            def mixer(L):
                for i, (kind, arg, b, half) in enumerate(MIX):
                    dense(L, MIX0 + i, kind, arg, b, half)
                    for stage, targ in TASKS.get(MIX0 + i, ()):
                        task(L, stage, targ)

            pe.sem_inc(used.sem, used.credit)
            pe.wait_ge(ident_loaded, 16)
            for t in range(NT):
                pe.wait_ge(mem_rows, t + 1)
                for kc in range(KC):
                    at = (kc % 2) * SEQ + t * P
                    mm = pe.transpose(bank[kc // 2][:, at:at + P], mem_n[:, t, kc * P:(kc + 1) * P], ident)
            mm.then_inc(mem_turned, 1)
            pe.wait_ge(memN_act, 1)
            pe.wait_ge(setup_loads, 16 * N_SETUP)
            with pe.Fori(0, DEPTH) as L:
                dense(L, 0, "mk", None, -1, 0)
                norm_transposes(L, 0, 4, True)
                dense(L, 1, "mk", None, -1, 1)
                feed_forward(L, 0, FFN1_0)
                mixer(L)
                norm_transposes(L, 2, 0, True, (1,))
                feed_forward(L, 1, FFN2_0)

        def split_target(name):
            return {"pooled": (pooledT, 4, 1.0), "o0": (brT[1], 4, 1.0), "o1": (brT[0], 6, 1.0), "o2": (brT[1], 4, 1.0),
                    "z0": (brT[0], 4, 0.5), "z1": (hT, 0, 0.5)}[name]

        PS_ORDER = [name for name in SPLITS if name != "mixed"]
        HEAD_DST = {"mk": (kmem, MH), "qa": (qk[:, 0], NH), "ka": (qk[:, 1], NH), "qc": (qk[:, 0], NH),
                    "kc": (qk[:, 1], NH), "qm": (qk[:, 0], MH)}
        GATES = [arg for kind, arg, _, _ in MIX if kind == "y"]

        def banks_of(s):
            b = TOP_MIX[s][2] if s < TOP else MIX[s - MIX0][2]
            return [bank[2 * (b % 2) + t] for t in range(NT)]

        def gain(at):
            return own[:, 0, at:at + 1]

        @block.scalar
        def _(act):
            def hi(L, step, k, j=None):
                n = 2 * step + k
                m, view, _ = unit_words(step, k)
                arrived, free = raw_ready[m % RAW].at(L, 16 * (m // RAW + 1)), used.at(L, n + 1 - SLOTS)
                act.wait_ge(raw_ready[m % RAW].sem, arrived if j is None else arrived + 16 * j)
                act.wait_ge(used.sem, free if j is None else free + 8 * j)
                act.activation(unit_out(0, step, k), view, ACT.Copy).then_inc(hi_done.sem, 1)

            def norm(L, index, t, ready, halves=(0, 1)):
                for half in halves:
                    if L is not None:
                        act.wait_ge(x_ready.sem, x_ready.at(L, ready if index == 0 else ready + 2 * t + half + 1))
                    at = slice(half * 512, (half + 1) * 512)
                    act.activation(xn[:, t, at], x[:, t, at], ACT.Square, accum_out=ss[:, t, half:half + 1]).then_inc(sumsq.sem, 1)

            def norm_second(L, index, t):
                act.wait_ge(rs_ready.sem, rs_ready.at(0 if L is None else L, 2 * index + t + 1))
                act.activation(xn[:, t, 512:], x[:, t, 512:], ACT.Copy, scale=row_rs[:, t:t + 1]).then_inc(xn_second.sem, 1)

            def norm_hi(L, index, banks):
                if index == 0:
                    act.wait_ge(own_ready.sem, own_ready.at(L, 1))
                for b in range(4):
                    act.wait_ge(xnT.sem, xnT.at(L, 4 * index + b + 1))
                    for kc in (2 * b, 2 * b + 1):
                        last = act.activation(hT[0][:, kc, :], bank[banks + b][:, (kc % 2) * SEQ:(kc % 2 + 1) * SEQ], ACT.Copy,
                                              scale=gain(NORM_AT + index * KC + kc))
                    last.then_inc(h_hi.sem, 1)

            def memory_hi(L, count):
                act.wait_ge(next_gain_ready.sem, next_gain_ready.at(L, count))
                for kc in range(KC):
                    last = act.activation(memhT[0][:, kc, :], memN[:, kc, :], ACT.Copy, scale=next_gain[:, 0, kc:kc + 1])
                    if kc % 2:
                        last.then_inc(memh_hi.sem, 1)

            def hidden(L, base, first_chunk):
                def body(j, c):
                    s = base + c
                    def plus(value, per_turn):
                        return value if j is None else value + per_turn * j
                    act.wait_ge(used.sem, plus(used.at(L, 2 * s + 2), 8))
                    act.activation(silu[:, c % 2, :], bank[c % 4][:, 0:SEQ], ACT.Silu).then_inc(silu_done.sem, 1)
                    hi(L, s + 2, 0, j)
                    hi(L, s + 2, 1, j)
                    act.wait_ge(prod_done.sem, plus(prod_done.at(L, first_chunk + c + 1), 4))
                    dst = act_hi[:, c:c + 1, :] if j is None else act_hi[:, bass.ds(4 * j + c, 1), :]
                    act.activation(dst, prod[:, c % 2:c % 2 + 1, :], ACT.Copy).then_inc(act_hi_done.sem, 1)
                return body

            def ahead(L, s):
                if s + 2 < STEPS:
                    hi(L, s + 2, 0)
                    hi(L, s + 2, 1)

            def boundary(L, index, s, ready):
                norm(L, index, 0, ready)
                if index == 1:
                    hi(L, s + 2, 0)
                    norm_second(L, index, 0)
                    hi(L, s + 2, 1)
                    hi(L, s + 3, 0)
                    norm(L, index, 1, ready)
                    norm_second(L, index, 1)
                    hi(L, s + 3, 1)
                else:
                    norm_second(L, index, 0)
                    norm(L, index, 1, ready, (0,))
                    hi(L, s + 2, 0)
                    norm(L, index, 1, ready, (1,))
                    hi(L, s + 2, 1)
                    norm_second(L, index, 1)
                    norm_hi(L, index, 0)
                    hi(L, s + 3, 0)
                    hi(L, s + 3, 1)

            def feed_forward(L, which, base):
                steps_in_loop(act, hidden(L, base, which * FC))
                for r in range(FC // 2 - 2):
                    ahead(L, base + FC + r)
                    if which == 0 and r == 2:
                        act.wait_ge(ang_ready.sem, ang_ready.at(L, 1))
                        act.activation(sinv[:, :, :], ang[:, :, :], ACT.Sin)
                        act.activation(absang[:, :, :], ang[:, :, :], ACT.Abs).then_inc(trig_done.sem, 1)
                        act.wait_ge(ang_ready.sem, ang_ready.at(L, 2))
                        act.activation(cosv[:, :, :], turns[:, :, :], ACT.Sin).then_inc(trig_done.sem, 1)
                    if which == 1 and r == 2:
                        memory_hi(L, 2)
                if which == 0:
                    boundary(L, 1, base + FFN_STEPS - 2, 0)
                else:
                    norm(L, 3, 0, 8)
                    norm_second(L, 3, 0)

            def split(L, name):
                dst, first, factor = split_target(name)
                at = 2 * PS_ORDER.index(name)
                for b in range(2):
                    act.wait_ge(split_ps.sem, split_ps.at(L, at + b + 1))
                    act.activation(dst[0][:, 2 * b:2 * b + 2, :], bank[first + b][:, :].rearrange("p (c t) -> p c t", c=2), ACT.Copy,
                                   scale=factor).then_inc(split_hi.sem, 1)

            def task(L, stage, arg):
                if stage == "norm":
                    norm_hi(L, 1, 4)
                elif stage == "qkT":
                    act.wait_ge(qkT_ps.sem, qkT_ps.at(L, arg + 1))
                    for b in range(2):
                        last = act.activation(qkT_buf[:, arg % 2, 0, 2 * b:2 * b + 2, :],
                                              bank[4 + b][:, :].rearrange("p (c t) -> p c t", c=2), ACT.Copy,
                                              scale=1.0 if arg == 0 else gain(HEAD_AT + 2 * (arg - 1)))
                    last.then_inc(qT_ready.sem, 1)
                elif stage == "scores":
                    act.wait_ge(max_ready.sem, max_ready.at(L, arg + 1))
                    if arg < 4:
                        for i in range(4):
                            for t in range(NT):
                                p = probs[:, i * P:(i + 1) * P] if t == 0 else probs[:, 512 + i * SEQ:512 + (i + 1) * SEQ]
                                last = act.activation(p, p, ACT.Exp, bias=nmx[:, 4 * t + i:4 * t + i + 1], scale=HD ** -0.5,
                                                      accum_out=den[:, arg % 2, 4 * t + i:4 * t + i + 1])
                    else:
                        act.wait_ge(pT_ps.sem, pT_ps.at(L, arg))
                        for i in range(2):
                            for t in range(NT):
                                last = act.activation(probs[:, t * 512 + i * SEQ:t * 512 + (i + 1) * SEQ],
                                                      bank[4 + t][:, i * SEQ:(i + 1) * SEQ], ACT.Exp,
                                                      bias=nmx[:, 2 * t + i:2 * t + i + 1], scale=MHD ** -0.5,
                                                      accum_out=den[:, arg % 2, 2 * t + i:2 * t + i + 1])
                    last.then_inc(probs_ready.sem, 1)
                elif stage == "probsT":
                    act.wait_ge(pT_ps.sem, pT_ps.at(L, arg + 1))
                    act.activation(pT[:, 0, :], bank[4][:, :], ACT.Copy).then_inc(pT_act.sem, 1)
                elif stage == "pool":
                    split(L, "pooled")
                elif stage == "oT":
                    split(L, f"o{arg}")
                elif stage == "zT":
                    split(L, f"z{arg}")

            def serve(L, s, kind, arg, half):
                if kind == "f":
                    act.wait_ge(fna_ready.sem, fna_ready.at(L, 1))
                    act.activation(fe[:, :], fna[:, :], ACT.Exp).then_inc(fe_done.sem, 1)
                    act.wait_ge(fe_done.sem, fe_done.at(L, 1))
                    act.activation(fl[:, :], fe[:, :], ACT.Ln, bias=1.0).then_inc(fl_done.sem, 1)
                elif kind == "mixing":
                    for b in range(2):
                        act.wait_ge(used.sem, used.at(L, 2 * s + b + 1))
                        for g in (2 * b, 2 * b + 1):
                            last = act.activation(brT[0][0][:, g, :], bank[6 + b][:, (g % 2) * SEQ:(g % 2 + 1) * SEQ], ACT.Copy,
                                                  scale=gain(POOL_AT + g))
                        last.then_inc(split_hi.sem, 1)
                elif half == 1 and kind != "out":
                    act.wait_ge(used.sem, used.at(L, 2 * s + 2))
                    banks = banks_of(s)
                    if kind == "gate":
                        idx = GATES.index(arg)
                        if idx >= 2:
                            act.wait_ge(taken_dve.sem, taken_dve.at(L, release("y", GATES[idx - 2])))
                        for t in range(NT):
                            last = act.activation(gate[:, idx % 2, t, :], banks[t][:, :], ACT.Tanh, scale=0.5)
                        last.then_inc(taken_act.sem, 1)
                    elif kind in BY_ACT:
                        dst = o[:, 2] if kind == "pu" else vals[:, {"va": 0, "vc": 1, "mv": 2}[kind]]
                        for t in range(NT):
                            last = act.activation(dst[:, t, :], banks[t][:, :], ACT.Copy)
                        last.then_inc(taken_act.sem, 1)
                    else:
                        if kind in ("qc", "kc", "qm"):
                            act.wait_ge(qkT_ps.sem, qkT_ps.at(L, 2 if kind == "qm" else 1))
                        dst, heads = HEAD_DST[kind]
                        for t in range(NT):
                            act.activation(dst[:, t, :], banks[t][:, :], ACT.Square).then_inc(squares.sem, 1)

            def mixer(L):
                for i, (kind, arg, b, half) in enumerate(MIX):
                    if (kind, arg) == ("out", 2):
                        break
                    ahead(L, MIX0 + i)
                    serve(L, MIX0 + i, kind, arg, half)
                    for stage, targ in TASKS.get(MIX0 + i, ()):
                        task(L, stage, targ)
                boundary(L, 2, FFN2_0 - 2, 4)

            act.dma_start(ident, const_d[:, 0:P]).then_inc(ident_loaded, 16)
            act.dma_start(gains[:, :, :], gains_d).then_inc(gains_loaded, 16)
            act.dma_start(const[:, P:], const_d[:, P:]).then_inc(setup_loads, 16)
            act.dma_start(freq[:, :], freq_d).then_inc(setup_loads, 16)
            act.dma_start(pos_i[:, :], pos_d).then_inc(setup_loads, 16)
            for t in range(NT):
                act.wait_ge(mem_loaded[t], 16)
                act.activation(mem_n[:, t, :], memx[:, t, :], ACT.Square, accum_out=hss[:, t:t + 1]).then_inc(mem_squares, 1)
            act.wait_ge(x_loaded, 16)
            norm(None, 0, 0, 0)
            norm_second(None, 0, 0)
            act.wait_ge(mem_turned, 1)
            for b in range(4):
                last = act.activation(memN[:, 2 * b:2 * b + 2, :], bank[b][:, :].rearrange("p (c t) -> p c t", c=2), ACT.Copy)
            last.then_inc(memN_act, 1)
            act.wait_ge(memN_act, 1)
            memory_hi(0, 1)
            with act.Fori(0, DEPTH) as L:
                for k in range(2):
                    hi(L, 0, k)
                norm(L, 0, 1, 0)
                hi(L, 1, 0)
                norm_second(L, 0, 1)
                hi(L, 1, 1)
                norm_hi(L, 0, 4)
                ahead(L, 0)
                ahead(L, 1)
                serve(L, 1, "mk", None, 1)
                feed_forward(L, 0, FFN1_0)
                mixer(L)
                feed_forward(L, 1, FFN2_0)

        @block.vector
        def _(dve):
            links, setups = [0], [0]

            def link(L, ins):
                if L is None:
                    setups[0] += 1
                    ins.then_inc(setup_step, 1)
                    dve.wait_ge(setup_step, setups[0])
                else:
                    links[0] += 1
                    ins.then_inc(vlink.sem, 1)
                    dve.wait_ge(vlink.sem, vlink.at(L, links[0]))

            def lo(L, step, k, j=None):
                done = hi_done.at(L, 2 * step + k + 1)
                dve.wait_ge(hi_done.sem, done if j is None else done + 8 * j)
                _, view, _ = unit_words(step, k)
                dve.tensor_tensor(unit_out(1, step, k), view, unit_out(0, step, k).bitcast(F32), ALU.subtract)\
                    .then_inc(lo_done.sem, 1)

            def newton(L, r, m, n):
                link(L, dve.tensor_scalar(r.bitcast(I32), m.bitcast(I32), -0.5, 1597463007.0, ALU.mult, ALU.add))
                for _ in range(3):
                    link(L, dve.scalar_tensor_tensor(ra[:, 0:n], r, -0.5, r, ALU.mult, ALU.mult))
                    link(L, dve.tensor_tensor(rb[:, 0:n], ra[:, 0:n], m, ALU.mult))
                    link(L, dve.scalar_tensor_tensor(r, rb[:, 0:n], 1.5, r, ALU.add, ALU.mult))

            def newton_row(L, r, done=None):
                link(L, dve.tensor_scalar(r.bitcast(I32), ms[:, 0:1].bitcast(I32), -0.5, 1597463007.0 - 2.0 ** 30 - 2.0 ** 22,
                                          ALU.mult, ALU.add))
                for step in range(3):
                    link(L, dve.scalar_tensor_tensor(ra[:, 0:1], r, ms[:, 0:1], r, ALU.mult, ALU.mult))
                    last = dve.scalar_tensor_tensor(r, ra[:, 0:1], 1.5, r, ALU.add, ALU.mult)
                    if done is None or step < 2:
                        link(L, last)
                if done is not None:
                    last.then_inc(done.sem, 1)

            def norm(L, index, t):
                layer = 0 if L is None else L
                dve.wait_ge(sumsq.sem, sumsq.at(layer, 4 * index + 2 * t + 1))
                link(L, dve.tensor_scalar(ms[:, 0:1], ss[:, t, 0:1], -0.5 / DM, -0.5 * EPS, ALU.mult, ALU.add))
                dve.wait_ge(sumsq.sem, sumsq.at(layer, 4 * index + 2 * t + 2))
                link(L, dve.scalar_tensor_tensor(ms[:, 0:1], ss[:, t, 1:2], -0.5 / DM, ms[:, 0:1], ALU.mult, ALU.add))
                newton_row(L, row_rs[:, t:t + 1], rs_ready)
                dve.wait_ge(rs_ready.sem, rs_ready.at(layer, 2 * index + t + 1))
                dve.tensor_scalar(xn[:, t, 0:512], x[:, t, 0:512], row_rs[:, t:t + 1], None, ALU.mult).then_inc(xn_first.sem, 1)

            def norm_lo(L, index, banks):
                for b in range(4):
                    dve.wait_ge(h_hi.sem, h_hi.at(L, 4 * index + b + 1))
                    for kc in (2 * b, 2 * b + 1):
                        last = dve.scalar_tensor_tensor(hT[1][:, kc, :], bank[banks + b][:, (kc % 2) * SEQ:(kc % 2 + 1) * SEQ],
                                                        gain(NORM_AT + index * KC + kc), hT[0][:, kc, :].bitcast(F32),
                                                        ALU.mult, ALU.subtract)
                    last.then_inc(h_ready.sem, 1)

            def memory_lo(L, count):
                for kc in range(KC):
                    if kc % 2 == 0:
                        dve.wait_ge(memh_hi.sem, memh_hi.at(L, 4 * (count - 1) + kc // 2 + 1))
                    last = dve.scalar_tensor_tensor(memhT[1][:, kc, :], memN[:, kc, :], next_gain[:, 0, kc:kc + 1],
                                                    memhT[0][:, kc, :].bitcast(F32), ALU.mult, ALU.subtract)
                    if kc % 2:
                        last.then_inc(memh_ready.sem, 1)

            def hidden(L, base, first_chunk):
                def body(j, c):
                    s = base + c
                    def plus(value, per_turn):
                        return value if j is None else value + per_turn * j
                    lo(L, s + 2, 0, j)
                    dve.wait_ge(silu_done.sem, plus(silu_done.at(L, first_chunk + c + 1), 4))
                    dve.tensor_tensor(prod[:, c % 2, :], silu[:, c % 2, :], bank[c % 4][:, SEQ:2 * SEQ], ALU.mult)\
                        .then_inc(prod_done.sem, 1)
                    lo(L, s + 2, 1, j)
                    dve.wait_ge(act_hi_done.sem, plus(act_hi_done.at(L, first_chunk + c + 1), 4))
                    at = slice(c, c + 1) if j is None else bass.ds(4 * j + c, 1)
                    dve.tensor_tensor(act_lo[:, at, :], prod[:, c % 2:c % 2 + 1, :], act_hi[:, at, :].bitcast(F32), ALU.subtract)\
                        .then_inc(act_ready.sem, 1)
                return body

            def ahead(L, s):
                if s + 2 < STEPS:
                    lo(L, s + 2, 0)
                    lo(L, s + 2, 1)

            def add_rows(L, phase, t, last_step, factor):
                for half in range(2):
                    if t == 0:
                        dve.wait_ge(rows0_ready.sem, rows0_ready.at(L, phase + 1))
                    elif phase == 1 and half == 0:
                        dve.wait_ge(half_row_ready.sem, half_row_ready.at(L, 1))
                    else:
                        dve.wait_ge(used.sem, used.at(L, 2 * last_step + 2))
                    xs = x[:, t, half * 512:(half + 1) * 512]
                    dve.scalar_tensor_tensor(xs, bank[4 + 2 * t + half][:, :], factor, xs, ALU.mult, ALU.add)\
                        .then_inc(x_ready.sem, 1)

            def boundary(L, phase, index, s, factor):
                add_rows(L, phase, 0, s + 1, factor)
                norm(L, index, 0)
                if index == 1:
                    lo(L, s + 2, 0)
                    add_rows(L, phase, 1, s + 1, factor)
                    lo(L, s + 2, 1)
                    norm(L, index, 1)
                    lo(L, s + 3, 0)
                    lo(L, s + 3, 1)
                else:
                    add_rows(L, phase, 1, s + 1, factor)
                    norm(L, index, 1)
                    lo(L, s + 2, 0)
                    lo(L, s + 2, 1)
                    norm_lo(L, index, 0)
                    lo(L, s + 3, 0)
                    lo(L, s + 3, 1)

            def angles(L):
                link(L, dve.tensor_copy(pos_f[:, :], pos_i[:, :]))
                for t in range(NT):
                    last = dve.tensor_scalar(ang[:, t, :], freq[:, :], pos_f[:, t:t + 1], None, ALU.mult)
                link(L, last)
                link(L, dve.tensor_scalar(turns[:, :, :], ang[:, :, :], float(1 / (2 * np.pi)), 12582912.0, ALU.mult, ALU.add))
                link(L, dve.tensor_scalar(turns[:, :, :], turns[:, :, :], 12582912.0, None, ALU.subtract))
                for part in TWO_PI_PARTS:
                    link(L, dve.scalar_tensor_tensor(ang[:, :, :], turns[:, :, :], -part, ang[:, :, :], ALU.mult, ALU.add))
                dve.tensor_scalar(ang[:, :, :], ang[:, :, :], 3.1415925, -3.1415925, ALU.min, ALU.max).then_inc(ang_ready.sem, 1)
                dve.wait_ge(trig_done.sem, trig_done.at(L, 1))
                dve.tensor_scalar(turns[:, :, :], absang[:, :, :], -1.0, float(np.pi / 2), ALU.mult, ALU.add).then_inc(ang_ready.sem, 1)

            def feed_forward(L, which, base):
                steps_in_loop(dve, hidden(L, base, which * FC))
                last_two = base + FFN_STEPS - 2
                for r in range(FC // 2 - 2):
                    ahead(L, base + FC + r)
                    if which == 0 and r == 2:
                        angles(L)
                    if which == 1 and r == 2:
                        dve.tensor_copy(next_gain[:, :, :], gains[:, bass.ds(L + 1, 1), MEMORY_AT:MEMORY_AT + KC])\
                            .then_inc(next_gain_ready.sem, 1)
                        memory_lo(L, 2)
                if which == 0:
                    boundary(L, 0, 1, last_two, 0.5)
                else:
                    add_rows(L, 2, 0, last_two + 1, 0.5)
                    norm(L, 3, 0)
                    add_rows(L, 2, 1, last_two + 1, 0.5)

            def split(L, name):
                dst, first, factor = split_target(name)
                at = 2 * SPLITS.index(name)
                for b in range(2):
                    dve.wait_ge(split_hi.sem, split_hi.at(L, at + b + 1))
                    chunks = slice(2 * b, 2 * b + 2)
                    dve.scalar_tensor_tensor(dst[1][:, chunks, :], bank[first + b][:, :].rearrange("p (c t) -> p c t", c=2), factor,
                                             dst[0][:, chunks, :].bitcast(F32), ALU.mult, ALU.subtract).then_inc(split_lo.sem, 1)

            def task(L, stage, arg):
                if stage == "norm":
                    norm_lo(L, 1, 4)
                elif stage == "qkT":
                    dve.wait_ge(qkT_ps.sem, qkT_ps.at(L, arg + 1))
                    for b in range(2):
                        last = dve.tensor_scalar(qkT_buf[:, arg % 2, 1, 2 * b:2 * b + 2, :],
                                                 bank[6 + b][:, :].rearrange("p (c t) -> p c t", c=2),
                                                 1.0 if arg == 0 else gain(HEAD_AT + 2 * (arg - 1) + 1), None, ALU.mult)
                    last.then_inc(kT_ready.sem, 1)
                elif stage == "scores":
                    dve.wait_ge(scores_ready.sem, scores_ready.at(L, arg + 1))
                    if arg < 4:
                        if arg:
                            dve.wait_ge(pT_ps.sem, pT_ps.at(L, arg))
                        dve.tensor_tensor(probs[:, 0:512].rearrange("p (h k) -> p h k", h=4),
                                          bank[4][:, :].rearrange("p (h k) -> p h k", h=4),
                                          mask[:, None, P:SEQ].to_broadcast([P, 4, P]), ALU.add)
                        for b in range(2):
                            at = 512 + 512 * b
                            last = dve.tensor_tensor(probs[:, at:at + 512].rearrange("p (h k) -> p h k", h=2),
                                                     bank[5 + b][:, :].rearrange("p (h k) -> p h k", h=2),
                                                     mask[:, None, :].to_broadcast([P, 2, SEQ]), ALU.add)
                        link(L, last)
                        dve.tensor_reduce(mx[:, 0:4], probs[:, 0:512].rearrange("p (h k) -> p h k", h=4), axis=AX.X, op=ALU.max)
                        link(L, dve.tensor_reduce(mx[:, 4:8], probs[:, 512:].rearrange("p (h k) -> p h k", h=4), axis=AX.X, op=ALU.max))
                        dve.tensor_scalar(nmx[:, :], mx[:, :], -(HD ** -0.5), None, ALU.mult).then_inc(max_ready.sem, 1)
                    else:
                        for t in range(NT):
                            last = dve.tensor_reduce(mx[:, 2 * t:2 * t + 2], bank[4 + t][:, :].rearrange("p (h k) -> p h k", h=2),
                                                     axis=AX.X, op=ALU.max)
                        link(L, last)
                        dve.tensor_scalar(nmx[:, 0:4], mx[:, 0:4], -(MHD ** -0.5), None, ALU.mult).then_inc(max_ready.sem, 1)
                elif stage == "probsT":
                    dve.wait_ge(pT_ps.sem, pT_ps.at(L, arg + 1))
                    for b in range(2 if arg < 4 else 1):
                        last = dve.tensor_copy(pT[:, 1 + b, :], bank[5 + b][:, :])
                    last.then_inc(pT_dve.sem, 1)
                elif stage == "values":
                    br, n, d = arg // 2, 4 if arg < 4 else 2, HD if arg < 4 else MHD
                    dve.wait_ge(pv_ready.sem, pv_ready.at(L, arg + 1))
                    link(L, dve.reciprocal(rden[:, 0:2 * n], den[:, arg % 2, 0:2 * n]))
                    if arg < 4:
                        dst = o[:, br].rearrange("p t (h two d) -> p t h two d", two=2, d=d)[:, :, :, arg % 2, :]
                    else:
                        dst = o[:, br].rearrange("p t (two h d) -> p t two h d", two=2, d=d)[:, :, arg % 2]
                    dve.tensor_tensor(dst,
                                      bank[7][:, :].rearrange("p (t h d) -> p t h d", t=NT, h=n),
                                      rden[:, 0:2 * n].rearrange("p (t h) -> p t h", t=NT)[:, :, :, None].to_broadcast([P, NT, n, d]),
                                      ALU.mult).then_inc(o_ready.sem, 1)
                elif stage == "pool":
                    split(L, "pooled")
                elif stage == "oT":
                    split(L, f"o{arg}")
                elif stage == "zT":
                    split(L, f"z{arg}")

            def serve(L, s, kind, arg, half):
                if kind == "f":
                    dve.wait_ge(used.sem, used.at(L, 2 * s + 2))
                    link(L, dve.tensor_scalar(fz[:, :], bank[7][0:NH, 0:SEQ], own[0:NH, 0, FORGET_AT:FORGET_AT + 1], None, ALU.add))
                    dve.scalar_tensor_tensor(fna[:, :], fz[:, :], -1.0, fz[:, :], ALU.mult, ALU.min).then_inc(fna_ready.sem, 1)
                    link(L, dve.tensor_scalar(fmin[:, :], fz[:, :], 0.0, None, ALU.min))
                    dve.wait_ge(fl_done.sem, fl_done.at(L, 1))
                    link(L, dve.tensor_tensor_scan(csum[:, :], fmin[:, :], fl[:, :], 0.0, ALU.add, ALU.subtract))
                    dve.tensor_scalar(negc[:, :], csum[:, :], -float(HD ** 0.5), None, ALU.mult).then_inc(negc_ready.sem, 1)
                elif kind == "mixing":
                    at = 2 * SPLITS.index("mixed")
                    for b in range(2):
                        dve.wait_ge(split_hi.sem, split_hi.at(L, at + b + 1))
                        for g in (2 * b, 2 * b + 1):
                            last = dve.scalar_tensor_tensor(brT[0][1][:, g, :], bank[6 + b][:, (g % 2) * SEQ:(g % 2 + 1) * SEQ],
                                                            gain(POOL_AT + g), brT[0][0][:, g, :].bitcast(F32),
                                                            ALU.mult, ALU.subtract)
                        last.then_inc(split_lo.sem, 1)
                elif kind == "y":
                    n, dh = arg
                    idx = GATES.index(arg)
                    dve.wait_ge(taken_act.sem, taken_act.at(L, release("gate", arg)))
                    dve.wait_ge(used.sem, used.at(L, 2 * s + 2))
                    banks = banks_of(s)
                    zs = [z[:, t, dh * BW:(dh + 1) * BW] for t in range(NT)]
                    gs = [gate[:, idx % 2, t, :] for t in range(NT)]
                    for t in range(NT):
                        last = dve.scalar_tensor_tensor(zs[t] if idx < 2 else gs[t], gs[t], 1.0, banks[t][:, :], ALU.add, ALU.mult)
                    if idx >= 2:
                        link(L, last)
                        for t in range(NT):
                            last = dve.tensor_tensor(zs[t], zs[t], gs[t], ALU.add)
                    last.then_inc(taken_dve.sem, 1)
                elif half == 1 and kind in NORMED:
                    dst, heads = HEAD_DST[kind]
                    d = BW // heads
                    banks = banks_of(s)
                    dve.wait_ge(squares.sem, squares.at(L, 2 * NORMED.index(kind) + 2))
                    link(L, dve.tensor_reduce(hss[:, 0:NT * heads].rearrange("p (t h) -> p t h", t=NT),
                                              dst[:, :, :].rearrange("p t (h d) -> p t h d", h=heads), axis=AX.X, op=ALU.add))
                    n = NT * heads
                    link(L, dve.tensor_scalar(ms[:, 0:n], hss[:, 0:n], 1.0 / d, EPS, ALU.mult, ALU.add))
                    newton(L, rs[:, 0:n], ms[:, 0:n], n)
                    for t in range(NT):
                        last = dve.tensor_tensor(dst[:, t, :].rearrange("p (h d) -> p h d", h=heads),
                                                 banks[t][:, :].rearrange("p (h d) -> p h d", h=heads),
                                                 rs[:, t * heads:(t + 1) * heads, None].to_broadcast([P, heads, d]), ALU.mult)
                    last.then_inc(taken_dve.sem, 1)
                    if kind in ("qa", "ka"):
                        dve.wait_ge(taken_dve.sem, taken_dve.at(L, release(kind)))
                        at = MOBA_AT + (0 if kind == "qa" else HD)
                        for t in range(NT):
                            rows = dst[:, t, :].rearrange("p (h d) -> p h d", h=heads)
                            last = dve.tensor_tensor(rows, rows, own[:, :, at:at + HD].to_broadcast([P, heads, HD]), ALU.mult)
                        link(L, last)
                        dve.wait_ge(trig_done.sem, trig_done.at(L, 2))
                        halves = [dst[:, :, :].rearrange("p t (h d) -> p t h d", h=heads)[:, :, :, 8 * i:8 * i + 8] for i in range(2)]
                        tables = [v[:, :, None, :].to_broadcast([P, NT, heads, 8]) for v in (cosv, sinv)]
                        for i, (a, b) in enumerate(((0, 0), (1, 1), (1, 0), (0, 1))):
                            last = dve.tensor_tensor(rot[:, i], halves[a], tables[b], ALU.mult)
                        link(L, last)
                        dve.tensor_tensor(halves[0], rot[:, 0], rot[:, 1], ALU.subtract)
                        dve.tensor_tensor(halves[1], rot[:, 2], rot[:, 3], ALU.add).then_inc(rotated.sem, 1)

            def mixer(L):
                for i, (kind, arg, b, half) in enumerate(MIX):
                    if (kind, arg) == ("out", 2):
                        break
                    ahead(L, MIX0 + i)
                    if kind != "qm":
                        serve(L, MIX0 + i, kind, arg, half)
                    for stage, targ in TASKS.get(MIX0 + i, ()):
                        task(L, stage, targ)
                    if kind == "qm":
                        serve(L, MIX0 + i, kind, arg, half)
                boundary(L, 1, 2, FFN2_0 - 2, 1.0)

            dve.sem_inc(lo_done.sem, lo_done.credit)
            dve.sem_inc(prod_done.sem, prod_done.credit)

            for t in range(NT):
                dve.wait_ge(mem_squares, t + 1)
                link(None, dve.tensor_scalar(ms[:, 0:1], hss[:, t:t + 1], -0.5 / DM, -0.5 * EPS, ALU.mult, ALU.add))
                newton_row(None, rs[:, 0:1])
                dve.tensor_scalar(mem_n[:, t, :], memx[:, t, :], rs[:, 0:1], None, ALU.mult).then_inc(mem_rows, 1)
            dve.wait_ge(gains_loaded, 16)
            dve.tensor_copy(next_gain[:, :, :], gains[:, 0:1, MEMORY_AT:MEMORY_AT + KC]).then_inc(next_gain_ready.sem, 1)
            dve.wait_ge(x_loaded, 16)
            norm(None, 0, 0)
            memory_lo(0, 1)
            dve.sem_inc(x_ready.sem, x_ready.credit)
            dve.wait_ge(setup_loads, 16 * N_SETUP)
            with dve.Fori(0, DEPTH) as L:
                for k in range(2):
                    lo(L, 0, k)
                dve.tensor_copy(own[:, :, :], gains[:, bass.ds(L, 1), :]).then_inc(own_ready.sem, 1)
                norm(L, 0, 1)
                for k in range(2):
                    lo(L, 1, k)
                dve.wait_ge(own_ready.sem, own_ready.at(L, 1))
                norm_lo(L, 0, 4)
                ahead(L, 0)
                ahead(L, 1)
                serve(L, 1, "mk", None, 1)
                feed_forward(L, 0, FFN1_0)
                mixer(L)
                feed_forward(L, 1, FFN2_0)
            assert links[0] == VLINKS, links


TWO_PI_PARTS = []
_rest = 2 * np.pi
for _bits in (9, 11, 24):
    _unit = 2.0 ** (np.floor(np.log2(abs(_rest))) - _bits + 1)
    _part = float(np.float32(np.round(_rest / _unit) * _unit))
    TWO_PI_PARTS.append(_part)
    _rest -= _part

_INS = ["x", "mem", "w_ffn1_in", "w_ffn1_out", "w_in", "w_mem_kv", "pool_mix", "w_branch", "w_out",
        "w_ffn2_in", "w_ffn2_out"]


def lay_out_gains(v):
    def columns(a):
        return a.reshape(DEPTH, -1, P).transpose(2, 0, 1)

    def rows(a):
        return np.broadcast_to(a[None], (P,) + a.shape)

    parts = [columns(v[n]) for n in ("norm_ffn1", "norm_mix", "norm_ffn2", "norm_mem", "pool_scale")]
    parts += [columns(np.concatenate([v[n], v[n]], axis=1)) for n in ("fox_q_gain", "fox_k_gain")]
    parts += [columns(v[n]) for n in ("mem_q_gain", "mem_k_gain")]
    parts += [columns(np.pad(v["b_forget"], ((0, 0), (0, P - NH))))]
    parts += [rows(v[n]) for n in ("moba_q_gain", "moba_k_gain")]
    laid = np.concatenate(parts, axis=2)
    return np.concatenate([laid, np.zeros_like(laid[:, :1])], axis=1)


def shape_constants():
    s, t = np.arange(P)[:, None], np.arange(SEQ)[None, :]
    mask = np.where((t >= P) & (t - P > s), NEG, 0.0)
    bands = []
    for w in WINDOWS:
        for first, tt in ((0, t), (P, t[:, P:])):
            src = s + first
            inside = (src <= tt) & (src > tt - w)
            bands.append(inside / np.minimum(tt + 1, w) - (src == tt))
    const = np.concatenate([np.eye(P), mask] + bands, axis=1).astype(np.float32)
    half = HD // 8
    freq = np.power(np.float32(500000.0), -np.arange(half, dtype=np.float32) * np.float32(2.0 / (2 * half))).astype(np.float32)
    return const, np.broadcast_to(freq[None], (P, half))


def kernel(**inputs):
    import concourse.bacc as bacc
    from concourse.bass_utils import run_bass_kernel_spmd

    nc = bacc.Bacc("TRN2", target_bir_lowering=False, num_devices=1)
    arrays, args = {}, []

    def take(name, a):
        arrays[name] = np.ascontiguousarray(a)
        args.append(nc.dram_tensor(name, a.shape, mybir.dt.from_np(a.dtype), kind="ExternalInput").ap())

    inputs = {name: np.asarray(a) for name, a in inputs.items()}
    for name in _INS:
        take(f"in_{name}", inputs[name])
    take("gains_dram", lay_out_gains(inputs))
    take("positions_dram", inputs["positions"].reshape(NT, P).T)
    for name, a in zip(("const_dram", "freq_dram"), shape_constants()):
        take(name, a)
    args.append(nc.dram_tensor("out_dram", (1, SEQ, DM), F32, kind="ExternalOutput").ap())
    build(nc, *args)
    r = run_bass_kernel_spmd(nc, [arrays], core_ids=[0])
    return r.results[0]["out_dram"]
```
